# Optimizing a Trainium2 kernel written in Bass

```python
import math
import jax, jax.numpy as jnp
from jax import lax
import numpy as np
import jax
import jax.numpy as jnp

D_MODEL = 1024
BATCH = 1
SEQ = 256
DEPTH = 2

POOL_WINDOWS = (2, 4, 8, 16)
POOL_GROUP = D_MODEL // 8
POOL_WIDTH = POOL_GROUP * len(POOL_WINDOWS)
SSM_D_INNER = D_MODEL
SSM_HEAD_DIM = 64
SSM_HEADS = SSM_D_INNER // SSM_HEAD_DIM
SSM_GROUPS = 2
SSM_STATE = 128
SSM_CONV = 4
SSM_CHUNK = 128
SSM_CONV_DIM = SSM_D_INNER + 2 * SSM_GROUPS * SSM_STATE
EVEN_IN = POOL_WIDTH + SSM_D_INNER + SSM_CONV_DIM + SSM_HEADS
EVEN_MIX = POOL_WIDTH + SSM_D_INNER
FOX_HEADS = 8
FOX_HEAD_DIM = 64
FOX_WIDTH = FOX_HEADS * FOX_HEAD_DIM
MLA_HEADS = 8
MLA_NOPE = 64
MLA_ROPE = 32
MLA_V = 64
MLA_Q_RANK = 512
MLA_KV_RANK = 256
ROPE_THETA = 10000.0
ODD_IN = 3 * FOX_WIDTH + FOX_HEADS + MLA_Q_RANK + MLA_KV_RANK + MLA_ROPE
ODD_MIX = FOX_WIDTH + MLA_HEADS * MLA_V
ATTN_BLOCK = 128
D_FF = -(-8 * D_MODEL // (3 * 256)) * 256
DEEPNORM_ALPHA = (2 * DEPTH) ** 0.25
DEEPNORM_BETA = (8 * DEPTH) ** -0.25
N_EVEN = (DEPTH + 1) // 2
N_ODD = DEPTH // 2
LN_EPS = 1e-5
RMS_EPS = 1e-6


F32 = jnp.float32

def layer_norm(x, g, b):
    xf = x.astype(F32)
    mu = jnp.mean(xf, axis=-1, keepdims=True)
    var = jnp.mean(jnp.square(xf - mu), axis=-1, keepdims=True)
    return ((xf - mu) * lax.rsqrt(var + LN_EPS) * g + b).astype(x.dtype)

def rms_norm(x, g):
    xf = x.astype(F32)
    return (xf * lax.rsqrt(jnp.mean(jnp.square(xf), axis=-1, keepdims=True) + RMS_EPS) * g).astype(x.dtype)

def rope(x, pos):
    half = x.shape[-1] // 2
    freqs = jnp.power(ROPE_THETA, -jnp.arange(half, dtype=F32) / half)
    ang = pos.astype(F32)[:, None] * freqs[None, :]
    cos, sin = jnp.cos(ang), jnp.sin(ang)
    x1 = x[..., :half].astype(F32)
    x2 = x[..., half:].astype(F32)
    return jnp.concatenate([x1 * cos - x2 * sin, x2 * cos + x1 * sin], axis=-1).astype(x.dtype)

def multiscale_pool(u, pool_w, pool_scale):
    b, s, _ = u.shape
    ng = len(POOL_WINDOWS)
    ug = u.reshape(b, s, ng, POOL_GROUP).astype(F32)
    cs = jnp.cumsum(ug, axis=1)
    pos = jnp.arange(s)
    means = []
    for g, w in enumerate(POOL_WINDOWS):
        c = cs[:, :, g]
        lagged = jnp.pad(c, ((0, 0), (w, 0), (0, 0)))[:, :s]
        count = jnp.minimum(pos + 1, w).astype(F32)[None, :, None]
        means.append((c - lagged) / count)
    diff = (jnp.stack(means, axis=2) - ug).astype(u.dtype)
    y = jnp.einsum('bsgc,gcd->bsgd', diff, pool_w).reshape(b, s, POOL_WIDTH)
    return y * pool_scale

def causal_dwconv(u, w, bias):
    c = u.shape[-1]
    out = lax.conv_general_dilated(
        u, w[:, None, :].astype(u.dtype), window_strides=(1,),
        padding=[(SSM_CONV - 1, 0)], dimension_numbers=('NWC', 'WIO', 'NWC'),
        feature_group_count=c)
    return out + bias

def mamba2_ssd(z, xbc, dt, conv_w, conv_b, dt_bias, a_log, d_skip, norm_w):
    b, s, _ = z.shape
    G, E, P, N, L = SSM_GROUPS, SSM_HEADS // SSM_GROUPS, SSM_HEAD_DIM, SSM_STATE, SSM_CHUNK
    nc = s // L
    xbc = jax.nn.silu(causal_dwconv(xbc, conv_w, conv_b))
    xs, bm, cm = jnp.split(xbc, [SSM_D_INNER, SSM_D_INNER + G * N], axis=-1)
    dt = jax.nn.softplus(dt.astype(F32) + dt_bias)
    a = -jnp.exp(a_log.astype(F32))
    xh = xs.reshape(b, nc, L, G, E, P).astype(F32)
    dtc = dt.reshape(b, nc, L, G, E)
    xdt = xh * dtc[..., None]
    da = dtc * a.reshape(G, E)
    bc = bm.reshape(b, nc, L, G, N).astype(F32)
    cc = cm.reshape(b, nc, L, G, N).astype(F32)
    acs = jnp.cumsum(da, axis=2).transpose(0, 1, 3, 4, 2)
    seg = acs[..., :, None] - acs[..., None, :]
    tri = jnp.tril(jnp.ones((L, L), dtype=bool))
    lmat = jnp.exp(jnp.where(tri, seg, -jnp.inf))
    cb = jnp.einsum('bclgn,bcsgn->bcgls', cc, bc)
    y_diag = jnp.einsum('bcgls,bcgels,bcsgep->bclgep', cb, lmat, xdt)
    decay_states = jnp.exp(acs[..., -1:] - acs)
    states = jnp.einsum('bclgn,bcgel,bclgep->bcgepn', bc, decay_states, xdt)
    chunk_decay = jnp.exp(acs[..., -1])

    def step(h, inp):
        st, dec = inp
        return h * dec[..., None, None] + st, h

    h0 = jnp.zeros((b, G, E, P, N), F32)
    _, prev = lax.scan(step, h0, (jnp.moveaxis(states, 1, 0), jnp.moveaxis(chunk_decay, 1, 0)))
    prev = jnp.moveaxis(prev, 0, 1)
    y_off = jnp.einsum('bclgn,bcgepn,bcgel->bclgep', cc, prev, jnp.exp(acs))
    y = y_diag + y_off + xh * d_skip.astype(F32).reshape(G, E)[:, :, None]
    y = y.reshape(b, s, SSM_D_INNER) * jax.nn.silu(z.astype(F32))
    return rms_norm(y, norm_w).astype(z.dtype)

def block_causal_attention(q, k, v, log_decay_cum):
    b, h, s, dk = q.shape
    nb = s // ATTN_BLOCK
    scale = dk ** -0.5
    qb = q.reshape(b, h, nb, ATTN_BLOCK, dk).transpose(2, 0, 1, 3, 4)
    fb = None if log_decay_cum is None else log_decay_cum.reshape(b, h, nb, ATTN_BLOCK).transpose(2, 0, 1, 3)
    kpos = jnp.arange(s)

    def one_block(args):
        qi, fi, i = args
        sc = jnp.einsum('bhqd,bhkd->bhqk', qi, k).astype(F32) * scale
        if fi is not None:
            sc = sc + fi[..., :, None] - log_decay_cum[:, :, None, :]
        qpos = i * ATTN_BLOCK + jnp.arange(ATTN_BLOCK)
        sc = jnp.where(kpos[None, :] <= qpos[:, None], sc, -jnp.inf)
        p = jax.nn.softmax(sc, axis=-1).astype(v.dtype)
        return jnp.einsum('bhqk,bhkd->bhqd', p, v)

    o = lax.map(one_block, (qb, fb, jnp.arange(nb)))
    return o.transpose(1, 0, 3, 2, 4).reshape(b, s, h * v.shape[-1])

def even_mixer(x, w_in, pool_w, pool_scale, conv_w, conv_b, dt_bias, a_log, d_skip, norm_w, w_out):
    proj = x @ w_in
    c1 = POOL_WIDTH
    c2 = c1 + SSM_D_INNER
    c3 = c2 + SSM_CONV_DIM
    u, z, xbc, dt = jnp.split(proj, [c1, c2, c3], axis=-1)
    y_pool = multiscale_pool(u, pool_w, pool_scale)
    y_ssm = mamba2_ssd(z, xbc, dt, conv_w, conv_b, dt_bias, a_log, d_skip, norm_w)
    return jnp.concatenate([y_pool, y_ssm], axis=-1) @ w_out

def odd_mixer(x, w_in, fgate_b, q_norm_w, w_uq, kv_norm_w, w_ukv, w_out):
    b, s, _ = x.shape
    proj = x @ w_in
    cuts = np.cumsum([FOX_WIDTH, FOX_WIDTH, FOX_WIDTH, FOX_HEADS, MLA_Q_RANK, MLA_KV_RANK]).tolist()
    qf, kf, vf, fl, cq, ckv, kr = jnp.split(proj, cuts, axis=-1)

    def heads(t, nh):
        return t.reshape(b, s, nh, -1).transpose(0, 2, 1, 3)

    log_f = jax.nn.log_sigmoid(fl.astype(F32) + fgate_b)
    fcum = jnp.cumsum(log_f, axis=1).transpose(0, 2, 1)
    o_fox = block_causal_attention(heads(qf, FOX_HEADS), heads(kf, FOX_HEADS), heads(vf, FOX_HEADS), fcum)

    pos = jnp.arange(s)
    q = heads(rms_norm(cq, q_norm_w) @ w_uq, MLA_HEADS)
    q = jnp.concatenate([q[..., :MLA_NOPE], rope(q[..., MLA_NOPE:], pos)], axis=-1)
    kv = heads(rms_norm(ckv, kv_norm_w) @ w_ukv, MLA_HEADS)
    k_rope = jnp.broadcast_to(rope(kr[:, None], pos), (b, MLA_HEADS, s, MLA_ROPE))
    k = jnp.concatenate([kv[..., :MLA_NOPE], k_rope], axis=-1)
    o_mla = block_causal_attention(q, k, kv[..., MLA_NOPE:], None)
    return jnp.concatenate([o_fox, o_mla], axis=-1) @ w_out

def swiglu(x, w_gate, w_up, w_down):
    return (jax.nn.silu(x @ w_gate) * (x @ w_up)) @ w_down

def first_inputs(seed: int = 0) -> dict:
    key = jax.random.key(seed)
    ks = iter(jax.random.split(key, 40))

    def nrm(shape, std):
        return jax.random.normal(next(ks), shape, F32) * std

    def gain(shape):
        return 1.0 + 0.1 * jax.random.normal(next(ks), shape, F32)

    dt0 = jnp.exp(jax.random.uniform(next(ks), (N_EVEN, SSM_HEADS), F32, math.log(1e-3), math.log(1e-1)))
    return {
        "x": jax.random.normal(next(ks), (BATCH, SEQ, D_MODEL), F32),
        "even_w_in": nrm((N_EVEN, D_MODEL, EVEN_IN), D_MODEL ** -0.5),
        "pool_w": nrm((N_EVEN, len(POOL_WINDOWS), POOL_GROUP, POOL_GROUP), POOL_GROUP ** -0.5),
        "pool_scale": gain((N_EVEN, POOL_WIDTH)),
        "conv_w": nrm((N_EVEN, SSM_CONV, SSM_CONV_DIM), SSM_CONV ** -0.5),
        "conv_b": nrm((N_EVEN, SSM_CONV_DIM), 0.01),
        "dt_bias": dt0 + jnp.log(-jnp.expm1(-dt0)),
        "a_log": jnp.log(jax.random.uniform(next(ks), (N_EVEN, SSM_HEADS), F32, 1.0, 16.0)),
        "d_skip": gain((N_EVEN, SSM_HEADS)),
        "ssm_norm_w": gain((N_EVEN, SSM_D_INNER)),
        "even_w_out": nrm((N_EVEN, EVEN_MIX, D_MODEL), EVEN_MIX ** -0.5 * DEEPNORM_BETA),
        "odd_w_in": nrm((N_ODD, D_MODEL, ODD_IN), D_MODEL ** -0.5),
        "fgate_b": jax.random.uniform(next(ks), (N_ODD, FOX_HEADS), F32, 1.0, 5.0),
        "q_norm_w": gain((N_ODD, MLA_Q_RANK)),
        "w_uq": nrm((N_ODD, MLA_Q_RANK, MLA_HEADS * (MLA_NOPE + MLA_ROPE)), MLA_Q_RANK ** -0.5),
        "kv_norm_w": gain((N_ODD, MLA_KV_RANK)),
        "w_ukv": nrm((N_ODD, MLA_KV_RANK, MLA_HEADS * (MLA_NOPE + MLA_V)), MLA_KV_RANK ** -0.5),
        "odd_w_out": nrm((N_ODD, ODD_MIX, D_MODEL), ODD_MIX ** -0.5 * DEEPNORM_BETA),
        "ffn_w_gate": nrm((DEPTH, D_MODEL, D_FF), D_MODEL ** -0.5),
        "ffn_w_up": nrm((DEPTH, D_MODEL, D_FF), D_MODEL ** -0.5),
        "ffn_w_down": nrm((DEPTH, D_FF, D_MODEL), D_FF ** -0.5 * DEEPNORM_BETA),
        "ln_mix_g": gain((DEPTH, D_MODEL)),
        "ln_mix_b": nrm((DEPTH, D_MODEL), 0.02),
        "ln_ffn_g": gain((DEPTH, D_MODEL)),
        "ln_ffn_b": nrm((DEPTH, D_MODEL), 0.02),
    }

def first_block(x, even_w_in, pool_w, pool_scale, conv_w, conv_b, dt_bias, a_log, d_skip, ssm_norm_w,
              even_w_out, odd_w_in, fgate_b, q_norm_w, w_uq, kv_norm_w, w_ukv, odd_w_out,
              ffn_w_gate, ffn_w_up, ffn_w_down, ln_mix_g, ln_mix_b, ln_ffn_g, ln_ffn_b):
    for l in range(DEPTH):
        i = l // 2
        if l % 2 == 0:
            h = even_mixer(x, even_w_in[i], pool_w[i], pool_scale[i], conv_w[i], conv_b[i], dt_bias[i],
                           a_log[i], d_skip[i], ssm_norm_w[i], even_w_out[i])
        else:
            h = odd_mixer(x, odd_w_in[i], fgate_b[i], q_norm_w[i], w_uq[i], kv_norm_w[i], w_ukv[i], odd_w_out[i])
        x = layer_norm(DEEPNORM_ALPHA * x + h, ln_mix_g[l], ln_mix_b[l])
        x = layer_norm(DEEPNORM_ALPHA * x + swiglu(x, ffn_w_gate[l], ffn_w_up[l], ffn_w_down[l]),
                       ln_ffn_g[l], ln_ffn_b[l])
    return x


DEPTH_2 = 1

GRID_W = 64
CTX_LEN = 256
N_MIXERS = 4
D_FF_2 = 4 * D_MODEL
N_MOD = 6
EPS = 1e-6
CONV_W = 3
HG_HEAD_DIM = 128
HG_HEADS = D_MODEL // HG_HEAD_DIM
HG_CHUNK = 32
S5_GROUP = 16
S5_GROUPS = D_MODEL // S5_GROUP
S5_STATE = 64
S5_DT_MIN = 1e-3
S5_DT_MAX = 1e-1
NA_HEADS = 16
NA_HEAD_DIM = D_MODEL // NA_HEADS
NA_ROWS = 8
NA_COLS = 16
NA_STRIP = 2 * NA_COLS


def _layers_of(mixer):
    return len(range(mixer, DEPTH_2, N_MIXERS))

def rmsnorm(x, g):
    xf = x.astype(jnp.float32)
    y = xf * lax.rsqrt(jnp.mean(xf * xf, axis=-1, keepdims=True) + EPS)
    return (y * g.astype(jnp.float32)).astype(x.dtype)

def modulate(h, shift, scale):
    return h * (1 + scale) + shift

def squared_relu_mlp(h, w_in, w_out):
    return jnp.square(jax.nn.relu(h @ w_in)) @ w_out

def depthwise_conv3(u, w):
    return lax.conv_general_dilated(u, w.astype(u.dtype)[:, None, :], window_strides=(1,),
                                    padding=((1, 1),), dimension_numbers=('NWC', 'WIO', 'NWC'),
                                    feature_group_count=u.shape[-1])

def short_gated_conv(h, w_in, conv_w, w_out):
    b_gate, c_gate, v = jnp.split(h @ w_in, 3, axis=-1)
    return (b_gate * depthwise_conv3(c_gate * v, conv_w)) @ w_out

def gla_chunked(q, k, v, log_f, s0):
    bsz, seq, nh, dk = q.shape
    dv = v.shape[-1]
    nc = seq // HG_CHUNK

    def chunks(t):
        return t.reshape(bsz, nc, HG_CHUNK, nh, t.shape[-1]).transpose(1, 0, 3, 2, 4)

    qc, kc, vc = chunks(q.astype(jnp.float32)), chunks(k.astype(jnp.float32)), chunks(v)
    b = jnp.cumsum(chunks(log_f.astype(jnp.float32)), axis=3)
    b_mid = b[:, :, :, HG_CHUNK // 2 - 1:HG_CHUNK // 2]
    b_last = b[:, :, :, -1:]
    scores = jnp.einsum('nbhtk,nbhsk->nbhts', qc * jnp.exp(b - b_mid), kc * jnp.exp(b_mid - b))
    prefix = jnp.tril(jnp.ones((HG_CHUNK, HG_CHUNK), dtype=bool))
    o_intra = jnp.einsum('nbhts,nbhsv->nbhtv', jnp.where(prefix, scores, 0.0), vc)
    q_out = qc * jnp.exp(b)
    k_state = kc * jnp.exp(b_last - b)
    decay_chunk = jnp.exp(b_last[:, :, :, 0, :])

    def step(s, xs):
        q_o, k_s, v_s, a = xs
        o = jnp.einsum('bhtk,bhkv->bhtv', q_o, s)
        s = a[..., None] * s + jnp.einsum('bhtk,bhtv->bhkv', k_s, v_s)
        return s, o

    s_fin, o_inter = lax.scan(step, s0, (q_out, k_state, vc, decay_chunk))
    o = (o_intra + o_inter).transpose(1, 0, 3, 2, 4).reshape(bsz, seq, nh, dv)
    return o, s_fin

def hgrn2_mixer(h_ctx, h_lat, w_in, lower_bound, g_norm, w_out, ctx_out):
    bsz = h_lat.shape[0]
    s0 = jnp.zeros((bsz, HG_HEADS, HG_HEAD_DIM, HG_HEAD_DIM), jnp.float32)

    def heads(t):
        return t.reshape(*t.shape[:2], HG_HEADS, HG_HEAD_DIM)

    def forget(t):
        f = lower_bound + (1 - lower_bound) * jax.nn.sigmoid(t.astype(jnp.float32))
        return heads(1 - f), heads(jnp.log(f))

    def project(h):
        q, inp, gate, f_fwd, f_bwd = jnp.split(h @ w_in, 5, axis=-1)
        return heads(q), heads(inp), gate, forget(f_fwd), forget(f_bwd)

    def flip(t):
        return t[:, ::-1]

    qc, vc, gc, (kcf, lcf), (kcb, lcb) = project(h_ctx)
    ql, vl, gl, (klf, llf), (klb, llb) = project(h_lat)
    oc_f, st_f = gla_chunked(qc, kcf, vc, lcf, s0)
    ol_f, _ = gla_chunked(ql, klf, vl, llf, st_f)
    oc_b, st_b = gla_chunked(flip(qc), flip(kcb), flip(vc), flip(lcb), s0)
    ol_b, _ = gla_chunked(flip(ql), flip(klb), flip(vl), flip(llb), st_b)

    def readout(o, gate):
        o = rmsnorm(o, g_norm.reshape(HG_HEADS, HG_HEAD_DIM))
        o = o.reshape(*o.shape[:2], D_MODEL).astype(gate.dtype)
        return (o * jax.nn.silu(gate)) @ w_out

    y_lat = readout(ol_f + flip(ol_b), gl)
    y_ctx = readout(oc_f + flip(oc_b), gc) if ctx_out else None
    return y_ctx, y_lat

def s5_discretise(lam_re, lam_im, log_dt, b_re, b_im):
    lam_re = jnp.minimum(lam_re.astype(jnp.float32), -1e-4)
    lam_im = lam_im.astype(jnp.float32)
    dt = jnp.exp(log_dt.astype(jnp.float32))[:, None]
    mag = jnp.exp(lam_re * dt)
    a_re, a_im = mag * jnp.cos(lam_im * dt), mag * jnp.sin(lam_im * dt)
    den = lam_re * lam_re + lam_im * lam_im
    f_re = ((a_re - 1) * lam_re + a_im * lam_im) / den
    f_im = (a_im * lam_re - (a_re - 1) * lam_im) / den
    b_re, b_im = b_re.astype(jnp.float32), b_im.astype(jnp.float32)
    bb_re = f_re[..., None] * b_re - f_im[..., None] * b_im
    bb_im = f_re[..., None] * b_im + f_im[..., None] * b_re
    return a_re, a_im, bb_re, bb_im

def s5_scan(bu_re, bu_im, a_re, a_im, init, reverse):
    if init is not None:
        i_re, i_im = init
        first = -1 if reverse else 0
        bu_re = bu_re.at[:, first].add(a_re * i_re - a_im * i_im)
        bu_im = bu_im.at[:, first].add(a_re * i_im + a_im * i_re)
    seq = bu_re.shape[1]
    a_seq_re = jnp.broadcast_to(a_re, (1, seq) + a_re.shape)
    a_seq_im = jnp.broadcast_to(a_im, (1, seq) + a_im.shape)

    def combine(e1, e2):
        a1r, a1i, b1r, b1i = e1
        a2r, a2i, b2r, b2i = e2
        return (a2r * a1r - a2i * a1i, a2r * a1i + a2i * a1r,
                a2r * b1r - a2i * b1i + b2r, a2r * b1i + a2i * b1r + b2i)

    _, _, x_re, x_im = lax.associative_scan(combine, (a_seq_re, a_seq_im, bu_re, bu_im),
                                            axis=1, reverse=reverse)
    return x_re, x_im

def s5_mixer(h_ctx, h_lat, lam_re, lam_im, log_dt, b_re, b_im, c_re, c_im, d_skip, w_glu, ctx_out):
    def grouped(h):
        return h.reshape(*h.shape[:2], S5_GROUPS, S5_GROUP).astype(jnp.float32)

    u_c, u_l = grouped(h_ctx), grouped(h_lat)
    d = d_skip.reshape(S5_GROUPS, S5_GROUP).astype(jnp.float32)
    y_c, y_l = d * u_c, d * u_l
    for direction in range(2):
        reverse = direction == 1
        a_re, a_im, bb_re, bb_im = s5_discretise(lam_re[direction], lam_im[direction],
                                                 log_dt[direction], b_re, b_im)
        cr, ci = c_re[direction].astype(jnp.float32), c_im[direction].astype(jnp.float32)

        def drive(u):
            return (jnp.einsum('bsgc,gnc->bsgn', u, bb_re), jnp.einsum('bsgc,gnc->bsgn', u, bb_im))

        def readout(xr, xi):
            return jnp.einsum('bsgn,gcn->bsgc', xr, cr) - jnp.einsum('bsgn,gcn->bsgc', xi, ci)

        xc_re, xc_im = s5_scan(*drive(u_c), a_re, a_im, None, reverse)
        end = 0 if reverse else -1
        xl_re, xl_im = s5_scan(*drive(u_l), a_re, a_im, (xc_re[:, end], xc_im[:, end]), reverse)
        y_l = y_l + readout(xl_re, xl_im)
        if ctx_out:
            y_c = y_c + readout(xc_re, xc_im)

    def glu(y):
        z = jax.nn.gelu(y.reshape(*y.shape[:2], D_MODEL)).astype(w_glu.dtype)
        val, gate = jnp.split(z @ w_glu, 2, axis=-1)
        return val * jax.nn.sigmoid(gate)

    return (glu(y_c) if ctx_out else None), glu(y_l)

def neighbourhood_attention(h_ctx, h_lat, w_qkv, rpb, w_out, ctx_out):
    bsz, seq, _ = h_lat.shape
    rows = seq // GRID_W
    kr = min(NA_ROWS, rows)
    n_cb = GRID_W // NA_COLS
    n_loc = kr * NA_STRIP
    scale = NA_HEAD_DIM ** -0.5

    def heads(t):
        return t.reshape(*t.shape[:2], NA_HEADS, NA_HEAD_DIM)

    q_l, k_l, v_l = (heads(t) for t in jnp.split(h_lat @ w_qkv, 3, axis=-1))
    k_c, v_c = (heads(t) for t in jnp.split(h_ctx @ w_qkv[:, D_MODEL:], 2, axis=-1))

    r = jnp.arange(rows)
    key_rows = jnp.clip(r - kr // 2, 0, rows - kr)[:, None] + jnp.arange(kr)
    qcol = (jnp.arange(n_cb) * NA_COLS)[:, None] + jnp.arange(NA_COLS)
    key_cols = (jnp.clip(jnp.arange(n_cb) * NA_COLS - NA_COLS // 2, 0, GRID_W - NA_STRIP)[:, None]
                + jnp.arange(NA_STRIP))
    q_start = jnp.clip(qcol - NA_COLS // 2, 0, GRID_W - NA_COLS)[..., None]
    kcol = key_cols[:, None, :]
    in_win = jnp.tile((kcol >= q_start) & (kcol < q_start + NA_COLS), (1, 1, kr))
    dr = key_rows - r[:, None] + (NA_ROWS - 1)
    dc = jnp.clip(kcol - qcol[..., None], 1 - NA_COLS, NA_COLS - 1) + (NA_COLS - 1)
    bias = rpb[:, dr[:, None, None, :, None], dc[None, :, :, None, :]]
    bias = bias.reshape(NA_HEADS, rows, n_cb, NA_COLS, n_loc).astype(jnp.float32)

    def gather(t):
        g = t.reshape(bsz, rows, GRID_W, NA_HEADS, NA_HEAD_DIM)
        g = g[:, key_rows[:, None, :, None], key_cols[None, :, None, :]]
        return g.reshape(bsz, rows, n_cb, n_loc, NA_HEADS, NA_HEAD_DIM)

    q_b = q_l.reshape(bsz, rows, n_cb, NA_COLS, NA_HEADS, NA_HEAD_DIM)
    k_win, v_win = gather(k_l), gather(v_l)
    s_loc = jnp.einsum('brjqhd,brjkhd->bhrjqk', q_b, k_win).astype(jnp.float32) * scale + bias
    s_loc = jnp.where(in_win, s_loc, -jnp.inf)
    s_ctx = jnp.einsum('brjqhd,bkhd->bhrjqk', q_b, k_c).astype(jnp.float32) * scale
    p = jax.nn.softmax(jnp.concatenate([s_loc, s_ctx], axis=-1), axis=-1).astype(v_l.dtype)
    o = (jnp.einsum('bhrjqk,brjkhd->brjqhd', p[..., :n_loc], v_win)
         + jnp.einsum('bhrjqk,bkhd->brjqhd', p[..., n_loc:], v_c))
    y_lat = o.reshape(bsz, seq, D_MODEL) @ w_out
    y_ctx = None
    if ctx_out:
        q_c = heads(h_ctx @ w_qkv[:, :D_MODEL])
        s_cc = jnp.einsum('bqhd,bkhd->bhqk', q_c, k_c).astype(jnp.float32) * scale
        p_cc = jax.nn.softmax(s_cc, axis=-1).astype(v_c.dtype)
        o_c = jnp.einsum('bhqk,bkhd->bqhd', p_cc, v_c)
        y_ctx = o_c.reshape(bsz, h_ctx.shape[1], D_MODEL) @ w_out
    return y_ctx, y_lat

def second_inputs(seed: int = 0) -> dict:
    key = jax.random.key(seed)
    keys = iter(jax.random.split(key, 32))
    f32 = jnp.float32

    def normal(shape, std):
        return jax.random.normal(next(keys), shape, f32) * std

    n_a, n_b, n_c, n_d = (_layers_of(m) for m in range(N_MIXERS))
    d = D_MODEL
    lam_shape = (n_c, 2, S5_GROUPS, S5_STATE)
    return {
        'x': normal((BATCH, SEQ, d), 1.0),
        'c': normal((BATCH, d), 1.0),
        'ctx': normal((BATCH, CTX_LEN, d), 1.0),
        'c_ctx': normal((d,), 1.0),
        'ada_w': normal((DEPTH_2, d, N_MOD * d), 0.5 * d ** -0.5),
        'ada_b': normal((DEPTH_2, N_MOD * d), 0.02),
        'norm_gains': 1.0 + normal((DEPTH_2, 4, d), 0.02),
        'mlp_w_in': normal((DEPTH_2, d, D_FF_2), d ** -0.5),
        'mlp_w_out': normal((DEPTH_2, D_FF_2, d), D_FF_2 ** -0.5),
        'sc_w_in': normal((n_a, d, 3 * d), d ** -0.5),
        'sc_conv': normal((n_a, CONV_W, d), CONV_W ** -0.5),
        'sc_w_out': normal((n_a, d, d), d ** -0.5),
        'hg_w_in': normal((n_b, d, 5 * d), d ** -0.5),
        'hg_lower_bound': normal((DEPTH_2, d), 0.1),
        'hg_norm': 1.0 + normal((n_b, d), 0.02),
        'hg_w_out': normal((n_b, d, d), d ** -0.5),
        's5_lam_re': -0.5 + normal(lam_shape, 0.01),
        's5_lam_im': math.pi * jnp.arange(S5_STATE, dtype=f32) + normal(lam_shape, 0.01),
        's5_log_dt': jax.random.uniform(next(keys), (n_c, 2, S5_GROUPS), f32,
                                        math.log(S5_DT_MIN), math.log(S5_DT_MAX)),
        's5_b_re': normal((n_c, S5_GROUPS, S5_STATE, S5_GROUP), (2 * S5_GROUP) ** -0.5),
        's5_b_im': normal((n_c, S5_GROUPS, S5_STATE, S5_GROUP), (2 * S5_GROUP) ** -0.5),
        's5_c_re': normal((n_c, 2, S5_GROUPS, S5_GROUP, S5_STATE), (2 * S5_STATE) ** -0.5),
        's5_c_im': normal((n_c, 2, S5_GROUPS, S5_GROUP, S5_STATE), (2 * S5_STATE) ** -0.5),
        's5_d': normal((n_c, d), 1.0),
        's5_w_glu': normal((n_c, d, 2 * d), d ** -0.5),
        'na_w_qkv': normal((n_d, d, 3 * d), d ** -0.5),
        'na_rpb': normal((n_d, NA_HEADS, 2 * NA_ROWS - 1, 2 * NA_COLS - 1), 0.1),
        'na_w_out': normal((n_d, d, d), d ** -0.5),
    }

def second_block(x, c, ctx, c_ctx, ada_w, ada_b, norm_gains, mlp_w_in, mlp_w_out,
              sc_w_in, sc_conv, sc_w_out, hg_w_in, hg_lower_bound, hg_norm, hg_w_out,
              s5_lam_re, s5_lam_im, s5_log_dt, s5_b_re, s5_b_im, s5_c_re, s5_c_im, s5_d, s5_w_glu,
              na_w_qkv, na_rpb, na_w_out):
    lb_all = jnp.cumsum(jax.nn.softmax(hg_lower_bound.astype(jnp.float32), axis=0), axis=0)
    lb_all = lb_all - lb_all[0]
    h_lat, h_ctx = x, ctx
    for i in range(DEPTH_2):
        kind, j = i % N_MIXERS, i // N_MIXERS
        ctx_out = i < DEPTH_2 - 1
        mod_lat = [m[:, None, :] for m in jnp.split(jax.nn.silu(c) @ ada_w[i] + ada_b[i], N_MOD, axis=-1)]
        mod_ctx = jnp.split(jax.nn.silu(c_ctx) @ ada_w[i] + ada_b[i], N_MOD, axis=-1)
        g_pre, g_post, g_pre_ff, g_post_ff = norm_gains[i]
        a_lat = modulate(rmsnorm(h_lat, g_pre), mod_lat[0], mod_lat[1])
        a_ctx = modulate(rmsnorm(h_ctx, g_pre), mod_ctx[0], mod_ctx[1]) if (ctx_out or kind != 0) else None
        if kind == 0:
            y_lat = short_gated_conv(a_lat, sc_w_in[j], sc_conv[j], sc_w_out[j])
            y_ctx = short_gated_conv(a_ctx, sc_w_in[j], sc_conv[j], sc_w_out[j]) if ctx_out else None
        elif kind == 1:
            y_ctx, y_lat = hgrn2_mixer(a_ctx, a_lat, hg_w_in[j], lb_all[i], hg_norm[j], hg_w_out[j], ctx_out)
        elif kind == 2:
            y_ctx, y_lat = s5_mixer(a_ctx, a_lat, s5_lam_re[j], s5_lam_im[j], s5_log_dt[j], s5_b_re[j],
                                    s5_b_im[j], s5_c_re[j], s5_c_im[j], s5_d[j], s5_w_glu[j], ctx_out)
        else:
            y_ctx, y_lat = neighbourhood_attention(a_ctx, a_lat, na_w_qkv[j], na_rpb[j], na_w_out[j], ctx_out)
        h_lat = h_lat + mod_lat[2] * rmsnorm(y_lat.astype(h_lat.dtype), g_post)
        if ctx_out:
            h_ctx = h_ctx + mod_ctx[2] * rmsnorm(y_ctx.astype(h_ctx.dtype), g_post)
        f_lat = squared_relu_mlp(modulate(rmsnorm(h_lat, g_pre_ff), mod_lat[3], mod_lat[4]), mlp_w_in[i], mlp_w_out[i])
        h_lat = h_lat + mod_lat[5] * rmsnorm(f_lat.astype(h_lat.dtype), g_post_ff)
        if ctx_out:
            f_ctx = squared_relu_mlp(modulate(rmsnorm(h_ctx, g_pre_ff), mod_ctx[3], mod_ctx[4]), mlp_w_in[i], mlp_w_out[i])
            h_ctx = h_ctx + mod_ctx[5] * rmsnorm(f_ctx.astype(h_ctx.dtype), g_post_ff)
    return h_lat


def setup_inputs(seed=0):
    out = dict(first_inputs(seed))
    for name, value in second_inputs(seed + 1).items():
        if name != "x":
            out[name + "_2"] = value
    return out


def reference(
    x, even_w_in, pool_w, pool_scale, conv_w, conv_b, dt_bias, a_log, d_skip, ssm_norm_w,
    even_w_out, odd_w_in, fgate_b, q_norm_w, w_uq, kv_norm_w, w_ukv, odd_w_out, ffn_w_gate,
    ffn_w_up, ffn_w_down, ln_mix_g, ln_mix_b, ln_ffn_g, ln_ffn_b, c_2, ctx_2, c_ctx_2, ada_w_2,
    ada_b_2, norm_gains_2, mlp_w_in_2, mlp_w_out_2, sc_w_in_2, sc_conv_2, sc_w_out_2, hg_w_in_2,
    hg_lower_bound_2, hg_norm_2, hg_w_out_2, s5_lam_re_2, s5_lam_im_2, s5_log_dt_2, s5_b_re_2,
    s5_b_im_2, s5_c_re_2, s5_c_im_2, s5_d_2, s5_w_glu_2, na_w_qkv_2, na_rpb_2, na_w_out_2,
):
    x = first_block(
        x, even_w_in, pool_w, pool_scale, conv_w, conv_b, dt_bias, a_log, d_skip, ssm_norm_w,
        even_w_out, odd_w_in, fgate_b, q_norm_w, w_uq, kv_norm_w, w_ukv, odd_w_out, ffn_w_gate,
        ffn_w_up, ffn_w_down, ln_mix_g, ln_mix_b, ln_ffn_g, ln_ffn_b,
    )
    return second_block(
        x, c_2, ctx_2, c_ctx_2, ada_w_2, ada_b_2, norm_gains_2, mlp_w_in_2, mlp_w_out_2,
        sc_w_in_2, sc_conv_2, sc_w_out_2, hg_w_in_2, hg_lower_bound_2, hg_norm_2, hg_w_out_2,
        s5_lam_re_2, s5_lam_im_2, s5_log_dt_2, s5_b_re_2, s5_b_im_2, s5_c_re_2, s5_c_im_2,
        s5_d_2, s5_w_glu_2, na_w_qkv_2, na_rpb_2, na_w_out_2,
    )


_drawn_inputs = setup_inputs


def setup_inputs(seed=0):
    import zlib

    import numpy as np

    out = dict(_drawn_inputs(seed))
    spreads = {}
    factors = {'pool_scale': 3.017,
     'conv_b': 8.0,
     'q_norm_w': 8.0,
     'kv_norm_w': 7.732,
     'norm_gains_2': 4.045}
    for name, (base, spread) in spreads.items():
        noise = np.random.default_rng([zlib.crc32(name.encode()), seed]).standard_normal(out[name].shape)
        drawn = base * np.exp(spread * noise) if base else spread * noise
        out[name] = jnp.asarray(drawn.astype(out[name].dtype))
    for name, factor in factors.items():
        out[name] = (out[name] * factor).astype(out[name].dtype)
    return out
```

```python
from contextlib import ExitStack

import numpy as np
import concourse.bass as bass
from concourse import mybir

F32 = mybir.dt.float32
F32R = mybir.dt.float32r
ALU = mybir.AluOpType
ACT = mybir.ActivationFunctionType
AX = mybir.AxisListType

P = 128
S = 256
D = 1024
KT = D // P
CH = 2048
RING = 3
HEADS = 16
FOX_H = 8
MLA_H = 8
D_FF = 2816
D_FF2 = 4096
ALPHA = (2 * 2) ** 0.25
LN_EPS = 1e-5
RMS_EPS = 1e-6
NEG = -1e30

CONST_COLS = {}
_at = 0
for _n, _w in (("ident", 128), ("triu", 128), ("attn_mask", 384), ("ssm_mask", 128), ("cos", 256), ("sin", 256),
               ("swap", 96), ("inv_count", 64)):
    CONST_COLS[_n] = (_at, _w)
    _at += _w
CONST_W = _at
ROPE_ROW = 64


def shape_constants():
    c = np.zeros((P, CONST_W), np.float32)

    def put(name, a):
        o, w = CONST_COLS[name]
        c[:a.shape[0], o:o + w] = a

    i, j = np.arange(P)[:, None], np.arange(P)[None, :]
    put("ident", (i == j).astype(np.float32))
    put("triu", (i <= j).astype(np.float32))
    causal = np.where(j <= i, 0, NEG).astype(np.float32)
    put("attn_mask", np.concatenate([causal, np.zeros((P, P), np.float32), causal], 1))
    put("ssm_mask", np.where(i <= j, 0, NEG).astype(np.float32))
    half = 16
    freqs = np.power(np.float32(10000.0), -np.arange(half, dtype=np.float32) / np.float32(half)).astype(np.float32)
    ang = (freqs[:, None] * np.arange(S, dtype=np.float32)[None, :]).astype(np.float32)
    cos, sin = np.ones((96, S), np.float32), np.zeros((96, S), np.float32)
    cos[64:80] = cos[80:96] = np.cos(ang)
    sin[64:80], sin[80:96] = -np.sin(ang), np.sin(ang)
    put("cos", cos)
    put("sin", sin)
    swap = np.zeros((96, 96), np.float32)
    for r in range(half):
        swap[ROPE_ROW + half + r, ROPE_ROW + r] = swap[ROPE_ROW + r, ROPE_ROW + half + r] = 1
    put("swap", swap)
    t = np.arange(16)
    put("inv_count", np.tile(np.concatenate([1 / np.minimum(t + 1, w) for w in (2, 4, 8, 16)])[None], (P, 1)).astype(np.float32))
    return c


def build(nc, A, out, stop=None):
    ctx = ExitStack()
    with ctx:
        def sb(name, shape, dt=F32, stack=ctx):
            return stack.enter_context(nc.sbuf_tensor(name, shape, dt))

        sems = {}

        def sem(name):
            if name not in sems:
                sems[name] = ctx.enter_context(nc.semaphore(name))
            return sems[name]

        raw = sb("raw", [P, RING, CH])
        w_hi = sb("w_hi", [P, RING, CH], F32R)
        w_lo = sb("w_lo", [P, RING, CH], F32R)
        x = sb("x_res", [P, KT, S])
        x_hi = sb("x_hi", [P, KT, S], F32R)
        x_lo = sb("x_lo", [P, KT, S], F32R)
        r = sb("r", [P, KT, S])
        sq = sb("sq", [P, KT, S])
        const = sb("const", [P, CONST_W])
        vecs = sb("vecs", [P, 3, P])
        ones = sb("ones", [P, P])
        mean_w = sb("mean_w", [P, P])
        d_skip = sb("d_skip_sb", [P, KT])
        head_vec = sb("head_vec", [16, 4])
        std = sb("std", [P, 2])
        eps_sb = sb("eps_sb", [P, 2])
        rstd = sb("rstd", [P, 2])
        mod = sb("mod", [P, 48])
        gain = sb("gain", [P, 32])
        silu_c = sb("silu_c", [P, KT])
        small = sb("small", [16, 4, S])
        hid = sb("hid", [P, 3, 2, S])
        gate_s = sb("gate_s", [P, 2, 2, S])
        hid_hi = sb("hid_hi", [P, 3, 2, S], F32R)
        hid_lo = sb("hid_lo", [P, 3, 2, S], F32R)

        with ExitStack() as even:
            pool_hi = sb("pool_hi", [P, 4, S], F32R, even)
            pool_lo = sb("pool_lo", [P, 4, S], F32R, even)
            pool_y = sb("pool_y", [P, 4, S], F32, even)
            u_pad = sb("u_pad", [P, 4, 16 + S], F32, even)
            wins = sb("wins", [P, 2, 4, 16 + S], F32, even)
            z_silu = sb("z_silu", [P, KT, S], F32, even)
            conv_in = sb("conv_in", [P, 2, 2, 3 + S], F32, even)
            conv_acc = sb("conv_acc", [P, 2, 2, S], F32, even)
            xbc = sb("xbc", [P, 12, S], F32, even)
            tok = sb("tok", [P, 2, 32], F32, even)
            neg_acs = sb("neg_acs", [P, 2, 16], F32, even)
            decay = sb("decay", [P, 2, 16], F32, even)
            b_tok = sb("b_tok", [P, 2 * P], F32, even)
            cb = sb("cb", [P, 4, P], F32, even)
            state = sb("state", [P, D], F32, even)
        win_a, win_b = wins[:, 0, :, :], wins[:, 1, :, :]
        e_acs = wins[:, :, :, :].rearrange("p a g s -> p (a g s)")[:, 0:HEADS * P].rearrange("p (h s) -> p h s", h=HEADS)
        x_dt = hid[:, 0:2, :, :].rearrange("p a b s -> p (a b s)")
        x_dec = gate_s[:, :, :, :].rearrange("p a b s -> p (a b s)")
        seg = hid[:, 2, :, :].rearrange("p b s -> p (b s)")
        lmat = sq[:, :, :].rearrange("p k (a s) -> p (k a) s", a=2)
        rows = [sb(f"vec_rows{i}", [P, P]) for i in range(3)]
        pool_w_sb = sb("pool_w_sb", [P, 4, P])

        with ExitStack() as ada:
            ada_raw = sb("ada_raw", [P, 2, CH], F32, ada)
            ada_acc = sb("ada_acc", [P, 3, CH], F32, ada)

        with ExitStack() as odd:
            qz = sb("qz", [P, FOX_H, S], F32, odd)
            kf = sb("kf", [P, 4, S], F32, odd)
            v_tok = sb("v_tok", [P, 2, 512], F32, odd)
            neg_f = sb("neg_f", [P, S], F32, odd)
            cq = sb("cq", [P, 4, S], F32, odd)
            cq_hi = sb("cq_hi", [P, 4, S], F32R, odd)
            cq_lo = sb("cq_lo", [P, 4, S], F32R, odd)
            ckv = sb("ckv", [P, 2, S], F32, odd)
            ckv_hi = sb("ckv_hi", [P, 2, S], F32R, odd)
            ckv_lo = sb("ckv_lo", [P, 2, S], F32R, odd)
            qm = sb("qm", [96, MLA_H, S], F32, odd)
            km = sb("km", [96, MLA_H, S], F32, odd)
            kr = sb("kr", [96, 2, S], F32, odd)
            vm_tok = sb("vm_tok", [P, 2, 512], F32, odd)
            row_max = sb("row_max", [P, 2, 2], F32, odd)
            row_sum = sb("row_sum", [P, 2, 2], F32, odd)

        hid_flat = hid[:, :, :, :].rearrange("p a b s -> p (a b s)")
        prob = hid_flat[:, 0:768].rearrange("p (a n) -> p a n", a=2)
        prob_t = hid_flat[:, 768:1536].rearrange("p (a n) -> p a n", a=2)
        sc_sb = x_dec[:, 0:768].rearrange("p (a n) -> p a n", a=2)

        with ExitStack() as conv2:
            c_sb = sb("c_sb", [P, 2, 2, S], F32, conv2)
            b_sb = sb("b_sb", [P, 2, 2, S], F32, conv2)
            cv = sb("cv", [P, 2, 2, 1 + S + 1], F32, conv2)
            cv_acc = sb("cv_acc", [P, 2, 2, S], F32, conv2)

        def cst(name, rows_=P):
            o, w = CONST_COLS[name]
            return const[0:rows_, o:o + w]

        ident, triu = cst("ident"), cst("triu")

        def vec(t, c):
            return vecs[:, t, c:c + 1]

        PS = ctx.enter_context(nc.psum_tensor("PS", [P, 8, 512], F32))
        ACC = [PS[:, n // 2, (n % 2) * S:(n % 2) * S + S] for n in range(8)]

        def bank2(b):
            return PS[:, b, :].rearrange("p (a s) -> p a s", a=2)

        chunks = []
        first = {}

        def col_chunk(w, k, c0, n, copies=1):
            chunks.append((w[0:k * P, c0:c0 + n].rearrange("(k p) n -> p k n", p=P), k, n, copies))

        def row_chunk(w, r0):
            chunks.append((w[r0:r0 + 2 * P, :].rearrange("(k p) n -> p k n", p=P), 2, D, 1))

        E_IN, O_IN = A["even_w_in"][0], A["odd_w_in"][0]
        XBC0, DT0 = 512 + 1024, 512 + 1024 + 1536
        first["even"] = len(chunks)
        col_chunk(E_IN, 8, DT0, 16, 8)
        for c in (XBC0 + 1024, XBC0 + 1280, XBC0, XBC0 + 256, XBC0 + 512, XBC0 + 768, 0, 256, 512, 768, 1024, 1280):
            col_chunk(E_IN, 8, c, 256)
        first["even_out"] = len(chunks)
        for q in range(6):
            row_chunk(A["even_w_out"][0], 2 * P * q)

        def ffn_chunks(name, gate, up, down, n):
            first[name] = len(chunks)
            col_chunk(gate, 8, 0, 256)
            col_chunk(up, 8, 0, 256)
            for i in range(1, n):
                col_chunk(gate, 8, 256 * i, 256)
                col_chunk(up, 8, 256 * i, 256)
                row_chunk(down, 256 * (i - 1))
            row_chunk(down, 256 * (n - 1))

        NF = D_FF // 256
        ffn_chunks("ffn0", A["ffn_w_gate"][0], A["ffn_w_up"][0], A["ffn_w_down"][0], NF)
        first["odd"] = len(chunks)
        col_chunk(O_IN, 8, 1536, 8, 16)
        for c in (512, 768, 0, 256, 1024, 1280, 1544, 1800, 2056):
            col_chunk(O_IN, 8, c, 256)
        col_chunk(O_IN, 8, 2312, 32, 3)
        chunks.append((A["w_uq"][0][:, 0:384].rearrange("(k p) n -> p k n", p=P), 4, 384, 1))
        chunks.append((A["w_uq"][0][:, 384:768].rearrange("(k p) n -> p k n", p=P), 4, 384, 1))
        chunks.append((A["w_ukv"][0].rearrange("(k p) n -> p k n", p=P), 2, 1024, 1))
        first["odd_out"] = len(chunks)
        for q in range(4):
            row_chunk(A["odd_w_out"][0], 2 * P * q)
        ffn_chunks("ffn1", A["ffn_w_gate"][1], A["ffn_w_up"][1], A["ffn_w_down"][1], NF)
        first["sc"] = len(chunks)
        SC_IN = A["sc_w_in_2"][0]
        for q in range(4):
            for part in (1, 2, 0):
                col_chunk(SC_IN, 8, part * D + 256 * q, 256)
            if q:
                row_chunk(A["sc_w_out_2"][0], 256 * (q - 1))
        row_chunk(A["sc_w_out_2"][0], 768)
        first["mlp"] = len(chunks)
        NM = D_FF2 // 256
        col_chunk(A["mlp_w_in_2"][0], 8, 0, 256)
        for i in range(1, NM):
            col_chunk(A["mlp_w_in_2"][0], 8, 256 * i, 256)
            row_chunk(A["mlp_w_out_2"][0], 256 * (i - 1))
        row_chunk(A["mlp_w_out_2"][0], 256 * (NM - 1))
        first["end"] = len(chunks)

        order = ["even", "ffn0", "odd", "ffn1", "sc", "mlp", "end"]
        n_chunks = first[order[order.index(stop) + 1]] if stop else len(chunks)
        last_stage = order.index(stop) if stop else len(order) - 1

        def on(stage):
            return order.index(stage) <= last_stage

        def slot(t, c):
            _, k, n, copies = chunks[c]
            n *= 1 if t is raw else copies
            return t[:, c % RING, 0:k * n].rearrange("p (k n) -> p k n", k=k)

        def split_view(t, c):
            _, k, n, copies = chunks[c]
            if copies == 1:
                return slot(t, c)
            if t is raw:
                return slot(t, c).rearrange("p k (o n) -> p k o n", o=1).to_broadcast([P, k, copies, n])
            return slot(t, c).rearrange("p k (o n) -> p k o n", o=copies)

        raw_landed = [sem(f"raw_landed{i}") for i in range(RING)]
        hi_split, lo_split, chunk_used = sem("hi_split"), sem("lo_split"), sem("chunk_used")

        NORM_TILES = {"ssm": 8, "ln0": 8, "ln1": 8, "qn": 4, "kvn": 2, "ln2": 8, "ln3": 8, "pre": 8, "post": 8,
                      "preff": 8, "postff": 8}

        def norm_incs(name, kind):
            pairs = NORM_TILES[name] // 2
            if kind in ("resid", "mean", "cent"):
                return (1 if kind == "mean" else 4) if name in LNS else 0
            if kind in ("hi", "full", "lo"):
                return 0 if name in ("ln3", "post", "postff") else 2 * pairs if kind == "hi" else pairs
            return pairs if kind in ("sq", "scaled") else 1

        def norm(name, kind, n):
            before = 0
            for other in NORM_TILES:
                if other == name:
                    return sem(f"norm_{kind}"), before + n
                before += norm_incs(other, kind)

        LNS = {"ln0": (60, 76), "ln1": (92, 108), "ln2": (68, 84), "ln3": (100, 116)}

        def ada_step(pool, n):
            b, k = n // KT, n % KT
            pool.wait_ge(sem(f"ada_landed{n % 2}"), 16 * (n // 2 + 1))
            if k:
                raw_n = ada_raw[:, n % 2, :]
                pool.tensor_scalar(raw_n, raw_n, silu_c[:, k:k + 1], None, ALU.mult).then_inc(sem("ada_scaled"), 1)
                pool.wait_ge(sem("ada_scaled"), n - b)
                pool.wait_ge(sem("ada_fma"), n)
                pool.tensor_tensor(ada_acc[:, b, :], ada_acc[:, b, :], raw_n, ALU.add).then_inc(sem("ada_fma"), 1)
            else:
                pool.tensor_scalar(ada_acc[:, b, :], ada_raw[:, n % 2, :], silu_c[:, k:k + 1], None, ALU.mult)\
                    .then_inc(sem("ada_fma"), 1)

        def conv_silu(act, p):
            t = 8 + 2 * (p - 1) if p <= 2 else 2 * (p - 3)
            act.wait_ge(sem("conv_done"), p)
            act.activation(xbc[:, t:t + 2, :], conv_acc[:, p % 2, :, :], ACT.Silu).then_inc(sem("xbc_ready"), 1)

        block = ctx.enter_context(nc.Block())

        @block.sync
        def _(sp):
            for c in range(n_chunks):
                if c >= RING:
                    sp.wait_ge(lo_split, c - RING + 1)
                sp.dma_start(slot(raw, c), chunks[c][0]).then_inc(raw_landed[c % RING], 16)
            if stop:
                return
            for t in range(2):
                sp.wait_ge(sem("out_rows"), t + 1)
                sp.dma_start(out[0, t * P:(t + 1) * P, :], sq[:, 4 * t:4 * t + 4, :].rearrange("p a s -> p (a s)"))\
                  .then_inc(sem("stored"), 16)
            sp.wait_ge(sem("stored"), 32)

        @block.gpsimd
        def _(pool):
            for t in range(2):
                pool.dma_start(sq[:, 4 * t:4 * t + 4, :].rearrange("p a s -> p (a s)"),
                               A["x"][0, t * P:(t + 1) * P, :]).then_inc(sem("x_landed"), 16)
            pool.dma_start(const[:, :], A["consts"]).then_inc(sem("const_landed"), 16)
            v1, v2, v3 = rows
            n_rows = 0
            for dst, o, n, src in (
                (v1, 0, 48, A["conv_w"][0].rearrange("j (t p) -> (j t) p", p=P)),
                (v1, 48, 12, A["conv_b"][0].rearrange("(t p) -> t p", p=P)),
                (v1, 60, 16, A["ln_mix_g"].rearrange("l (t p) -> (l t) p", p=P)),
                (v1, 76, 16, A["ln_mix_b"].rearrange("l (t p) -> (l t) p", p=P)),
                (v1, 92, 16, A["ln_ffn_g"].rearrange("l (t p) -> (l t) p", p=P)),
                (v1, 108, 16, A["ln_ffn_b"].rearrange("l (t p) -> (l t) p", p=P)),
                (v2, 0, 4, A["pool_scale"][0].rearrange("(t p) -> t p", p=P)),
                (v2, 4, 8, A["ssm_norm_w"][0].rearrange("(t p) -> t p", p=P)),
                (v2, 12, 4, A["q_norm_w"][0].rearrange("(t p) -> t p", p=P)),
                (v2, 16, 2, A["kv_norm_w"][0].rearrange("(t p) -> t p", p=P)),
                (v2, 18, 32, A["norm_gains_2"][0].rearrange("i (t p) -> (i t) p", p=P)),
                (v2, 50, 24, A["sc_conv_2"][0].rearrange("j (t p) -> (j t) p", p=P)),
                (v3, 0, 48, A["ada_b_2"][0].rearrange("(t p) -> t p", p=P)),
                (v3, 48, 8, A["c_2"][0].rearrange("(t p) -> t p", p=P)),
            ):
                pool.dma_start(dst[o:o + n, :], src).then_inc(sem("rows_landed"), 16)
                n_rows += 1
            assert n_rows == 14
            pool.memset(ones[:, :], 1.0).then_inc(sem("fixed"), 1)
            pool.memset(mean_w[:, :], 1.0 / D).then_inc(sem("fixed"), 1)
            with nc.allow_non_contiguous_dma(reason="a few small vectors"):
                for i, (name, n) in enumerate((("dt_bias", 16), ("a_log", 16), ("fgate_b", 8))):
                    pool.dma_start(head_vec[0:n, (0, 1, 3)[i]:(0, 1, 3)[i] + 1],
                                   A[name].rearrange("a (h o) -> (a h) o", o=1)).then_inc(sem("heads_landed"), 16)
                for e in range(2):
                    pool.dma_start(d_skip[64 * e:64 * e + 64, :],
                                   A["d_skip"][0:1, e::2].to_broadcast([64, KT])).then_inc(sem("heads_landed"), 16)
            pool.dma_start(pool_w_sb[:, :, :], A["pool_w"][0].rearrange("g c d -> c g d")).then_inc(sem("poolw_landed"), 16)

            for t in (u_pad[:, :, 0:16], win_a[:, :, 0:16], win_b[:, :, 0:16]):
                pool.memset(t, 0.0).then_inc(sem("pad_zero"), 1)
            pool.wait_ge(sem("pad_zero"), 3)
            pool.wait_ge(sem("even_evac"), 8)
            src = u_pad
            for lv, dst in enumerate((win_a, win_b, win_a, win_b)):
                sh = 1 << lv
                pool.tensor_tensor(dst[:, lv:4, 16:16 + S], src[:, lv:4, 16:16 + S], src[:, lv:4, 16 - sh:16 - sh + S],
                                   ALU.add).then_inc(sem("window"), 1)
                pool.wait_ge(sem("window"), lv + 1)
                src = dst
            for g, w in enumerate((2, 4, 8, 16)):
                t = (win_a, win_b)[g % 2]
                if g == 0:
                    pool.wait_ge(sem("const_landed"), 16)
                o = CONST_COLS["inv_count"][0] + 16 * g
                pool.tensor_tensor(t[:, g, 16:32], t[:, g, 16:32], const[:, o:o + 16], ALU.mult).then_inc(sem("window"), 1)
                pool.tensor_scalar(t[:, g, 32:16 + S], t[:, g, 32:16 + S], 1.0 / w, None, ALU.mult).then_inc(sem("window"), 1)
                pool.wait_ge(sem("window"), 4 + 2 * g + 2)
                pool.tensor_tensor(pool_y[:, g, :], t[:, g, 16:16 + S], u_pad[:, g, 16:16 + S], ALU.subtract)\
                    .then_inc(sem("pool_diff"), 1)

            if on("ffn0"):
                pool.wait_ge(*norm("ln0", "lo", 4))
                n = 0
                for b in range(3):
                    for k in range(KT):
                        if n >= 2:
                            pool.wait_ge(sem("ada_fma"), n - 1)
                        pool.dma_start(ada_raw[:, n % 2, :], A["ada_w_2"][0][k * P:(k + 1) * P, b * CH:(b + 1) * CH])\
                            .then_inc(sem(f"ada_landed{n % 2}"), 16)
                        if n == 0:
                            pool.wait_ge(sem("silu_c_ready"), 1)
                        if n >= 1:
                            ada_step(pool, n - 1)
                        n += 1
                ada_step(pool, n - 1)

        @block.tensor
        def _(pe):
            def mm3(dst, c, cols, k, hi, lo, start, stop_, kk=None):
                kk = k if kk is None else kk
                wh, wl = slot(w_hi, c)[:, kk, cols], slot(w_lo, c)[:, kk, cols]
                pe.matmul(dst, wh, hi, start=start, stop=False, skip_group_check=True)
                pe.matmul(dst, wh, lo, start=False, stop=False, skip_group_check=True)
                return pe.matmul(dst, wl, hi, start=False, stop=stop_, skip_group_check=True)

            def col(c, bank, hi, lo, operand=None):
                _, kt, n, copies = chunks[c]
                n *= copies
                pe.wait_ge(lo_split, c + 1)
                for m in range(0, n, P):
                    w = min(P, n - m)
                    for k in range(kt):
                        if operand and m == 0 and k % 2 == 0:
                            pe.wait_ge(operand[0], operand[1] + k // 2 + 1)
                        last = mm3(PS[0:w, bank, (m // P) * S:(m // P) * S + S], c, slice(m, m + w), k,
                                   hi[:, k, :], lo[:, k, :], k == 0, k == kt - 1)
                last.then_inc(chunk_used, 1)

            def rows_acc(c, hi, lo, k_first, k_last):
                pe.wait_ge(lo_split, c + 1)
                for kk in range(2):
                    for n in range(8):
                        last = mm3(ACC[n], c, slice(n * P, n * P + P), 0, hi[:, kk, :], lo[:, kk, :],
                                   k_first and kk == 0 and n % 2 == 0, k_last and kk == 1, kk=kk)
                last.then_inc(chunk_used, 1)

            def norm_mean(name):
                for k in range(KT):
                    if k % 2 == 0:
                        pe.wait_ge(*norm(name, "resid", k // 2 + 1))
                    last = pe.matmul(PS[:, 4, 0:S], mean_w[:, :], r[:, k, :], start=k == 0, stop=k == KT - 1)
                last.then_inc(sem("norm_mean"), 1)

            def norm_scale(name, t=KT):
                for j in range(2):
                    for k in range(t):
                        if j == 0 and k % 2 == 0:
                            pe.wait_ge(*norm(name, "sq", k // 2 + 1))
                        last = pe.matmul(PS[:, 5, j:j + 1], sq[:, k, j * P:(j + 1) * P], ones[:, 0:1],
                                         start=k == 0, stop=k == t - 1)
                last.then_inc(sem("norm_var"), 1)
                pe.wait_ge(*norm(name, "rcp", 1))
                for j in range(2):
                    last = pe.matmul(PS[:, 6, j * P:(j + 1) * P], rstd[:, j:j + 1].to_broadcast([P, P]), ident,
                                     start=True, stop=True)
                last.then_inc(sem("norm_rb"), 1)

            def ffn(name, base, operand):
                ready, hid_lo_ok = sem(f"{name}_fill"), sem(f"{name}_hid_lo")

                def fill(i, c):
                    b = 4 + 2 * (i % 2)
                    op = norm(operand, "lo", 0) if i == 0 else None
                    col(c, b, x_hi, x_lo, op)
                    col(c + 1, b + 1, x_hi, x_lo)

                fill(0, base)
                for i in range(1, NF):
                    fill(i, base + 2 + 3 * (i - 1))
                    pe.wait_ge(hid_lo_ok, i)
                    rows_acc(base + 4 + 3 * (i - 1), hid_hi[:, (i - 1) % 2, :, :], hid_lo[:, (i - 1) % 2, :, :],
                             i == 1, False)
                pe.wait_ge(hid_lo_ok, NF)
                rows_acc(base + 2 + 3 * (NF - 1), hid_hi[:, (NF - 1) % 2, :, :], hid_lo[:, (NF - 1) % 2, :, :],
                         False, True)

            pe.wait_ge(sem("const_landed"), 16)
            pe.wait_ge(sem("x_landed"), 32)
            xt = sq[:, :, :].rearrange("p (t q) s -> p t (q s)", t=2)
            for b in range(4):
                for k in (2 * b, 2 * b + 1):
                    for t in range(2):
                        o = (k % 2) * S + t * P
                        last = pe.transpose(PS[:, b, o:o + P], xt[:, t, k * P:(k + 1) * P], ident)
                last.then_inc(sem("x_turned"), 1)
            pe.wait_ge(sem("rows_landed"), 16 * 14)
            for i, n in enumerate((124, 74, 56)):
                last = pe.transpose(PS[:, 4, i * P:i * P + n], rows[i][0:n, :], ident[0:n, 0:n])
            last.then_inc(sem("vecs_turned"), 1)

            base = first["even"]
            pe.wait_ge(sem("vecs_ready"), 1)
            for p in range(13):
                if p >= 4:
                    if p == 4:
                        pe.wait_ge(sem("dt_raw"), 1)
                    else:
                        pe.wait_ge(sem("even_evac"), p - 4)
                col(base + p, 4 + p % 4, x_hi, x_lo, (sem("x_lo_ready"), 0) if p == 0 else None)

            pe.wait_ge(sem("da_ready"), 1)
            for j in range(2):
                for q in range(2):
                    o = 32 * j + 16 * q
                    last = pe.transpose(PS[:, 0, o:o + 16], small[0:16, q, j * P:(j + 1) * P], ident[0:16, 0:16])
            last.then_inc(sem("tok_turned"), 1)
            pe.wait_ge(sem("xbc_ready"), 6)
            for g in range(2):
                last = pe.transpose(PS[:, 1, g * P:(g + 1) * P], xbc[:, 8 + g, 0:P], ident)
            last.then_inc(sem("b_turned"), 1)
            for j in range(2):
                for g in range(2):
                    q = 2 * j + g
                    last = pe.matmul(PS[:, 2, q * P:(q + 1) * P], xbc[:, 8 + g, j * P:(j + 1) * P],
                                     xbc[:, 10 + g, j * P:(j + 1) * P], start=True, stop=True)
            last.then_inc(sem("cb_done"), 1)
            pe.wait_ge(sem("tok_ready"), 1)
            pe.wait_ge(sem("fixed"), 2)
            for j in range(2):
                pe.matmul(PS[:, 0, 64 + 16 * j:80 + 16 * j], triu, tok[:, j, 16:32], start=True, stop=True)
            pe.matmul(PS[:, 0, 96:112], ones[:, :], tok[:, 0, 16:32], start=True, stop=True).then_inc(sem("acs_done"), 1)

            for j in range(2):
                pe.wait_ge(sem("even_evac"), 12) if j == 0 else pe.wait_ge(sem("state_ready"), 2)
                for k in range(KT):
                    o = (k % 4) * P
                    last = pe.transpose(PS[:, 4 + k // 4, o:o + P], xbc[:, k, j * P:(j + 1) * P], ident)
                last.then_inc(sem("xtok_done"), 1)
                if j == 0:
                    pe.wait_ge(sem("acs_ready"), 2)
                    pe.wait_ge(sem("b_tok_ready"), 1)
                    pe.wait_ge(sem("cb_ready"), 1)
                else:
                    pe.wait_ge(sem("seg_done"), 4)
                for h in range(HEADS):
                    last = pe.matmul(PS[:, h // 4, (h % 4) * P:(h % 4) * P + P],
                                     tok[:, j, 16 + h:17 + h].to_broadcast([P, P]), triu, start=True, stop=True)
                    if h % 4 == 3:
                        last.then_inc(sem("acs_bcast"), 1)
                if j == 0:
                    pe.wait_ge(sem("xdec_ready"), 1)
                    for g in range(2):
                        pe.matmul(PS[:, 4 + g, :], b_tok[:, g * P:(g + 1) * P], x_dec[:, g * 512:(g + 1) * 512],
                                  start=True, stop=True).then_inc(sem("state_done"), 1)
                pe.wait_ge(sem("lmat_ready"), 2 * j + 2)
                if j:
                    pe.wait_ge(sem("y_ready"), 8)
                    pe.wait_ge(sem("cdec_ready"), 2)
                for k in range(KT):
                    o = (k % 4) * P
                    for e in range(2):
                        h = 2 * k + e
                        dst = PS[64 * e:64 * e + 64, 6 + k // 4, o:o + P]
                        last = pe.matmul(dst, x_dt[:, h * 64:h * 64 + 64], lmat[:, h, :], start=True, stop=j == 0)
                        if j:
                            last = pe.matmul(dst, state[:, h * 64:h * 64 + 64], e_acs[:, h, :], start=False, stop=True)
                    last.then_inc(sem("y_done"), 1)
            pe.wait_ge(sem("pool_diff"), 4)
            pe.wait_ge(sem("poolw_landed"), 16)
            pe.wait_ge(sem("seg_done"), 8)
            pe.wait_ge(sem("eacs_done"), 4)
            for g in range(4):
                last = pe.matmul(ACC[g], pool_w_sb[:, g, :], pool_y[:, g, :], start=True, stop=True)
            last.then_inc(sem("pool_done"), 1)
            norm_scale("ssm")
            base = first["even_out"]
            pe.wait_ge(sem("pool_lo_ready"), 1)
            for q in range(6):
                if q >= 2:
                    pe.wait_ge(*norm("ssm", "lo", q - 1))
                hi, lo = (pool_hi, pool_lo) if q < 2 else (x_hi, x_lo)
                kk = 2 * q if q < 2 else 2 * q - 4
                rows_acc(base + q, hi[:, kk:kk + 2, :], lo[:, kk:kk + 2, :], q == 0, q == 5)
            norm_mean("ln0")
            norm_scale("ln0")
            if not on("ffn0"):
                return
            ffn("ffn0", first["ffn0"], "ln0")
            norm_mean("ln1")
            norm_scale("ln1")
            pe.wait_ge(sem("ada_fma"), 3 * KT)
            for n in range(48):
                last = pe.matmul(PS[:, 7, n:n + 1], ada_acc[:, n // 16, (n % 16) * P:(n % 16) * P + P], ones[:, 0:1],
                                 start=True, stop=True)
            last.then_inc(sem("mod_done"), 1)
            if not on("odd"):
                return

            base = first["odd"]
            pe.wait_ge(sem("mod_ready"), 1)
            for p in range(5):
                if p >= 4:
                    pe.wait_ge(sem("odd_evac"), p - 3)
                col(base + p, 4 + p % 4, x_hi, x_lo, norm("ln1", "lo", 0) if p == 0 else None)
            for p in (5, 6):
                pe.wait_ge(sem("odd_evac"), p - 3)
                pe.wait_ge(lo_split, base + p + 1)
                wh, wl = slot(w_hi, base + p), slot(w_lo, base + p)
                for j in range(2):
                    dst = PS[:, 4 + p % 4, j * S:(j + 1) * S]
                    for k in range(KT):
                        xh, xl = x_hi[:, k, j * P:(j + 1) * P], x_lo[:, k, j * P:(j + 1) * P]
                        pe.matmul(dst, xh, wh[:, k, :], start=k == 0, stop=False)
                        pe.matmul(dst, xh, wl[:, k, :], start=False, stop=False)
                        last = pe.matmul(dst, xl, wh[:, k, :], start=False, stop=k == KT - 1)
                last.then_inc(chunk_used, 1)
            for p in (7, 8, 9):
                pe.wait_ge(sem("odd_evac"), p - 3)
                col(base + p, 4 + p % 4, x_hi, x_lo)
            p = 10
            pe.wait_ge(sem("odd_evac"), p - 3)
            col(base + p, 4 + p % 4, x_hi, x_lo)
            pe.wait_ge(sem("odd_evac"), 11)
            norm_scale("qn", 4)
            norm_scale("kvn", 2)
            for c in range(2):
                pe.wait_ge(lo_split, base + 12 + c)
                if c == 0:
                    pe.wait_ge(*norm("qn", "lo", 2))
                for h in range(4 * c, 4 * c + 4):
                    for k in range(4):
                        last = mm3(ACC[h][0:96], base + 11 + c, slice(96 * (h % 4), 96 * (h % 4) + 96), k, cq_hi[:, k, :],
                                   cq_lo[:, k, :], k == 0, k == 3)
                    if h < 4 * c + 3:
                        last.then_inc(sem("qm_done"), 1)
                last.then_inc(chunk_used, 1)
            pe.wait_ge(lo_split, base + 14)
            pe.wait_ge(*norm("kvn", "lo", 1))
            pe.wait_ge(*norm("kvn", "scaled", 1))
            kv_h, kv_l = (slot(t, base + 13).rearrange("p k (h e) -> p k h e", h=MLA_H) for t in (w_hi, w_lo))
            for h in range(MLA_H):
                dst = PS[0:96, 4 + h // 2, (h % 2) * S:(h % 2) * S + S]
                for k in range(2):
                    pe.matmul(dst, kv_h[:, k, h, 0:96], ckv_hi[:, k, :], start=k == 0, stop=False)
                    pe.matmul(dst, kv_h[:, k, h, 0:96], ckv_lo[:, k, :], start=False, stop=False)
                    last = pe.matmul(dst, kv_l[:, k, h, 0:96], ckv_hi[:, k, :], start=False, stop=k == 1)
                if h % 2:
                    last.then_inc(sem("km_done"), 1)
            pe.wait_ge(sem("qm_ready"), 4)
            for j in range(2):
                for k in range(2):
                    xh, xl = ckv_hi[:, k, j * P:(j + 1) * P], ckv_lo[:, k, j * P:(j + 1) * P]
                    pe.matmul(PS[:, j, :], xh, kv_h[:, k, :, 64:128], start=k == 0, stop=False)
                    pe.matmul(PS[:, j, :], xh, kv_l[:, k, :, 64:128], start=False, stop=False)
                    last = pe.matmul(PS[:, j, :], xl, kv_h[:, k, :, 64:128], start=False, stop=k == 1)
            last.then_inc(chunk_used, 1)
            pe.wait_ge(sem("odd_evac"), 11)
            swap = cst("swap", 96)
            pe.matmul(PS[0:96, 2, 0:S], swap, kr[:, 0, :], start=True, stop=True).then_inc(sem("kr_swapped"), 1)
            for h in range(MLA_H):
                if h % 2 == 0:
                    pe.wait_ge(sem("km_ready"), h // 2 + 1)
                last = pe.matmul(PS[0:96, 4 + h // 2, (h % 2) * S:(h % 2) * S + S], swap, qm[:, h, :], start=True, stop=True)
                if h % 2:
                    last.then_inc(sem("q_swapped"), 1)

            def scores(a):
                if a >= 2:
                    pe.wait_ge(sem("masked"), 2 * (a - 1))
                elif a == 0:
                    pe.wait_ge(sem("vm_ready"), 1)
                    pe.wait_ge(sem("kr_rot"), 1)
                    pe.wait_ge(sem("qm_rot"), 4)
                b = a % 2
                for j, kw, o in ((0, P, 0), (1, S, P)):
                    dst = PS[:, b, o:o + kw]
                    qs = slice(j * P, (j + 1) * P)
                    if a < FOX_H:
                        pe.matmul(dst, qz[:, a, qs], kf[:, a // 2, 0:kw], start=True, stop=False)
                        last = pe.matmul(dst, ident[:, a:a + 1].to_broadcast([P, P]), neg_f[:, 0:kw], start=False, stop=True)
                    else:
                        h = a - FOX_H
                        last = pe.matmul(dst, qm[:, h, qs], km[:, h, 0:kw], start=True, stop=True)
                last.then_inc(sem("scored"), 1)

            def turn(a):
                pe.wait_ge(sem("prob_ready"), 2 * a + 2)
                if a >= 2:
                    pe.wait_ge(sem("prob_t_ready"), a - 1)
                b = a % 2
                for o in (0, P, 2 * P):
                    last = pe.transpose(PS[:, 2 + b, o:o + P], prob[:, b, o:o + P], ident)
                last.then_inc(sem("prob_turned"), 1)

            def attend(a):
                pe.wait_ge(sem("prob_t_ready"), a + 1)
                pair, e = a // 2, a % 2
                if e == 0 and pair >= 2:
                    pe.wait_ge(sem("o_lo"), pair - 1)
                v, h = (v_tok, a) if a < FOX_H else (vm_tok, a - FOX_H)
                b, pt = 4 + pair % 2, prob_t[:, a % 2, :]
                pe.matmul(PS[64 * e:64 * e + 64, b, 0:S], v[:, 0, h * 64:h * 64 + 64], pt[:, 0:S], start=True, stop=False,
                          skip_group_check=True)
                pe.matmul(PS[64 * e:64 * e + 64, b, P:S], v[:, 1, h * 64:h * 64 + 64], pt[:, S:384], start=False, stop=True,
                          skip_group_check=True).then_inc(sem("attended"), 1)

            for a in range(18):
                if a < 16:
                    scores(a)
                if 1 <= a <= 16:
                    turn(a - 1)
                if a >= 2:
                    attend(a - 2)
            base = first["odd_out"]
            for q in range(4):
                pe.wait_ge(sem("o_lo"), 2 * q + 2)
                rows_acc(base + q, x_hi[:, 2 * q:2 * q + 2, :], x_lo[:, 2 * q:2 * q + 2, :], q == 0, q == 3)
            norm_mean("ln2")
            norm_scale("ln2")
            if not on("ffn1"):
                return
            ffn("ffn1", first["ffn1"], "ln2")
            norm_mean("ln3")
            norm_scale("ln3")
            if not on("sc"):
                return
            norm_scale("pre")
            base = first["sc"]
            c, f = base, 0
            for q in range(4):
                for part in range(3):
                    if f >= 4:
                        pe.wait_ge(sem(("sc_evac_c", "cv_ready", "sc_evac_b")[(f - 4) % 3]), (f - 4) // 3 + 1)
                    col(c, 4 + f % 4, x_hi, x_lo, norm("pre", "lo", 0) if c == base else None)
                    c, f = c + 1, f + 1
                if q:
                    pe.wait_ge(sem("sc_lo"), q)
                    rows_acc(c, hid_hi[:, (q - 1) % 2, :, :], hid_lo[:, (q - 1) % 2, :, :], q == 1, False)
                    c += 1
            pe.wait_ge(sem("sc_lo"), 4)
            rows_acc(c, hid_hi[:, 1, :, :], hid_lo[:, 1, :, :], False, True)
            norm_scale("post")
            norm_scale("preff")
            if not on("mlp"):
                return
            base = first["mlp"]
            col(base, 4, x_hi, x_lo, norm("preff", "lo", 0))
            for i in range(1, NM):
                col(base + 1 + 2 * (i - 1), 4 + i % 3, x_hi, x_lo)
                pe.wait_ge(sem("mlp_lo"), i)
                rows_acc(base + 2 + 2 * (i - 1), hid_hi[:, (i - 1) % 3, :, :], hid_lo[:, (i - 1) % 3, :, :], i == 1, False)
            pe.wait_ge(sem("mlp_lo"), NM)
            rows_acc(base + 1 + 2 * (NM - 1), hid_hi[:, (NM - 1) % 3, :, :], hid_lo[:, (NM - 1) % 3, :, :], False, True)
            norm_scale("postff")
            for k in range(KT):
                pe.wait_ge(sem("final_x"), k + 1)
                for t in range(2):
                    last = pe.transpose(PS[:, 2 * t + k // 4, (k % 4) * P:(k % 4) * P + P], x[:, k, t * P:(t + 1) * P], ident)
            last.then_inc(sem("out_turned"), 1)

        @block.scalar
        def _(act):
            done = [0]

            def split(upto):
                while done[0] <= min(upto, n_chunks - 1):
                    c = done[0]
                    act.wait_ge(raw_landed[c % RING], 16 * (c // RING + 1))
                    if c >= RING:
                        act.wait_ge(chunk_used, c - RING + 1)
                    act.activation(split_view(w_hi, c), split_view(raw, c), ACT.Copy).then_inc(hi_split, 1)
                    done[0] += 1

            def norm_stats(name, src, t=KT, eps=RMS_EPS, ready=None, width=D):
                for q in range(t // 2):
                    if ready:
                        act.wait_ge(ready[0], ready[1] + q + 1)
                    act.activation(sq[:, 2 * q:2 * q + 2, :], src[:, 2 * q:2 * q + 2, :], ACT.Square)\
                       .then_inc(sem("norm_sq"), 1)
                act.wait_ge(*norm(name, "var", 1))
                act.wait_ge(sem("eps_set"), 1)
                act.activation(std[:, :], PS[:, 5, 0:2], ACT.Sqrt, bias=eps_col(eps), scale=1.0 / width)\
                   .then_inc(sem("norm_std"), 1)

            def eps_col(eps):
                return eps_sb[:, 0:1] if eps == LN_EPS else eps_sb[:, 1:2]

            def operand_hi(name, src, dst, gains, biases, t=KT):
                for k in range(t):
                    if k % 2 == 0:
                        act.wait_ge(*norm(name, "scaled", k // 2 + 1))
                    act.activation(dst[:, k, :], src[:, k, :], ACT.Identity, scale=gains(k),
                                   bias=biases(k) if biases else 0.0).then_inc(sem("norm_hi"), 1)

            def ffn(name, base):
                for i in range(NF):
                    g = base if i == 0 else base + 2 + 3 * (i - 1)
                    split(g + 2)
                    act.wait_ge(chunk_used, g + 1)
                    if i >= 2:
                        act.wait_ge(sem(f"{name}_hid"), i - 1)
                    act.activation(gate_s[:, i % 2, :, :], bank2(4 + 2 * (i % 2)), ACT.Silu).then_inc(sem(f"{name}_silu"), 1)
                    split(g + 3)
                    act.wait_ge(sem(f"{name}_hid"), i + 1)
                    act.activation(hid_hi[:, i % 2, :, :], hid[:, i % 2, :, :], ACT.Copy).then_inc(sem(f"{name}_hid_hi"), 1)
                    if i < NF - 1:
                        split(g + 4 if i else g + 3)

            split(0)
            for b in range(4):
                act.wait_ge(sem("x_turned"), b + 1)
                act.activation(x_hi[:, 2 * b:2 * b + 2, :], bank2(b), ACT.Copy).then_inc(sem("x_hi_ready"), 1)
            split(2)
            act.wait_ge(sem("vecs_ready"), 1)
            act.wait_ge(sem("heads_landed"), 16 * 5)
            act.activation(head_vec[:, 2:3], head_vec[:, 1:2], ACT.Exp).then_inc(sem("a_ready"), 1)
            act.wait_ge(sem("dt_raw"), 1)
            act.activation(small[:, 2, :], small[:, 0, :], ACT.Abs).then_inc(sem("dt_act"), 1)
            act.wait_ge(sem("dt_act"), 1)
            act.activation(small[:, 2, :], small[:, 2, :], ACT.Exp, scale=-1.0).then_inc(sem("dt_act"), 1)
            act.wait_ge(sem("dt_act"), 2)
            act.activation(small[:, 2, :], small[:, 2, :], ACT.Ln, bias=1.0).then_inc(sem("dt_act"), 1)
            act.activation(silu_c[:, :], vecs[:, 2, 48:56], ACT.Silu).then_inc(sem("silu_c_ready"), 1)

            base = first["even"]
            for p in range(1, 13):
                split(base + p + 2)
                act.wait_ge(chunk_used, base + p + 1)
                b = 4 + p % 4
                if p <= 6:
                    if p == 1:
                        act.wait_ge(sem("conv_pad"), 1)
                    if p >= 3:
                        act.wait_ge(sem("conv_done"), p - 2)
                    act.activation(conv_in[:, p % 2, :, 3:3 + S], bank2(b), ACT.Copy).then_inc(sem("even_evac"), 1)
                    if p >= 2:
                        conv_silu(act, p - 1)
                elif p <= 8:
                    if p == 7:
                        act.wait_ge(sem("pad_zero"), 3)
                        conv_silu(act, 6)
                    act.activation(u_pad[:, 2 * (p - 7):2 * (p - 7) + 2, 16:16 + S], bank2(b), ACT.Copy)\
                       .then_inc(sem("even_evac"), 1)
                else:
                    act.activation(z_silu[:, 2 * (p - 9):2 * (p - 9) + 2, :], bank2(b), ACT.Silu).then_inc(sem("even_evac"), 1)
            split(first["even_out"] + 2)
            act.wait_ge(sem("b_turned"), 1)
            act.activation(b_tok[:, :], PS[:, 1, 0:S], ACT.Copy).then_inc(sem("b_tok_ready"), 1)
            act.wait_ge(sem("acs_ready"), 2)
            act.activation(decay[:, 1, :], decay[:, 0, :], ACT.Exp).then_inc(sem("decay_ready"), 1)
            for j in range(2):
                for q in range(4):
                    act.wait_ge(sem("seg_done"), 4 * j + q + 1)
                    for h in range(4 * q, 4 * q + 4):
                        if j and h == 0:
                            act.wait_ge(sem("y_done"), 8)
                        last = act.activation(lmat[:, h, :], seg[:, (h % 4) * P:(h % 4) * P + P], ACT.Exp,
                                              bias=neg_acs[:, j, h:h + 1])
                    last.then_inc(sem("exp_done"), 1)
                    if j:
                        if q == 0:
                            act.wait_ge(sem("pool_diff"), 4)
                        act.activation(e_acs[:, 4 * q:4 * q + 4, :], PS[:, q, :].rearrange("p (h s) -> p h s", h=4), ACT.Exp)\
                           .then_inc(sem("eacs_done"), 1)
                if j == 0:
                    for g in range(2):
                        act.wait_ge(sem("state_done"), g + 1)
                        act.activation(state[:, g * 512:(g + 1) * 512], PS[:, 4 + g, :], ACT.Copy)\
                           .then_inc(sem("state_ready"), 1)
            act.wait_ge(sem("pool_done"), 1)
            for g in range(4):
                act.activation(pool_y[:, g, :], ACC[g], ACT.Identity, scale=vec(1, g)).then_inc(sem("pool_scaled"), 1)
            act.wait_ge(sem("pool_scaled"), 4)
            act.activation(pool_hi[:, :, :], pool_y[:, :, :], ACT.Copy).then_inc(sem("pool_hi_ready"), 1)
            norm_stats("ssm", r, ready=(sem("gated"), 0))
            operand_hi("ssm", r, x_hi, lambda k: vec(1, 4 + k), None)
            base = first["even_out"]

            def layer_norm(name, need_hi=True):
                g, b = LNS[name]
                norm_stats(name, r, eps=LN_EPS, ready=norm(name, "cent", 0))
                if need_hi:
                    operand_hi(name, r, x_hi, lambda k: vec(0, g + k), lambda k: vec(0, b + k))

            split(first["ffn0"] + 2)
            layer_norm("ln0")
            if not on("ffn0"):
                return
            ffn("ffn0", first["ffn0"])
            split(first["odd"] + 2)
            layer_norm("ln1")
            if not on("odd"):
                return

            base = first["odd"]
            act.wait_ge(chunk_used, base + 1)
            act.activation(small[0:8, 0, :], PS[0:8, 4, 0:S], ACT.Identity, bias=head_vec[0:8, 3:4])\
               .then_inc(sem("odd_evac"), 1)
            act.wait_ge(sem("odd_evac"), 1)
            act.activation(small[0:8, 1, :], small[0:8, 0, :], ACT.Abs).then_inc(sem("fg_act"), 1)
            act.wait_ge(sem("fg_act"), 1)
            act.activation(small[0:8, 1, :], small[0:8, 1, :], ACT.Exp, scale=-1.0).then_inc(sem("fg_act"), 1)
            act.wait_ge(sem("fg_act"), 2)
            act.activation(small[0:8, 1, :], small[0:8, 1, :], ACT.Ln, bias=1.0).then_inc(sem("fg_act"), 1)
            act.wait_ge(sem("qz_zero"), 1)
            for p in range(1, 10):
                split(base + p + 2)
                act.wait_ge(chunk_used, base + p + 1)
                b = 4 + p % 4
                if p <= 2:
                    act.activation(kf[:, 2 * (p - 1):2 * (p - 1) + 2, :], bank2(b), ACT.Copy).then_inc(sem("odd_evac"), 1)
                elif p <= 4:
                    t = 2 * (p - 3)
                    for e in range(2):
                        rs = slice(64 * e, 64 * e + 64)
                        last = act.activation(qz[rs, 2 * t + e:2 * t + e + 3:2, :], bank2(b)[rs], ACT.Copy, scale=0.125)
                    last.then_inc(sem("odd_evac"), 1)
                elif p <= 6:
                    act.activation(v_tok[:, :, (p - 5) * S:(p - 4) * S], bank2(b), ACT.Copy).then_inc(sem("odd_evac"), 1)
                elif p <= 8:
                    act.activation(cq[:, 2 * (p - 7):2 * (p - 7) + 2, :], bank2(b), ACT.Copy).then_inc(sem("odd_evac"), 1)
                else:
                    act.activation(ckv[:, :, :], bank2(b), ACT.Copy).then_inc(sem("odd_evac"), 1)
            split(base + 12)
            act.wait_ge(chunk_used, base + 11)
            act.activation(kr[:, 0, :], PS[0:96, 4 + 10 % 4, 0:S], ACT.Copy).then_inc(sem("odd_evac"), 1)
            split(base + 13)
            act.wait_ge(sem("odd_evac"), 11)
            norm_stats("qn", cq, 4, width=512)
            operand_hi("qn", cq, cq_hi, lambda k: vec(1, 12 + k), None, 4)
            act.wait_ge(*norm("qn", "rb", 1))
            norm_stats("kvn", ckv, 2, width=256)
            operand_hi("kvn", ckv, ckv_hi, lambda k: vec(1, 16 + k), None, 2)
            for q in range(4):
                if q in (1, 3):
                    act.wait_ge(chunk_used, base + 12 + q // 2)
                else:
                    act.wait_ge(sem("qm_done"), 2 if q == 0 else 5)
                act.activation(qm[:, 2 * q:2 * q + 2, :], bank2(q)[0:96], ACT.Copy, scale=96 ** -0.5).then_inc(sem("qm_ready"), 1)
            for q in range(4):
                act.wait_ge(sem("km_done"), q + 1)
                act.activation(km[0:64, 2 * q:2 * q + 2, :], bank2(4 + q)[0:64], ACT.Copy).then_inc(sem("km_ready"), 1)
            split(base + 16)
            act.wait_ge(chunk_used, base + 14)
            act.activation(vm_tok[:, :, :], PS[:, 0:2, :], ACT.Copy).then_inc(sem("vm_ready"), 1)

            def exps(a):
                for j, kw, o in ((0, P, 0), (1, S, P)):
                    act.wait_ge(sem("neg_max"), a + 1)
                    if a >= 2 and j == 0:
                        act.wait_ge(sem("prob_turned"), a - 1)
                    act.activation(prob[:, a % 2, o:o + kw], sc_sb[:, a % 2, o:o + kw], ACT.Exp,
                                   bias=row_max[:, a % 2, j:j + 1], accum_out=row_sum[:, a % 2, j:j + 1])\
                       .then_inc(sem("exped"), 1)

            def o_hi(pair):
                act.wait_ge(sem("attended"), 2 * pair + 2)
                act.activation(x_hi[:, pair, :], PS[:, 4 + pair % 2, 0:S], ACT.Copy).then_inc(sem("o_hi"), 1)

            for a in range(18):
                if a < 16:
                    exps(a)
                if 1 <= a <= 16:
                    act.wait_ge(sem("prob_turned"), a)
                    if a >= 3:
                        act.wait_ge(sem("attended"), a - 2)
                    act.activation(prob_t[:, (a - 1) % 2, :], PS[:, 2 + (a - 1) % 2, 0:384], ACT.Copy)\
                       .then_inc(sem("prob_t_ready"), 1)
                if a >= 3 and a % 2:
                    o_hi((a - 3) // 2)
            base = first["odd_out"]
            split(base + 3)
            split(first["ffn1"] + 2)
            layer_norm("ln2")
            if not on("ffn1"):
                return
            ffn("ffn1", first["ffn1"])
            split(first["sc"] + 2)
            layer_norm("ln3", need_hi=False)
            if not on("sc"):
                return
            norm_stats("pre", x, ready=(sem("ln3_x"), 0))
            operand_hi("pre", r, x_hi, lambda k: gain[:, k:k + 1], lambda k: mod[:, k:k + 1])
            c, f = first["sc"], 0
            for q in range(4):
                for part in range(3):
                    split(c + 2)
                    act.wait_ge(chunk_used, c + 1)
                    b = 4 + f % 4
                    if part == 0:
                        if q >= 2:
                            act.wait_ge(sem("cv_ready"), q - 1)
                        act.activation(c_sb[:, q % 2, :, :], bank2(b), ACT.Copy).then_inc(sem("sc_evac_c"), 1)
                    elif part == 2:
                        if q >= 2:
                            act.wait_ge(sem("sc_y"), q - 1)
                        act.activation(b_sb[:, q % 2, :, :], bank2(b), ACT.Copy).then_inc(sem("sc_evac_b"), 1)
                    c, f = c + 1, f + 1
                if q:
                    split(c + 2)
                    c += 1
                act.wait_ge(sem("sc_y"), q + 1)
                act.activation(hid_hi[:, q % 2, :, :], hid[:, q % 2, :, :], ACT.Copy).then_inc(sem("sc_hi"), 1)
            split(first["mlp"] + 2)

            def take_acc(name):
                act.wait_ge(chunk_used, first["mlp"] if name == "post" else len(chunks))
                for q in range(4):
                    act.activation(r[:, 2 * q:2 * q + 2, :], bank2(q), ACT.Copy).then_inc(sem(f"{name}_taken"), 1)

            take_acc("post")
            norm_stats("post", r, ready=(sem("post_taken"), 0))
            norm_stats("preff", x, ready=(sem("post_x"), 0))
            operand_hi("preff", r, x_hi, lambda k: gain[:, 16 + k:17 + k], lambda k: mod[:, 24 + k:25 + k])
            if not on("mlp"):
                return
            base = first["mlp"]
            for i in range(NM):
                c = base if i == 0 else base + 1 + 2 * (i - 1)
                split(c + 2)
                act.wait_ge(chunk_used, c + 1)
                if i >= 2:
                    act.wait_ge(sem("mlp_hid"), i - 1)
                act.activation(gate_s[:, i % 2, :, :], bank2(4 + i % 3), ACT.Relu).then_inc(sem("mlp_relu"), 1)
                act.wait_ge(sem("mlp_hid"), i + 1)
                act.activation(hid_hi[:, i % 3, :, :], hid[:, i % 3, :, :], ACT.Copy).then_inc(sem("mlp_hi"), 1)
                split(c + 3)
            split(n_chunks)
            take_acc("postff")
            norm_stats("postff", r, ready=(sem("postff_taken"), 0))
            act.wait_ge(sem("out_turned"), 1)
            act.activation(sq[:, 0:4, :], PS[:, 0:2, :].rearrange("p b (a s) -> p (b a) s", a=2), ACT.Copy)\
               .then_inc(sem("out_rows"), 1)
            act.activation(sq[:, 4:8, :], PS[:, 2:4, :].rearrange("p b (a s) -> p (b a) s", a=2), ACT.Copy)\
               .then_inc(sem("out_rows"), 1)

        @block.vector
        def _(dve):
            done = [0]
            steps = [0]

            def split(upto):
                while done[0] <= min(upto, n_chunks - 1):
                    c = done[0]
                    dve.wait_ge(hi_split, c + 1)
                    dve.tensor_tensor(split_view(w_lo, c), split_view(raw, c), split_view(w_hi, c).bitcast(F32), ALU.subtract)\
                       .then_inc(lo_split, 1)
                    done[0] += 1

            def link(ins):
                steps[0] += 1
                ins.then_inc(sem("dve_link"), 1)
                dve.wait_ge(sem("dve_link"), steps[0])

            def resid(name, c_last):
                dve.wait_ge(chunk_used, c_last + 1)
                for q in range(4):
                    dve.scalar_tensor_tensor(out=r[:, 2 * q:2 * q + 2, :], in0=x[:, 2 * q:2 * q + 2, :], scalar=ALPHA,
                                             in1=bank2(q), op0=ALU.mult, op1=ALU.add).then_inc(sem("norm_resid"), 1)
                dve.wait_ge(*norm(name, "resid", 4))
                dve.wait_ge(*norm(name, "mean", 1))
                for q in range(4):
                    dve.tensor_tensor(r[:, 2 * q:2 * q + 2, :], r[:, 2 * q:2 * q + 2, :],
                                      PS[:, 4:5, 0:S].to_broadcast([P, 2, S]), ALU.subtract).then_inc(sem("norm_cent"), 1)

            def scaled(name, src, dst, t=KT):
                dve.wait_ge(*norm(name, "std", 1))
                dve.reciprocal(rstd[:, :], std[:, :]).then_inc(sem("norm_rcp"), 1)
                dve.wait_ge(*norm(name, "rb", 1))
                for q in range(t // 2):
                    dve.tensor_tensor(dst[:, 2 * q:2 * q + 2, :], src[:, 2 * q:2 * q + 2, :],
                                      PS[:, 6:7, 0:S].to_broadcast([P, 2, S]), ALU.mult).then_inc(sem("norm_scaled"), 1)
                dve.wait_ge(*norm(name, "scaled", t // 2))

            def operand_lo(name, src, full, hi, lo, gains, biases, t=KT):
                for q in range(t // 2):
                    for k in (2 * q, 2 * q + 1):
                        if biases:
                            ins = dve.tensor_scalar(full[:, k, :], src[:, k, :], gains(k), biases(k), ALU.mult, ALU.add)
                        else:
                            ins = dve.tensor_scalar(full[:, k, :], src[:, k, :], gains(k), None, ALU.mult)
                    ins.then_inc(sem("norm_full"), 1)
                    dve.wait_ge(*norm(name, "full", q + 1))
                    dve.wait_ge(*norm(name, "hi", 2 * q + 2))
                    dve.tensor_tensor(lo[:, 2 * q:2 * q + 2, :], full[:, 2 * q:2 * q + 2, :],
                                      hi[:, 2 * q:2 * q + 2, :].bitcast(F32), ALU.subtract).then_inc(sem("norm_lo"), 1)

            def layer_norm(name, c_last):
                g, b = LNS[name]
                resid(name, c_last)
                scaled(name, r, r)
                if name != "ln3":
                    operand_lo(name, r, x, x_hi, x_lo, lambda k: vec(0, g + k), lambda k: vec(0, b + k))
                else:
                    for k in range(KT):
                        ins = dve.tensor_scalar(x[:, k, :], r[:, k, :], vec(0, g + k), vec(0, b + k), ALU.mult, ALU.add)
                        if k % 2:
                            ins.then_inc(sem("ln3_x"), 1)

            def ffn(name, base):
                for i in range(NF):
                    g = base if i == 0 else base + 2 + 3 * (i - 1)
                    split(g + 2)
                    split(g + 3)
                    dve.wait_ge(sem(f"{name}_silu"), i + 1)
                    dve.wait_ge(chunk_used, g + 2)
                    dve.tensor_tensor(hid[:, i % 2, :, :], gate_s[:, i % 2, :, :], bank2(5 + 2 * (i % 2)), ALU.mult)\
                       .then_inc(sem(f"{name}_hid"), 1)
                    dve.wait_ge(sem(f"{name}_hid_hi"), i + 1)
                    dve.tensor_tensor(hid_lo[:, i % 2, :, :], hid[:, i % 2, :, :], hid_hi[:, i % 2, :, :].bitcast(F32),
                                      ALU.subtract).then_inc(sem(f"{name}_hid_lo"), 1)
                    if i < NF - 1:
                        split(g + 4 if i else g + 3)

            dve.memset(eps_sb[:, 0:1], LN_EPS)
            dve.memset(eps_sb[:, 1:2], RMS_EPS).then_inc(sem("eps_set"), 1)
            dve.memset(conv_in[:, :, :, 0:3], 0.0).then_inc(sem("conv_pad"), 1)
            for b in range(4):
                dve.wait_ge(sem("x_turned"), b + 1)
                dve.wait_ge(sem("x_hi_ready"), b + 1)
                link(dve.tensor_copy(x[:, 2 * b:2 * b + 2, :], bank2(b)))
                dve.tensor_tensor(x_lo[:, 2 * b:2 * b + 2, :], x[:, 2 * b:2 * b + 2, :],
                                  x_hi[:, 2 * b:2 * b + 2, :].bitcast(F32), ALU.subtract).then_inc(sem("x_lo_ready"), 1)
            dve.wait_ge(sem("vecs_turned"), 1)
            dve.tensor_copy(vecs[:, 0, 0:124], PS[:, 4, 0:124])
            dve.tensor_copy(vecs[:, 1, 0:74], PS[:, 4, P:P + 74])
            dve.tensor_copy(vecs[:, 2, 0:56], PS[:, 4, 2 * P:2 * P + 56]).then_inc(sem("vecs_ready"), 1)
            split(2)
            base = first["even"]
            dve.wait_ge(chunk_used, base + 1)
            dve.wait_ge(sem("heads_landed"), 16 * 5)
            dve.tensor_scalar(small[:, 0, :], PS[0:16, 4, 0:S], head_vec[:, 0:1], None, ALU.add).then_inc(sem("dt_raw"), 1)
            dve.wait_ge(sem("dt_act"), 3)
            dve.wait_ge(sem("a_ready"), 1)
            dve.wait_ge(sem("dt_raw"), 1)
            link(dve.scalar_tensor_tensor(out=small[:, 0, :], in0=small[:, 0, :], scalar=0.0, in1=small[:, 2, :],
                                          op0=ALU.max, op1=ALU.add))
            dve.tensor_scalar(small[:, 1, :], small[:, 0, :], head_vec[:, 2:3], -1.0, ALU.mult, ALU.mult)\
               .then_inc(sem("da_ready"), 1)
            dve.wait_ge(sem("vecs_ready"), 1)
            for p in range(1, 13):
                split(base + p + 2)
                if p <= 6:
                    t0 = 8 + 2 * (p - 1) if p <= 2 else 2 * (p - 3)
                    dve.wait_ge(sem("even_evac"), p)
                    if p >= 3:
                        dve.wait_ge(sem("xbc_ready"), p - 2)
                    for j in range(4):
                        for q in range(2):
                            w, src, dst = vec(0, 12 * j + t0 + q), conv_in[:, p % 2, q, j:j + S], conv_acc[:, p % 2, q, :]
                            if j == 0:
                                ins = dve.tensor_scalar(dst, src, w, vec(0, 48 + t0 + q), ALU.mult, ALU.add)
                            else:
                                ins = dve.scalar_tensor_tensor(out=dst, in0=src, scalar=w, in1=dst, op0=ALU.mult, op1=ALU.add)
                        if j < 3:
                            link(ins)
                        else:
                            ins.then_inc(sem("conv_done"), 1)
            dve.wait_ge(sem("tok_turned"), 1)
            dve.tensor_copy(tok[:, :, :], PS[:, 0, 0:64].rearrange("p (j c) -> p j c", j=2)).then_inc(sem("tok_ready"), 1)
            dve.wait_ge(sem("cb_done"), 1)
            dve.tensor_copy(cb[:, :, :], PS[:, 2, :].rearrange("p (q s) -> p q s", q=4)).then_inc(sem("cb_ready"), 1)
            dve.wait_ge(sem("acs_done"), 1)
            dve.tensor_scalar(neg_acs[:, :, :], PS[:, 0, 64:96].rearrange("p (j c) -> p j c", j=2), -1.0, None, ALU.mult)\
               .then_inc(sem("acs_ready"), 1)
            dve.wait_ge(sem("acs_ready"), 1)
            dve.tensor_tensor(decay[:, 0, :], neg_acs[:, 0, :], PS[:, 0, 96:112], ALU.add).then_inc(sem("acs_ready"), 1)
            dve.wait_ge(sem("tok_ready"), 1)

            def by_head(t, n=8):
                return t.rearrange("p (h o) -> p h o", o=1).to_broadcast([P, n, 64])

            for j in range(2):
                dve.wait_ge(sem("xtok_done"), j + 1)
                if j:
                    dve.wait_ge(sem("y_done"), 8)
                for g in range(2):
                    dve.tensor_tensor(x_dt[:, g * 512:(g + 1) * 512].rearrange("p (h e) -> p h e", h=8),
                                      PS[:, 4 + g, :].rearrange("p (h e) -> p h e", h=8),
                                      by_head(tok[:, j, 8 * g:8 * g + 8]), ALU.mult).then_inc(sem("xdt_ready"), 1)
                if j == 0:
                    dve.wait_ge(sem("decay_ready"), 1)
                    dve.wait_ge(sem("xdt_ready"), 2)
                    dve.tensor_tensor(x_dec.rearrange("p (h e) -> p h e", h=16), x_dt.rearrange("p (h e) -> p h e", h=16),
                                      by_head(decay[:, 1, :], 16), ALU.mult).then_inc(sem("xdec_ready"), 1)
                for q in range(4):
                    dve.wait_ge(sem("acs_bcast"), 4 * j + q + 1)
                    if 4 * j + q:
                        dve.wait_ge(sem("exp_done"), 4 * j + q)
                    dve.tensor_tensor(seg.rearrange("p (h s) -> p h s", h=4), PS[:, q, :].rearrange("p (h s) -> p h s", h=4),
                                      cst("ssm_mask").rearrange("p (o s) -> p o s", o=1).to_broadcast([P, 4, P]), ALU.add)\
                       .then_inc(sem("seg_done"), 1)
                for g in range(2):
                    dve.wait_ge(sem("exp_done"), 4 * j + 2 * g + 2)
                    if g == 0:
                        dve.wait_ge(sem("cb_ready"), 1)
                    dve.tensor_tensor(lmat[:, 8 * g:8 * g + 8, :], lmat[:, 8 * g:8 * g + 8, :],
                                      cb[:, 2 * j + g:2 * j + g + 1, :].to_broadcast([P, 8, P]), ALU.mult)\
                       .then_inc(sem("lmat_ready"), 1)
                if j:
                    for g in range(2):
                        dve.wait_ge(sem("eacs_done"), 2 * g + 2)
                        dve.tensor_tensor(e_acs[:, 8 * g:8 * g + 8, :], e_acs[:, 8 * g:8 * g + 8, :],
                                          xbc[:, 10 + g:11 + g, P:S].to_broadcast([P, 8, P]), ALU.mult)\
                           .then_inc(sem("cdec_ready"), 1)
                for k in range(KT):
                    dve.wait_ge(sem("y_done"), 8 * j + 4 * (k // 4) + 4)
                    dve.scalar_tensor_tensor(out=r[:, k, j * P:(j + 1) * P], in0=xbc[:, k, j * P:(j + 1) * P],
                                             scalar=d_skip[:, k:k + 1], in1=PS[:, 6 + k // 4, (k % 4) * P:(k % 4) * P + P],
                                             op0=ALU.mult, op1=ALU.add).then_inc(sem("y_ready"), 1)
            dve.wait_ge(sem("y_ready"), 16)
            dve.wait_ge(sem("even_evac"), 12)
            for q in range(4):
                dve.tensor_tensor(r[:, 2 * q:2 * q + 2, :], r[:, 2 * q:2 * q + 2, :], z_silu[:, 2 * q:2 * q + 2, :], ALU.mult)\
                   .then_inc(sem("gated"), 1)
            dve.wait_ge(sem("pool_hi_ready"), 1)
            dve.tensor_tensor(pool_lo[:, :, :], pool_y[:, :, :], pool_hi[:, :, :].bitcast(F32), ALU.subtract)\
               .then_inc(sem("pool_lo_ready"), 1)
            split(first["even_out"] + 2)
            dve.wait_ge(sem("gated"), 4)
            scaled("ssm", r, r)
            operand_lo("ssm", r, sq, x_hi, x_lo, lambda k: vec(1, 4 + k), None)
            split(first["ffn0"] + 2)
            layer_norm("ln0", first["ffn0"] - 1)
            if not on("ffn0"):
                return
            ffn("ffn0", first["ffn0"])
            split(first["odd"] + 2)
            layer_norm("ln1", first["odd"] - 1)
            dve.wait_ge(sem("mod_done"), 1)
            link(dve.tensor_tensor(mod[:, :], PS[:, 7, 0:48], vecs[:, 2, 0:48], ALU.add))
            dve.scalar_tensor_tensor(out=gain[:, 0:8], in0=mod[:, 8:16], scalar=1.0, in1=vecs[:, 1, 18:26], op0=ALU.add, op1=ALU.mult)
            dve.tensor_tensor(gain[:, 8:16], mod[:, 16:24], vecs[:, 1, 26:34], ALU.mult)
            dve.scalar_tensor_tensor(out=gain[:, 16:24], in0=mod[:, 32:40], scalar=1.0, in1=vecs[:, 1, 34:42], op0=ALU.add, op1=ALU.mult)
            dve.tensor_tensor(gain[:, 24:32], mod[:, 40:48], vecs[:, 1, 42:50], ALU.mult).then_inc(sem("mod_ready"), 1)
            if not on("odd"):
                return
            base = first["odd"]
            dve.memset(neg_f[:, :], 0.0)
            dve.memset(qz[:, :, :], 0.0).then_inc(sem("qz_zero"), 1)
            dve.wait_ge(sem("fg_act"), 3)
            dve.wait_ge(sem("qz_zero"), 1)
            link(dve.tensor_scalar(small[0:8, 2, :], small[0:8, 0, :], -1.0, 0.0, ALU.mult, ALU.max))
            link(dve.tensor_tensor(small[0:8, 3, :], small[0:8, 2, :], small[0:8, 1, :], ALU.add))
            dve.tensor_tensor_scan(neg_f[0:8, :], small[0:8, 3, :], small[0:8, 3, :], 0.0, ALU.add, ALU.bypass)\
               .then_inc(sem("neg_f_ready"), 1)
            split(base + 13)
            scaled("qn", cq, cq, 4)
            operand_lo("qn", cq, r, cq_hi, cq_lo, lambda k: vec(1, 12 + k), None, 4)
            scaled("kvn", ckv, ckv, 2)
            dve.wait_ge(*norm("qn", "lo", 2))
            operand_lo("kvn", ckv, r, ckv_hi, ckv_lo, lambda k: vec(1, 16 + k), None, 2)
            cos, sin = cst("cos", 96), cst("sin", 96)
            RR = slice(ROPE_ROW, 96)
            dve.wait_ge(sem("kr_swapped"), 1)
            link(dve.tensor_tensor(kr[RR, 1, :], PS[RR, 2, 0:S], sin[RR, :], ALU.mult))
            link(dve.tensor_tensor(kr[RR, 0, :], kr[RR, 0, :], cos[RR, :], ALU.mult))
            link(dve.tensor_tensor(kr[RR, 0, :], kr[RR, 0, :], kr[RR, 1, :], ALU.add))
            dve.tensor_copy(km[RR, :, :], kr[RR, 0:1, :].to_broadcast([32, MLA_H, S])).then_inc(sem("kr_rot"), 1)
            for q in range(4):
                dve.wait_ge(sem("q_swapped"), q + 1)
                two = slice(2 * q, 2 * q + 2)
                if q:
                    dve.wait_ge(sem("qm_rot"), q)
                dve.tensor_tensor(hid[RR, 0, :, :], bank2(4 + q)[RR], sin[RR, :].rearrange("p (o s) -> p o s", o=1)
                                  .to_broadcast([32, 2, S]), ALU.mult)
                link(dve.tensor_tensor(qm[RR, two, :], qm[RR, two, :], cos[RR, :].rearrange("p (o s) -> p o s", o=1)
                                       .to_broadcast([32, 2, S]), ALU.mult))
                dve.tensor_tensor(qm[RR, two, :], qm[RR, two, :], hid[RR, 0, :, :], ALU.add).then_inc(sem("qm_rot"), 1)
            split(base + 16)

            def masked(a):
                dve.wait_ge(sem("scored"), a + 1)
                b = a % 2
                if a >= 2:
                    dve.wait_ge(sem("exped"), 2 * a - 2)
                for j, kw, o in ((0, P, 0), (1, S, P)):
                    dve.tensor_tensor_reduce(out=sc_sb[:, b, o:o + kw], in0=PS[:, b, o:o + kw], in1=cst("attn_mask")[:, o:o + kw],
                                             scale=1.0, scalar=-3e38, op0=ALU.add, op1=ALU.max,
                                             accum_out=row_max[:, b, j:j + 1]).then_inc(sem("masked"), 1)
                dve.wait_ge(sem("masked"), 2 * a + 2)
                dve.tensor_scalar(row_max[:, b, :], row_max[:, b, :], -1.0, None, ALU.mult).then_inc(sem("neg_max"), 1)

            def normalised(a):
                b = a % 2
                dve.wait_ge(sem("exped"), 2 * a + 2)
                link(dve.reciprocal(row_sum[:, b, :], row_sum[:, b, :]))
                for j, kw, o in ((0, P, 0), (1, S, P)):
                    dve.tensor_scalar(prob[:, b, o:o + kw], prob[:, b, o:o + kw], row_sum[:, b, j:j + 1], None, ALU.mult)\
                       .then_inc(sem("prob_ready"), 1)

            def o_low(pair):
                dve.wait_ge(sem("o_hi"), pair + 1)
                dve.tensor_tensor(x_lo[:, pair, :], PS[:, 4 + pair % 2, 0:S], x_hi[:, pair, :].bitcast(F32), ALU.subtract)\
                   .then_inc(sem("o_lo"), 1)

            for a in range(18):
                if a < 16:
                    masked(a)
                    normalised(a)
                if a >= 3 and a % 2:
                    o_low((a - 3) // 2)
            split(first["odd_out"] + 3)
            split(first["ffn1"] + 2)
            layer_norm("ln2", first["ffn1"] - 1)
            if not on("ffn1"):
                return
            ffn("ffn1", first["ffn1"])
            split(first["sc"] + 2)
            layer_norm("ln3", first["sc"] - 1)
            if not on("sc"):
                return
            dve.wait_ge(sem("ln3_x"), 4)
            scaled("pre", x, r)
            operand_lo("pre", r, sq, x_hi, x_lo, lambda k: gain[:, k:k + 1], lambda k: mod[:, k:k + 1])
            dve.memset(cv[:, :, :, 0:1], 0.0)
            link(dve.memset(cv[:, :, :, 1 + S:2 + S], 0.0))
            c, f = first["sc"], 0
            for q in range(4):
                i = q % 2
                split(c + 3)
                dve.wait_ge(sem("sc_evac_c"), q + 1)
                dve.wait_ge(chunk_used, c + 2)
                dve.tensor_tensor(cv[:, i, :, 1:1 + S], c_sb[:, i, :, :], bank2(4 + (f + 1) % 4), ALU.mult)\
                   .then_inc(sem("cv_ready"), 1)
                dve.wait_ge(sem("cv_ready"), q + 1)
                split(c + 4)
                for j in range(3):
                    for e in range(2):
                        w, src, dst = vec(1, 50 + 8 * j + 2 * q + e), cv[:, i, e, j:j + S], cv_acc[:, i, e, :]
                        if j == 0:
                            ins = dve.tensor_scalar(dst, src, w, None, ALU.mult)
                        else:
                            ins = dve.scalar_tensor_tensor(out=dst, in0=src, scalar=w, in1=dst, op0=ALU.mult, op1=ALU.add)
                    link(ins)
                dve.wait_ge(sem("sc_evac_b"), q + 1)
                dve.tensor_tensor(hid[:, i, :, :], cv_acc[:, i, :, :], b_sb[:, i, :, :], ALU.mult).then_inc(sem("sc_y"), 1)
                dve.wait_ge(sem("sc_hi"), q + 1)
                dve.tensor_tensor(hid_lo[:, i, :, :], hid[:, i, :, :], hid_hi[:, i, :, :].bitcast(F32), ALU.subtract)\
                   .then_inc(sem("sc_lo"), 1)
                c, f = c + (4 if q else 3), f + 3
                split(c + 1)
            split(first["mlp"] + 2)

            def add_post(name, g0):
                for k in range(KT):
                    ins = dve.scalar_tensor_tensor(out=x[:, k, :], in0=r[:, k, :], scalar=gain[:, g0 + k:g0 + k + 1],
                                                   in1=x[:, k, :], op0=ALU.mult, op1=ALU.add)
                    if name == "final_x" or k % 2:
                        ins.then_inc(sem(name), 1)

            scaled("post", r, r)
            add_post("post_x", 8)
            dve.wait_ge(sem("post_x"), 4)
            scaled("preff", x, r)
            operand_lo("preff", r, sq, x_hi, x_lo, lambda k: gain[:, 16 + k:17 + k], lambda k: mod[:, 24 + k:25 + k])
            if not on("mlp"):
                return
            base = first["mlp"]
            for i in range(NM):
                c = base if i == 0 else base + 1 + 2 * (i - 1)
                split(c + 2)
                dve.wait_ge(sem("mlp_relu"), i + 1)
                dve.tensor_tensor(hid[:, i % 3, :, :], gate_s[:, i % 2, :, :], gate_s[:, i % 2, :, :], ALU.mult)\
                   .then_inc(sem("mlp_hid"), 1)
                dve.wait_ge(sem("mlp_hi"), i + 1)
                dve.tensor_tensor(hid_lo[:, i % 3, :, :], hid[:, i % 3, :, :], hid_hi[:, i % 3, :, :].bitcast(F32),
                                  ALU.subtract).then_inc(sem("mlp_lo"), 1)
                split(c + 3)
            split(n_chunks)
            scaled("postff", r, r)
            add_post("final_x", 24)


_INS = ["x", "even_w_in", "pool_w", "pool_scale", "conv_w", "conv_b", "dt_bias", "a_log", "d_skip", "ssm_norm_w",
        "even_w_out", "odd_w_in", "fgate_b", "q_norm_w", "w_uq", "kv_norm_w", "w_ukv", "odd_w_out", "ffn_w_gate",
        "ffn_w_up", "ffn_w_down", "ln_mix_g", "ln_mix_b", "ln_ffn_g", "ln_ffn_b", "c_2", "ada_w_2", "ada_b_2",
        "norm_gains_2", "mlp_w_in_2", "mlp_w_out_2", "sc_w_in_2", "sc_conv_2", "sc_w_out_2"]


def kernel(**inputs):
    import concourse.bacc as bacc
    from concourse.bass_utils import run_bass_kernel_spmd

    nc = bacc.Bacc("TRN2", target_bir_lowering=False, num_devices=1)
    arrays = {name: np.ascontiguousarray(inputs[name]) for name in _INS}
    arrays["consts"] = shape_constants()
    aps = {n: nc.dram_tensor(n, a.shape, mybir.dt.from_np(a.dtype), kind="ExternalInput").ap() for n, a in arrays.items()}
    out = nc.dram_tensor("out", (1, S, D), F32, kind="ExternalOutput").ap()
    build(nc, aps, out)
    result = run_bass_kernel_spmd(nc, [arrays], core_ids=[0])
    return result.results[0]["out"]
```

```python
from contextlib import ExitStack

import numpy as np
import concourse.bass as bass
from concourse import mybir

F32 = mybir.dt.float32
F32R = mybir.dt.float32r
ALU = mybir.AluOpType
ACT = mybir.ActivationFunctionType
AX = mybir.AxisListType

P = 128
S = 256
D = 1024
KT = D // P
CH = 2048
RING = 3
HEADS = 16
FOX_H = 8
MLA_H = 8
D_FF = 2816
D_FF2 = 4096
ALPHA = (2 * 2) ** 0.25
LN_EPS = 1e-5
RMS_EPS = 1e-6
NEG = -1e30

CONST_COLS = {}
_at = 0
for _n, _w in (("ident", 128), ("triu", 128), ("attn_mask", 384), ("ssm_mask", 128), ("cos", 256), ("sin", 256),
               ("swap", 96), ("inv_count", 64)):
    CONST_COLS[_n] = (_at, _w)
    _at += _w
CONST_W = _at
ROPE_ROW = 64


def shape_constants():
    c = np.zeros((P, CONST_W), np.float32)

    def put(name, a):
        o, w = CONST_COLS[name]
        c[:a.shape[0], o:o + w] = a

    i, j = np.arange(P)[:, None], np.arange(P)[None, :]
    put("ident", (i == j).astype(np.float32))
    put("triu", (i <= j).astype(np.float32))
    causal = np.where(j <= i, 0, NEG).astype(np.float32)
    put("attn_mask", np.concatenate([causal, np.zeros((P, P), np.float32), causal], 1))
    put("ssm_mask", np.where(i <= j, 0, NEG).astype(np.float32))
    half = 16
    freqs = np.power(np.float32(10000.0), -np.arange(half, dtype=np.float32) / np.float32(half)).astype(np.float32)
    ang = (freqs[:, None] * np.arange(S, dtype=np.float32)[None, :]).astype(np.float32)
    cos, sin = np.ones((96, S), np.float32), np.zeros((96, S), np.float32)
    cos[64:80] = cos[80:96] = np.cos(ang)
    sin[64:80], sin[80:96] = -np.sin(ang), np.sin(ang)
    put("cos", cos)
    put("sin", sin)
    swap = np.zeros((96, 96), np.float32)
    for r in range(half):
        swap[ROPE_ROW + half + r, ROPE_ROW + r] = swap[ROPE_ROW + r, ROPE_ROW + half + r] = 1
    put("swap", swap)
    t = np.arange(16)
    put("inv_count", np.tile(np.concatenate([1 / np.minimum(t + 1, w) for w in (2, 4, 8, 16)])[None], (P, 1)).astype(np.float32))
    return c


def build(nc, A, out, stop=None):
    ctx = ExitStack()
    with ctx:
        def sb(name, shape, dt=F32, stack=ctx):
            return stack.enter_context(nc.sbuf_tensor(name, shape, dt))

        sems = {}

        def sem(name):
            if name not in sems:
                sems[name] = ctx.enter_context(nc.semaphore(name))
            return sems[name]

        raw = sb("raw", [P, RING, CH])
        w_hi = sb("w_hi", [P, RING, CH], F32R)
        w_lo = sb("w_lo", [P, RING, CH], F32R)
        x = sb("x_res", [P, KT, S])
        x_hi = sb("x_hi", [P, KT, S], F32R)
        x_lo = sb("x_lo", [P, KT, S], F32R)
        r = sb("r", [P, KT, S])
        sq = sb("sq", [P, KT, S])
        const = sb("const", [P, CONST_W])
        vecs = sb("vecs", [P, 3, P])
        ones = sb("ones", [P, P])
        d_skip = sb("d_skip_sb", [P, KT])
        head_vec = sb("head_vec", [16, 4])
        std = sb("std", [P, 2])
        eps_sb = sb("eps_sb", [P, 2])
        table_sb = sb("table_sb", [P, 22])
        rstd = sb("rstd", [P, 4])
        moments = sb("moments", [P, 6])
        mod = sb("mod", [P, 48])
        gain = sb("gain", [P, 32])
        silu_c = sb("silu_c", [P, KT])
        small = sb("small", [16, 4, S])
        hid = sb("hid", [P, 3, 2, S])
        gate_s = sb("gate_s", [P, 2, 2, S])
        hid_hi = sb("hid_hi", [P, 3, 2, S], F32R)
        hid_lo = sb("hid_lo", [P, 3, 2, S], F32R)

        with ExitStack() as even:
            pool_hi = sb("pool_hi", [P, 4, S], F32R, even)
            pool_lo = sb("pool_lo", [P, 4, S], F32R, even)
            pool_y = sb("pool_y", [P, 4, S], F32, even)
            u_pad = sb("u_pad", [P, 4, 16 + S], F32, even)
            wins = sb("wins", [P, 2, 4, 16 + S], F32, even)
            z_silu = sb("z_silu", [P, KT, S], F32, even)
            conv_in = sb("conv_in", [P, 2, 2, 3 + S], F32, even)
            conv_acc = sb("conv_acc", [P, 2, 2, S], F32, even)
            xbc = sb("xbc", [P, 12, S], F32, even)
            tok = sb("tok", [P, 2, 32], F32, even)
            neg_acs = sb("neg_acs", [P, 2, 16], F32, even)
            decay = sb("decay", [P, 2, 16], F32, even)
            b_tok = sb("b_tok", [P, 2 * P], F32, even)
            cb = sb("cb", [P, 4, P], F32, even)
            state = sb("state", [P, D], F32, even)
        win_a, win_b = wins[:, 0, :, :], wins[:, 1, :, :]
        e_acs = wins[:, :, :, :].rearrange("p a g s -> p (a g s)")[:, 0:HEADS * P].rearrange("p (h s) -> p h s", h=HEADS)
        x_dt = hid[:, 0:2, :, :].rearrange("p a b s -> p (a b s)")
        x_dec = gate_s[:, :, :, :].rearrange("p a b s -> p (a b s)")
        seg = hid[:, 2, :, :].rearrange("p b s -> p (b s)")
        lmat = sq[:, :, :].rearrange("p k (a s) -> p (k a) s", a=2)
        rows = [sb(f"vec_rows{i}", [P, P]) for i in range(3)]
        pool_w_sb = sb("pool_w_sb", [P, 4, P])

        with ExitStack() as odd:
            qz = sb("qz", [P, FOX_H, S], F32, odd)
            kf = sb("kf", [P, 4, S], F32, odd)
            v_tok = sb("v_tok", [P, 2, 512], F32, odd)
            neg_f = sb("neg_f", [P, S], F32, odd)
            cq = sb("cq", [P, 4, S], F32, odd)
            cq_hi = sb("cq_hi", [P, 4, S], F32R, odd)
            cq_lo = sb("cq_lo", [P, 4, S], F32R, odd)
            ckv = sb("ckv", [P, 2, S], F32, odd)
            ckv_hi = sb("ckv_hi", [P, 2, S], F32R, odd)
            ckv_lo = sb("ckv_lo", [P, 2, S], F32R, odd)
            qm = sb("qm", [96, MLA_H, S], F32, odd)
            km = sb("km", [96, MLA_H, S], F32, odd)
            kr = sb("kr", [96, 2, S], F32, odd)
            vm_tok = sb("vm_tok", [P, 2, 512], F32, odd)
            row_max = sb("row_max", [P, 2, 2], F32, odd)
            row_sum = sb("row_sum", [P, 2, 2], F32, odd)

        hid_flat = hid[:, :, :, :].rearrange("p a b s -> p (a b s)")
        prob = hid_flat[:, 0:768].rearrange("p (a n) -> p a n", a=2)
        prob_t = hid_flat[:, 768:1536].rearrange("p (a n) -> p a n", a=2)
        sc_sb = x_dec[:, 0:768].rearrange("p (a n) -> p a n", a=2)

        with ExitStack() as conv2:
            ada_raw = sb("ada_raw", [P, 2, CH], F32, conv2)
            ada_acc = sb("ada_acc", [P, 3, CH], F32, conv2)
            c_sb = sb("c_sb", [P, 2, 2, S], F32, conv2)
            b_sb = sb("b_sb", [P, 2, 2, S], F32, conv2)
            cv = sb("cv", [P, 2, 2, 1 + S + 1], F32, conv2)
            cv_acc = sb("cv_acc", [P, 2, 2, S], F32, conv2)

        def cst(name, rows_=P):
            o, w = CONST_COLS[name]
            return const[0:rows_, o:o + w]

        ident, triu = cst("ident"), cst("triu")

        def vec(t, c):
            return vecs[:, t, c:c + 1]

        PS = ctx.enter_context(nc.psum_tensor("PS", [P, 8, 512], F32))
        ACC = [PS[:, n // 2, (n % 2) * S:(n % 2) * S + S] for n in range(8)]

        def bank2(b):
            return PS[:, b, :].rearrange("p (a s) -> p a s", a=2)

        chunks = []
        first = {}

        def col_chunk(w, k, c0, n, copies=1):
            chunks.append((w[0:k * P, c0:c0 + n].rearrange("(k p) n -> p k n", p=P), k, n, copies))

        def row_chunk(w, r0):
            chunks.append((w[r0:r0 + 2 * P, :].rearrange("(k p) n -> p k n", p=P), 2, D, 1))

        E_IN, O_IN = A["even_w_in"][0], A["odd_w_in"][0]
        XBC0, DT0 = 512 + 1024, 512 + 1024 + 1536
        first["even"] = len(chunks)
        col_chunk(E_IN, 8, DT0, 16, 8)
        for c in (XBC0 + 1024, XBC0 + 1280, XBC0, XBC0 + 256, XBC0 + 512, XBC0 + 768, 0, 256, 512, 768, 1024, 1280):
            col_chunk(E_IN, 8, c, 256)
        first["even_out"] = len(chunks)
        for q in range(6):
            row_chunk(A["even_w_out"][0], 2 * P * q)

        def ffn_chunks(name, gate, up, down, n):
            first[name] = len(chunks)
            col_chunk(gate, 8, 0, 256)
            col_chunk(up, 8, 0, 256)
            for i in range(1, n):
                col_chunk(gate, 8, 256 * i, 256)
                col_chunk(up, 8, 256 * i, 256)
                row_chunk(down, 256 * (i - 1))
            row_chunk(down, 256 * (n - 1))

        NF = D_FF // 256
        ffn_chunks("ffn0", A["ffn_w_gate"][0], A["ffn_w_up"][0], A["ffn_w_down"][0], NF)
        first["odd"] = len(chunks)
        col_chunk(O_IN, 8, 1536, 8, 16)
        for c in (512, 768, 0, 256, 1024, 1280, 1544, 1800, 2056):
            col_chunk(O_IN, 8, c, 256)
        col_chunk(O_IN, 8, 2312, 32, 3)
        chunks.append((A["w_uq"][0][:, 0:384].rearrange("(k p) n -> p k n", p=P), 4, 384, 1))
        chunks.append((A["w_uq"][0][:, 384:768].rearrange("(k p) n -> p k n", p=P), 4, 384, 1))
        chunks.append((A["w_ukv"][0].rearrange("(k p) n -> p k n", p=P), 2, 1024, 1))
        first["odd_out"] = len(chunks)
        for q in range(4):
            row_chunk(A["odd_w_out"][0], 2 * P * q)
        ffn_chunks("ffn1", A["ffn_w_gate"][1], A["ffn_w_up"][1], A["ffn_w_down"][1], NF)
        first["sc"] = len(chunks)
        SC_IN = A["sc_w_in_2"][0]
        for q in range(4):
            for part in (1, 2, 0):
                col_chunk(SC_IN, 8, part * D + 256 * q, 256)
            if q:
                row_chunk(A["sc_w_out_2"][0], 256 * (q - 1))
        row_chunk(A["sc_w_out_2"][0], 768)
        first["mlp"] = len(chunks)
        NM = D_FF2 // 256
        col_chunk(A["mlp_w_in_2"][0], 8, 0, 256)
        for i in range(1, NM):
            col_chunk(A["mlp_w_in_2"][0], 8, 256 * i, 256)
            row_chunk(A["mlp_w_out_2"][0], 256 * (i - 1))
        row_chunk(A["mlp_w_out_2"][0], 256 * (NM - 1))
        first["end"] = len(chunks)

        order = ["even", "ffn0", "odd", "ffn1", "sc", "mlp", "end"]
        n_chunks = first[order[order.index(stop) + 1]] if stop else len(chunks)
        last_stage = order.index(stop) if stop else len(order) - 1

        def on(stage):
            return order.index(stage) <= last_stage

        def slot(t, c):
            _, k, n, copies = chunks[c]
            n *= 1 if t is raw else copies
            return t[:, c % RING, 0:k * n].rearrange("p (k n) -> p k n", k=k)

        def split_view(t, c):
            _, k, n, copies = chunks[c]
            if copies == 1:
                return slot(t, c)
            if t is raw:
                return slot(t, c).rearrange("p k (o n) -> p k o n", o=1).to_broadcast([P, k, copies, n])
            return slot(t, c).rearrange("p k (o n) -> p k o n", o=copies)

        raw_landed = [sem(f"raw_landed{i}") for i in range(RING)]
        hi_split, lo_split, chunk_used = sem("hi_split"), sem("lo_split"), sem("chunk_used")

        NORM_TILES = {"ssm": 8, "ln0": 8, "ln1": 8, "qn": 4, "kvn": 2, "ln2": 8, "ln3": 8, "pre": 8, "post": 8,
                      "preff": 8, "postff": 8}

        def norm_incs(name, kind):
            pairs = NORM_TILES[name] // 2
            if kind in ("resid", "scaled_r"):
                return 4 if name in LNS else 0
            if kind == "folded":
                return 0 if name in ("qn", "kvn") else 5 if name in LNS else 3
            if kind == "small":
                return 4 if name in LNS else 0
            if kind in ("hi", "full", "lo"):
                return 0 if name in ("ln3", "post", "postff") else 2 * pairs if kind == "hi" else pairs
            return pairs if kind in ("sq", "scaled") else 1

        def norm(name, kind, n):
            before = 0
            for other in NORM_TILES:
                if other == name:
                    return sem(f"norm_{kind}"), before + n
                before += norm_incs(other, kind)

        LNS = {"ln0": (60, 76), "ln1": (92, 108), "ln2": (68, 84), "ln3": (100, 116)}

        EVEN_STEPS = [("proj", p) for p in range(2, 7)] + [
            ("small", 0), ("proj", 7), ("head", 0), ("proj", 8), ("bcast", 0), ("proj", 9), ("state", 0), ("proj", 10),
            ("y", 0), ("proj", 11), ("head", 1), ("bcast", 1), ("pool", 0), ("proj", 12), ("pool", 1), ("y", 1)]
        ODD_STEPS = [("proj", p) for p in range(2, 7)] + [
            ("proj", 7), ("att", 0), ("proj", 8), ("att", 1), ("proj", 9), ("att", 2), ("proj", 10), ("att", 3),
            ("qn_sum", 0), ("att", 4), ("qn_out", 0), ("att", 5), ("kvn_sum", 0), ("uq", 0), ("att", 6),
            ("kvn_out", 0), ("uq", 1), ("att", 7), ("km", 0), ("vm", 0), ("swap", 0)] + [("att", a) for a in range(8, 18)]
        MLA_FILLS = [f for f in range(11, 26) if f not in (12, 14, 20)]

        def wait_fill(eng, f):
            if f in MLA_FILLS:
                eng.wait_ge(sem("mla_fill"), MLA_FILLS.index(f) + 1)
            else:
                eng.wait_ge(chunk_used, first["odd"] + {12: 12, 14: 13, 20: 14}.get(f, f + 1))

        ACC_ENDS = ["even_out", "ffn0", "odd_out", "ffn1", "sc", "mlp"]

        def wait_acc(eng, which, q):
            if q < 3:
                eng.wait_ge(sem("acc_done"), 3 * ACC_ENDS.index(which) + q + 1)
            else:
                order_ = ["even", "even_out", "ffn0", "odd", "odd_out", "ffn1", "sc", "mlp", "end"]
                eng.wait_ge(chunk_used, first[order_[order_.index(which) + 1]])

        ADA_N = 3 * KT

        def ada_step(dve, n):
            b, k = n // KT, n % KT
            dve.wait_ge(sem(f"ada_landed{n % 2}"), 16 * (n // 2 + 1))
            if k:
                dve.wait_ge(sem("ada_fma"), n)
                dve.scalar_tensor_tensor(out=ada_acc[:, b, :], in0=ada_raw[:, n % 2, :], scalar=silu_c[:, k:k + 1],
                                         in1=ada_acc[:, b, :], op0=ALU.mult, op1=ALU.add).then_inc(sem("ada_fma"), 1)
            else:
                dve.tensor_scalar(ada_acc[:, b, :], ada_raw[:, n % 2, :], silu_c[:, k:k + 1], None, ALU.mult)\
                    .then_inc(sem("ada_fma"), 1)

        def conv_silu(act, p):
            t = 8 + 2 * (p - 1) if p <= 2 else 2 * (p - 3)
            act.wait_ge(sem("conv_done"), p)
            act.activation(xbc[:, t:t + 2, :], conv_acc[:, p % 2, :, :], ACT.Silu).then_inc(sem("xbc_ready"), 1)

        v1, v2, v3 = rows
        vector_rows = (
            (v1, 0, 48, A["conv_w"][0].rearrange("j (t p) -> (j t) p", p=P)),
            (v1, 48, 12, A["conv_b"][0].rearrange("(t p) -> t p", p=P)),
            (v1, 60, 16, A["ln_mix_g"].rearrange("l (t p) -> (l t) p", p=P)),
            (v1, 76, 16, A["ln_mix_b"].rearrange("l (t p) -> (l t) p", p=P)),
            (v1, 92, 16, A["ln_ffn_g"].rearrange("l (t p) -> (l t) p", p=P)),
            (v1, 108, 16, A["ln_ffn_b"].rearrange("l (t p) -> (l t) p", p=P)),
            (v2, 0, 4, A["pool_scale"][0].rearrange("(t p) -> t p", p=P)),
            (v2, 4, 8, A["ssm_norm_w"][0].rearrange("(t p) -> t p", p=P)),
            (v2, 12, 4, A["q_norm_w"][0].rearrange("(t p) -> t p", p=P)),
            (v2, 16, 2, A["kv_norm_w"][0].rearrange("(t p) -> t p", p=P)),
            (v2, 18, 32, A["norm_gains_2"][0].rearrange("i (t p) -> (i t) p", p=P)),
            (v2, 50, 24, A["sc_conv_2"][0].rearrange("j (t p) -> (j t) p", p=P)),
            (v3, 0, 48, A["ada_b_2"][0].rearrange("(t p) -> t p", p=P)),
            (v3, 48, 8, A["c_2"][0].rearrange("(t p) -> t p", p=P)))

        block = ctx.enter_context(nc.Block())

        @block.sync
        def _(sp):
            for t in range(2):
                sp.dma_start(sq[:, 4 * t:4 * t + 4, :].rearrange("p a s -> p (a s)"),
                             A["x"][0, t * P:(t + 1) * P, :]).then_inc(sem("x_landed"), 16)
            for c in range(n_chunks):
                if c >= RING:
                    sp.wait_ge(lo_split, c - RING + 1)
                sp.dma_start(slot(raw, c), chunks[c][0]).then_inc(raw_landed[c % RING], 16)
            if stop:
                return
            for half in range(2):
                for t in range(2):
                    sp.wait_ge(sem(("out_rows_act", "out_rows_dve")[t]), half + 1)
                    sp.dma_start(out[0, t * P:(t + 1) * P, half * 512:half * 512 + 512],
                                 sq[:, 4 * t + 2 * half:4 * t + 2 * half + 2, :].rearrange("p a s -> p (a s)"))\
                      .then_inc(sem("stored"), 16)
            sp.wait_ge(sem("stored"), 64)

        @block.gpsimd
        def _(pool):
            for dst, o, n, src in vector_rows[6:]:
                pool.dma_start(dst[o:o + n, :], src).then_inc(sem("rows_landed_pool"), 16)
            pool.memset(ones[:, :], 1.0).then_inc(sem("fixed"), 1)
            with nc.allow_non_contiguous_dma(reason="a few small vectors"):
                for i, (name, n) in enumerate((("dt_bias", 16), ("a_log", 16), ("fgate_b", 8))):
                    pool.dma_start(head_vec[0:n, (0, 1, 3)[i]:(0, 1, 3)[i] + 1],
                                   A[name].rearrange("a (h o) -> (a h) o", o=1)).then_inc(sem("heads_landed"), 16)
                for e in range(2):
                    pool.dma_start(d_skip[64 * e:64 * e + 64, :],
                                   A["d_skip"][0:1, e::2].to_broadcast([64, KT])).then_inc(sem("heads_landed"), 16)
            pool.dma_start(pool_w_sb[:, :, :], A["pool_w"][0].rearrange("g c d -> c g d")).then_inc(sem("poolw_landed"), 16)

            for t in (u_pad[:, :, 0:16], win_a[:, :, 0:16], win_b[:, :, 0:16]):
                pool.memset(t, 0.0).then_inc(sem("pad_zero"), 1)
            pool.wait_ge(sem("pad_zero"), 3)
            pool.wait_ge(sem("even_evac"), 8)
            src = u_pad
            for lv, dst in enumerate((win_a, win_b, win_a, win_b)):
                sh = 1 << lv
                pool.tensor_tensor(dst[:, lv:4, 16:16 + S], src[:, lv:4, 16:16 + S], src[:, lv:4, 16 - sh:16 - sh + S],
                                   ALU.add).then_inc(sem("window"), 1)
                pool.wait_ge(sem("window"), lv + 1)
                src = dst
            for g, w in enumerate((2, 4, 8, 16)):
                t = (win_a, win_b)[g % 2]
                if g == 0:
                    pool.wait_ge(sem("const_landed"), 16)
                o = CONST_COLS["inv_count"][0] + 16 * g
                pool.tensor_tensor(t[:, g, 16:32], t[:, g, 16:32], const[:, o:o + 16], ALU.mult).then_inc(sem("window"), 1)
                pool.tensor_scalar(t[:, g, 32:16 + S], t[:, g, 32:16 + S], 1.0 / w, None, ALU.mult).then_inc(sem("window"), 1)
                pool.wait_ge(sem("window"), 4 + 2 * g + 2)
                pool.tensor_tensor(pool_y[:, g, :], t[:, g, 16:16 + S], u_pad[:, g, 16:16 + S], ALU.subtract)\
                    .then_inc(sem("pool_diff"), 1)

            if on("ffn1"):
                pool.wait_ge(*norm("ln2", "lo", 4))
                for n in range(ADA_N):
                    if n >= 2:
                        pool.wait_ge(sem("ada_fma"), n - 1)
                    pool.dma_start(ada_raw[:, n % 2, :], A["ada_w_2"][0][n % KT * P:(n % KT + 1) * P,
                                                                         n // KT * CH:(n // KT + 1) * CH])\
                        .then_inc(sem(f"ada_landed{n % 2}"), 16)

        @block.tensor
        def _(pe):
            def mm3(dst, c, cols, k, hi, lo, start, stop_, kk=None):
                kk = k if kk is None else kk
                wh, wl = slot(w_hi, c)[:, kk, cols], slot(w_lo, c)[:, kk, cols]
                pe.matmul(dst, wh, hi, start=start, stop=False, skip_group_check=True)
                pe.matmul(dst, wh, lo, start=False, stop=False, skip_group_check=True)
                return pe.matmul(dst, wl, hi, start=False, stop=stop_, skip_group_check=True)

            def col(c, bank, hi, lo, operand=None):
                _, kt, n, copies = chunks[c]
                n *= copies
                pe.wait_ge(lo_split, c + 1)
                for m in range(0, n, P):
                    w = min(P, n - m)
                    for k in range(kt):
                        if operand and m == 0 and k % 2 == 0:
                            pe.wait_ge(operand[0], operand[1] + k // 2 + 1)
                        last = mm3(PS[0:w, bank, (m // P) * S:(m // P) * S + S], c, slice(m, m + w), k,
                                   hi[:, k, :], lo[:, k, :], k == 0, k == kt - 1)
                last.then_inc(chunk_used, 1)

            def first_two(c, banks, hi, lo, operand):
                pe.wait_ge(lo_split, c + 2)
                for k in range(KT):
                    if k % 2 == 0:
                        pe.wait_ge(operand[0], operand[1] + k // 2 + 1)
                    for i in range(2):
                        n = chunks[c + i][2] * chunks[c + i][3]
                        for m in range(0, n, P):
                            last = mm3(PS[:, banks[i], (m // P) * S:(m // P) * S + S], c + i, slice(m, m + P), k,
                                       hi[:, k, :], lo[:, k, :], k == 0 and m == 0, k == KT - 1)
                        if k == KT - 1:
                            last.then_inc(chunk_used, 1)

            def rows_acc(c, hi, lo, k_first, k_last):
                pe.wait_ge(lo_split, c + 1)
                if k_last:
                    for n in range(8):
                        for kk in range(2):
                            last = mm3(ACC[n], c, slice(n * P, n * P + P), 0, hi[:, kk, :], lo[:, kk, :], False, kk == 1, kk=kk)
                        if n in (1, 3, 5):
                            last.then_inc(sem("acc_done"), 1)
                    last.then_inc(chunk_used, 1)
                    return
                for kk in range(2):
                    for n in range(8):
                        last = mm3(ACC[n], c, slice(n * P, n * P + P), 0, hi[:, kk, :], lo[:, kk, :],
                                   k_first and kk == 0 and n % 2 == 0, k_last and kk == 1, kk=kk)
                last.then_inc(chunk_used, 1)

            def norm_sums(name, t=KT, bank=5):
                if name in LNS:
                    parts = [(hid[:, 0, :, :], 0, "folded", 1, 0), (hid[:, 1, :, :], 0, "folded", 2, 0),
                             (hid[:, 2, :, :], 0, "folded", 5, 2)]
                elif t == KT:
                    parts = [(hid[:, 2, :, :], 0, "folded", 3, 2)]
                else:
                    parts = [(sq, q, "sq", q + 1, 2) for q in range(t // 2)]
                last_part = {o: i for i, (_, _, _, _, o) in enumerate(parts)}
                for i, (src, q, kind, n, o) in enumerate(parts):
                    pe.wait_ge(*norm(name, kind, n))
                    for k in (2 * q, 2 * q + 1):
                        for j in range(2):
                            last = pe.matmul(PS[:, bank, o + j:o + j + 1], src[:, k, j * P:(j + 1) * P], ones[:, 0:1],
                                             start=i == 0 and k == 0 and j == 0, stop=i == last_part[o] and k == 2 * q + 1,
                                             skip_group_check=True)
                last.then_inc(sem("norm_var"), 1)

            def norm_bcast(name, bank=6):
                pe.wait_ge(*norm(name, "rcp", 1))
                for i in range(4 if name in LNS else 2):
                    last = pe.matmul(PS[:, bank, i * P:(i + 1) * P], rstd[:, i:i + 1].to_broadcast([P, P]), ident,
                                     start=True, stop=True)
                last.then_inc(sem("norm_rb"), 1)

            def norm_scale(name, t=KT):
                norm_sums(name, t)
                norm_bcast(name)

            def ffn(name, base, operand):
                hid_lo_ok = sem(f"{name}_hid_lo")

                def fill(i, c):
                    b = 4 + 2 * (i % 2)
                    col(c, b, x_hi, x_lo)
                    col(c + 1, b + 1, x_hi, x_lo)

                first_two(base, (4, 5), x_hi, x_lo, norm(operand, "lo", 0))
                for i in range(1, NF):
                    fill(i, base + 2 + 3 * (i - 1))
                    pe.wait_ge(hid_lo_ok, i)
                    rows_acc(base + 4 + 3 * (i - 1), hid_hi[:, (i - 1) % 2, :, :], hid_lo[:, (i - 1) % 2, :, :],
                             i == 1, False)
                pe.wait_ge(hid_lo_ok, NF)
                rows_acc(base + 2 + 3 * (NF - 1), hid_hi[:, (NF - 1) % 2, :, :], hid_lo[:, (NF - 1) % 2, :, :],
                         False, True)

            pe.wait_ge(sem("ident_landed"), 16)
            pe.wait_ge(sem("x_landed"), 32)
            xt = sq[:, :, :].rearrange("p (t q) s -> p t (q s)", t=2)
            for b in range(4):
                for k in (2 * b, 2 * b + 1):
                    for t in range(2):
                        o = (k % 2) * S + t * P
                        last = pe.transpose(PS[:, b, o:o + P], xt[:, t, k * P:(k + 1) * P], ident)
                last.then_inc(sem("x_turned"), 1)

            base = first["even"]
            col(base, 4, x_hi, x_lo, (sem("x_lo_ready"), 0))
            col(base + 1, 5, x_hi, x_lo)
            pe.wait_ge(sem("rows_landed_act"), 16 * 6)
            pe.wait_ge(sem("rows_landed_pool"), 16 * 8)
            for i, n in enumerate((124, 74, 56)):
                last = pe.transpose(PS[:, 7, i * P:i * P + n], rows[i][0:n, :], ident[0:n, 0:n])
            last.then_inc(sem("vecs_turned"), 1)
            pe.wait_ge(sem("const_landed"), 16)

            def even_proj(p):
                if p >= 9:
                    pe.wait_ge(sem("even_evac"), p - 2)
                elif p == 3:
                    pe.wait_ge(sem("vecs_ready"), 1)
                elif p == 4:
                    pe.wait_ge(sem("dt_raw"), 1)
                elif p > 4:
                    pe.wait_ge(sem("even_evac"), 6 if p == 8 else p - 4)
                col(base + p, 4 + p % 4 if p < 7 else 6 + p % 2, x_hi, x_lo)

            def even_small(_):
                pe.wait_ge(sem("da_ready"), 1)
                for j in range(2):
                    for q in range(2):
                        o = 32 * j + 16 * q
                        last = pe.transpose(PS[:, 0, o:o + 16], small[0:16, q, j * P:(j + 1) * P], ident[0:16, 0:16])
                last.then_inc(sem("tok_turned"), 1)
                pe.wait_ge(sem("xbc_ready"), 2)
                for g in range(2):
                    last = pe.transpose(PS[:, 1, g * P:(g + 1) * P], xbc[:, 8 + g, 0:P], ident)
                last.then_inc(sem("b_turned"), 1)
                for j in range(2):
                    for g in range(2):
                        q = 2 * j + g
                        last = pe.matmul(PS[:, 2, q * P:(q + 1) * P], xbc[:, 8 + g, j * P:(j + 1) * P],
                                         xbc[:, 10 + g, j * P:(j + 1) * P], start=True, stop=True)
                last.then_inc(sem("cb_done"), 1)

            def even_head(j):
                if j == 0:
                    pe.wait_ge(sem("tok_ready"), 1)
                    pe.wait_ge(sem("fixed"), 1)
                    for c in range(2):
                        pe.matmul(PS[:, 0, 64 + 16 * c:80 + 16 * c], triu, tok[:, c, 16:32], start=True, stop=True)
                    pe.matmul(PS[:, 0, 96:112], ones[:, :], tok[:, 0, 16:32], start=True, stop=True)\
                        .then_inc(sem("acs_done"), 1)
                if j == 0:
                    pe.wait_ge(sem("xbc_ready"), 6)
                    pe.wait_ge(sem("even_evac"), 5)
                else:
                    pe.wait_ge(sem("y_ready"), 8)
                for k in range(KT):
                    o = (k % 4) * P
                    last = pe.transpose(PS[:, 4 + k // 4, o:o + P], xbc[:, k, j * P:(j + 1) * P], ident)
                last.then_inc(sem("xtok_done"), 1)

            def even_bcast(j):
                if j == 0:
                    pe.wait_ge(sem("acs_ready"), 2)
                    pe.wait_ge(sem("b_tok_ready"), 1)
                    pe.wait_ge(sem("cb_ready"), 1)
                else:
                    pe.wait_ge(sem("seg_done"), 4)
                for h in range(HEADS):
                    last = pe.matmul(PS[:, h // 4, (h % 4) * P:(h % 4) * P + P],
                                     tok[:, j, 16 + h:17 + h].to_broadcast([P, P]), triu, start=True, stop=True)
                    if h % 4 == 3:
                        last.then_inc(sem("acs_bcast"), 1)

            def even_state(_):
                pe.wait_ge(sem("xdec_ready"), 1)
                for g in range(2):
                    pe.matmul(PS[:, 4 + g, :], b_tok[:, g * P:(g + 1) * P], x_dec[:, g * 512:(g + 1) * 512],
                              start=True, stop=True).then_inc(sem("state_done"), 1)

            def even_y(j):
                pe.wait_ge(sem("lmat_ready"), 2 * j + 2)
                if j:
                    pe.wait_ge(sem("xdt_ready"), 4)
                    pe.wait_ge(sem("cdec_ready"), 2)
                else:
                    pe.wait_ge(sem("state_ready"), 2)
                for k in range(KT):
                    o = (k % 4) * P
                    for e in range(2):
                        h = 2 * k + e
                        dst = PS[64 * e:64 * e + 64, 4 + k // 4, o:o + P]
                        last = pe.matmul(dst, x_dt[:, h * 64:h * 64 + 64], lmat[:, h, :], start=True, stop=j == 0)
                        if j:
                            last = pe.matmul(dst, state[:, h * 64:h * 64 + 64], e_acs[:, h, :], start=False, stop=True)
                    last.then_inc(sem("y_done"), 1)

            def even_pool(i):
                if i == 0:
                    pe.wait_ge(sem("even_evac"), 11)
                    pe.wait_ge(sem("pool_diff"), 4)
                    pe.wait_ge(sem("poolw_landed"), 16)
                else:
                    pe.wait_ge(sem("pool_scaled"), 2)
                for g in (2 * i, 2 * i + 1):
                    last = pe.matmul(PS[:, 7, (g % 2) * S:(g % 2) * S + S], pool_w_sb[:, g, :], pool_y[:, g, :],
                                     start=True, stop=True)
                last.then_inc(sem("pool_done"), 1)
                if i == 1:
                    pe.wait_ge(sem("seg_done"), 8)
                    pe.wait_ge(sem("eacs_done"), 4)
                    pe.wait_ge(sem("pool_lo_ready"), 1)
                    rows_acc(base + 13, pool_hi[:, 0:2, :], pool_lo[:, 0:2, :], True, False)

            for step, arg in EVEN_STEPS:
                {"proj": even_proj, "small": even_small, "head": even_head, "bcast": even_bcast, "state": even_state,
                 "y": even_y, "pool": even_pool}[step](arg)
            pe.wait_ge(sem("pool_lo_ready"), 2)
            rows_acc(base + 14, pool_hi[:, 2:4, :], pool_lo[:, 2:4, :], False, False)
            norm_scale("ssm")
            for q in range(4):
                pe.wait_ge(*norm("ssm", "lo", q + 1))
                rows_acc(base + 15 + q, x_hi[:, 2 * q:2 * q + 2, :], x_lo[:, 2 * q:2 * q + 2, :], False, q == 3)
            norm_scale("ln0")
            if not on("ffn0"):
                return
            ffn("ffn0", first["ffn0"], "ln0")
            norm_scale("ln1")
            if not on("odd"):
                return

            base = first["odd"]
            first_two(base, (4, 5), x_hi, x_lo, norm("ln1", "lo", 0))

            def odd_free(f):
                if f < 24:
                    pe.wait_ge(sem("odd_evac"), f - 2)
                else:
                    pe.wait_ge(*((sem("kr_rot"), 1) if f == 24 else (sem("qm_rot"), 1)))
                return 4 + f % 3

            def odd_proj(p):
                bank = odd_free(p) if p > 2 else 6
                if p not in (5, 6):
                    col(base + p, bank, x_hi, x_lo)
                    return
                pe.wait_ge(lo_split, base + p + 1)
                wh, wl = slot(w_hi, base + p), slot(w_lo, base + p)
                for j in range(2):
                    dst = PS[:, bank, j * S:(j + 1) * S]
                    for k in range(KT):
                        xh, xl = x_hi[:, k, j * P:(j + 1) * P], x_lo[:, k, j * P:(j + 1) * P]
                        pe.matmul(dst, xh, wh[:, k, :], start=k == 0, stop=False)
                        pe.matmul(dst, xh, wl[:, k, :], start=False, stop=False)
                        last = pe.matmul(dst, xl, wh[:, k, :], start=False, stop=k == KT - 1)
                last.then_inc(chunk_used, 1)

            def qn_sum(_):
                norm_sums("qn", 4, 7)

            def qn_out(_):
                norm_bcast("qn", 7)

            def kvn_sum(_):
                pe.wait_ge(*norm("qn", "scaled", 2))
                norm_sums("kvn", 2, 7)

            def kvn_out(_):
                norm_bcast("kvn", 7)

            def uq(c):
                pe.wait_ge(lo_split, base + 12 + c)
                if c == 0:
                    pe.wait_ge(*norm("qn", "lo", 2))
                for h in range(4 * c, 4 * c + 4):
                    bank = odd_free(11 + h // 2) if h % 2 == 0 else bank
                    for k in range(4):
                        last = mm3(PS[0:96, bank, (h % 2) * S:(h % 2) * S + S], base + 11 + c,
                                   slice(96 * (h % 4), 96 * (h % 4) + 96), k, cq_hi[:, k, :], cq_lo[:, k, :], k == 0, k == 3)
                    if h == 4 * c + 1:
                        last.then_inc(sem("mla_fill"), 1)
                last.then_inc(chunk_used, 1)

            kv_h, kv_l = (slot(t, base + 13).rearrange("p k (h e) -> p k h e", h=MLA_H) for t in (w_hi, w_lo))

            def km_fills(_):
                pe.wait_ge(lo_split, base + 14)
                pe.wait_ge(*norm("kvn", "lo", 1))
                for h in range(MLA_H):
                    bank = odd_free(15 + h // 2) if h % 2 == 0 else bank
                    dst = PS[0:96, bank, (h % 2) * S:(h % 2) * S + S]
                    for k in range(2):
                        pe.matmul(dst, kv_h[:, k, h, 0:96], ckv_hi[:, k, :], start=k == 0, stop=False)
                        pe.matmul(dst, kv_h[:, k, h, 0:96], ckv_lo[:, k, :], start=False, stop=False)
                        last = pe.matmul(dst, kv_l[:, k, h, 0:96], ckv_hi[:, k, :], start=False, stop=k == 1)
                    if h % 2:
                        last.then_inc(sem("mla_fill"), 1)

            def vm_fills(_):
                for j in range(2):
                    bank = odd_free(19 + j)
                    for k in range(2):
                        xh, xl = ckv_hi[:, k, j * P:(j + 1) * P], ckv_lo[:, k, j * P:(j + 1) * P]
                        pe.matmul(PS[:, bank, :], xh, kv_h[:, k, :, 64:128], start=k == 0, stop=False)
                        pe.matmul(PS[:, bank, :], xh, kv_l[:, k, :, 64:128], start=False, stop=False)
                        last = pe.matmul(PS[:, bank, :], xl, kv_h[:, k, :, 64:128], start=False, stop=k == 1)
                    last.then_inc(sem("mla_fill") if j == 0 else chunk_used, 1)

            def swap_fills(_):
                swap = cst("swap", 96)
                pe.matmul(PS[0:96, odd_free(21), 0:S], swap, kr[:, 0, :], start=True, stop=True).then_inc(sem("mla_fill"), 1)
                for h in range(MLA_H):
                    bank = odd_free(22 + h // 2) if h % 2 == 0 else bank
                    last = pe.matmul(PS[0:96, bank, (h % 2) * S:(h % 2) * S + S], swap, qm[:, h, :], start=True, stop=True)
                    if h % 2:
                        last.then_inc(sem("mla_fill"), 1)

            def scores(a):
                if a >= 2:
                    pe.wait_ge(sem("masked"), 2 * (a - 1))
                if a == 0:
                    pe.wait_ge(sem("neg_f_ready"), 1)
                    pe.wait_ge(sem("odd_evac"), 5)
                if a == FOX_H:
                    pe.wait_ge(sem("odd_evac"), 19)
                    pe.wait_ge(sem("kr_rot"), 1)
                    pe.wait_ge(sem("qm_rot"), 4)
                b = a % 2
                for j, kw, o in ((0, P, 0), (1, S, P)):
                    dst = PS[:, b, o:o + kw]
                    qs = slice(j * P, (j + 1) * P)
                    if a < FOX_H:
                        pe.matmul(dst, qz[:, a, qs], kf[:, a // 2, 0:kw], start=True, stop=False)
                        last = pe.matmul(dst, ident[:, a:a + 1].to_broadcast([P, P]), neg_f[:, 0:kw], start=False, stop=True)
                    else:
                        h = a - FOX_H
                        last = pe.matmul(dst, qm[:, h, qs], km[:, h, 0:kw], start=True, stop=True)
                last.then_inc(sem("scored"), 1)

            def turn(a):
                pe.wait_ge(sem("prob_ready"), 2 * a + 2)
                if a >= 1:
                    pe.wait_ge(sem("prob_t_ready"), a)
                for o in (0, P, 2 * P):
                    last = pe.transpose(PS[:, 2, o:o + P], prob[:, a % 2, o:o + P], ident)
                last.then_inc(sem("prob_turned"), 1)

            def attend(a):
                pe.wait_ge(sem("prob_t_ready"), a + 1)
                pair, e = a // 2, a % 2
                if e == 0 and pair >= 1:
                    pe.wait_ge(sem("o_lo"), pair)
                if a in (0, FOX_H):
                    pe.wait_ge(sem("odd_evac"), 21 if a else 7)
                v, h = (v_tok, a) if a < FOX_H else (vm_tok, a - FOX_H)
                pt = prob_t[:, a % 2, :]
                pe.matmul(PS[64 * e:64 * e + 64, 3, 0:S], v[:, 0, h * 64:h * 64 + 64], pt[:, 0:S], start=True, stop=False,
                          skip_group_check=True)
                pe.matmul(PS[64 * e:64 * e + 64, 3, P:S], v[:, 1, h * 64:h * 64 + 64], pt[:, S:384], start=False, stop=True,
                          skip_group_check=True).then_inc(sem("attended"), 1)

            def attention(a):
                if a < 16:
                    scores(a)
                if 1 <= a <= 16:
                    turn(a - 1)
                if a >= 2:
                    attend(a - 2)

            for step, arg in ODD_STEPS:
                {"proj": odd_proj, "att": attention, "qn_sum": qn_sum, "qn_out": qn_out, "kvn_sum": kvn_sum,
                 "kvn_out": kvn_out, "uq": uq, "km": km_fills, "vm": vm_fills, "swap": swap_fills}[step](arg)
            base = first["odd_out"]
            pe.wait_ge(sem("o_lo"), MLA_H)
            for q in range(4):
                rows_acc(base + q, x_hi[:, 2 * q:2 * q + 2, :], x_lo[:, 2 * q:2 * q + 2, :], q == 0, q == 3)
            norm_scale("ln2")
            if not on("ffn1"):
                return
            ffn("ffn1", first["ffn1"], "ln2")
            if not on("sc"):
                norm_scale("ln3")
                return
            def mod_sums(n0, n1):
                pe.wait_ge(sem("ada_fma"), KT * ((n1 - 1) // 16 + 1))
                for n in range(n0, n1):
                    last = pe.matmul(PS[:, 7, n:n + 1], ada_acc[:, n // 16, (n % 16) * P:(n % 16) * P + P], ones[:, 0:1],
                                     start=True, stop=True)
                last.then_inc(sem("mod_done"), 1)

            norm_sums("ln3")
            mod_sums(0, 4)
            norm_bcast("ln3")
            mod_sums(4, 24)
            norm_scale("pre")
            base = first["sc"]
            c, f = base, 0
            for q in range(4):
                for part in range(3):
                    if q == 0 and part < 2:
                        if part == 0:
                            first_two(base, (4, 5), x_hi, x_lo, norm("pre", "lo", 0))
                        c, f = c + 1, f + 1
                        continue
                    if f == 3:
                        pe.wait_ge(sem("mod_evac"), 2)
                    if f >= 4:
                        pe.wait_ge(sem(("sc_evac_c", "cv_ready", "sc_evac_b")[(f - 4) % 3]), (f - 4) // 3 + 1)
                    col(c, 4 + f % 4, x_hi, x_lo)
                    c, f = c + 1, f + 1
                if q:
                    pe.wait_ge(sem("sc_lo"), q)
                    rows_acc(c, hid_hi[:, (q - 1) % 2, :, :], hid_lo[:, (q - 1) % 2, :, :], q == 1, False)
                    c += 1
            pe.wait_ge(sem("sc_lo"), 4)
            rows_acc(c, hid_hi[:, 1, :, :], hid_lo[:, 1, :, :], False, True)
            mod_sums(24, 32)
            norm_scale("post")
            mod_sums(32, 48)
            norm_scale("preff")
            if not on("mlp"):
                return
            base = first["mlp"]
            first_two(base, (4, 5), x_hi, x_lo, norm("preff", "lo", 0))
            for i in range(1, NM):
                if i > 1:
                    col(base + 1 + 2 * (i - 1), 4 + i % 3, x_hi, x_lo)
                pe.wait_ge(sem("mlp_lo"), i)
                rows_acc(base + 2 + 2 * (i - 1), hid_hi[:, (i - 1) % 3, :, :], hid_lo[:, (i - 1) % 3, :, :], i == 1, False)
            pe.wait_ge(sem("mlp_lo"), NM)
            rows_acc(base + 1 + 2 * (NM - 1), hid_hi[:, (NM - 1) % 3, :, :], hid_lo[:, (NM - 1) % 3, :, :], False, True)
            norm_scale("postff")
            for k in range(KT):
                pe.wait_ge(sem("final_x"), k + 1)
                for t in range(2):
                    last = pe.transpose(PS[:, 2 * t + k // 4, (k % 4) * P:(k % 4) * P + P], x[:, k, t * P:(t + 1) * P], ident)
                if k % 4 == 3:
                    last.then_inc(sem("out_turned"), 1)

        @block.scalar
        def _(act):
            done = [0]

            def split(upto):
                while done[0] <= min(upto, n_chunks - 1):
                    c = done[0]
                    act.wait_ge(raw_landed[c % RING], 16 * (c // RING + 1))
                    if c >= RING:
                        act.wait_ge(chunk_used, c - RING + 1)
                    act.activation(split_view(w_hi, c), split_view(raw, c), ACT.Copy).then_inc(hi_split, 1)
                    done[0] += 1

            def squares(name, src, t=KT, ready=None):
                for q in range(t // 2):
                    if ready:
                        act.wait_ge(ready[0], ready[1] + q + 1)
                    act.activation(sq[:, 2 * q:2 * q + 2, :], src[:, 2 * q:2 * q + 2, :], ACT.Square)\
                       .then_inc(sem("norm_sq"), 1)

            def norm_std(name, eps=RMS_EPS, width=D, bank=5):
                act.wait_ge(sem("eps_set"), 1)
                i = list(NORM_TILES).index(name)
                act.activation(table_sb[:, i:i + 1], eps_sb[:, 0:1], ACT.Sqrt)
                if name in LNS:
                    act.wait_ge(*norm(name, "small", 4))
                    act.activation(std[:, :], moments[:, 2:4], ACT.Sqrt, bias=eps_col(eps)).then_inc(sem("norm_std"), 1)
                else:
                    act.wait_ge(*norm(name, "var", 1))
                    act.activation(std[:, :], PS[:, bank, 2:4], ACT.Sqrt, bias=eps_col(eps), scale=1.0 / width)\
                       .then_inc(sem("norm_std"), 1)

            def norm_stats(name, src, eps=RMS_EPS, ready=None, upto=None):
                squares(name, src, KT, ready)
                if upto is not None:
                    split(upto)
                norm_std(name, eps)

            def eps_col(eps):
                return eps_sb[:, 0:1] if eps == LN_EPS else eps_sb[:, 1:2]

            def operand_hi(name, src, dst, gains, biases, t=KT):
                for k in range(t):
                    if k % 2 == 0:
                        act.wait_ge(*norm(name, "scaled", k // 2 + 1))
                    act.activation(dst[:, k, :], src[:, k, :], ACT.Identity, scale=gains(k),
                                   bias=biases(k) if biases else 0.0).then_inc(sem("norm_hi"), 1)

            def ffn(name, base):
                for i in range(NF):
                    g = base if i == 0 else base + 2 + 3 * (i - 1)
                    split(g + 2)
                    act.wait_ge(chunk_used, g + 1)
                    if i >= 2:
                        act.wait_ge(sem(f"{name}_hid"), i - 1)
                    act.activation(gate_s[:, i % 2, :, :], bank2(4 + 2 * (i % 2)), ACT.Silu).then_inc(sem(f"{name}_silu"), 1)
                    split(g + 3)
                    act.wait_ge(sem(f"{name}_hid"), i + 1)
                    act.activation(hid_hi[:, i % 2, :, :], hid[:, i % 2, :, :], ACT.Copy).then_inc(sem(f"{name}_hid_hi"), 1)
                    if i < NF - 1:
                        split(g + 4 if i else g + 3)

            act.dma_start(const[:, 0:P], A["consts"][:, 0:P]).then_inc(sem("ident_landed"), 16)
            for dst, o, n, src in vector_rows[:6]:
                act.dma_start(dst[o:o + n, :], src).then_inc(sem("rows_landed_act"), 16)
            act.dma_start(const[:, P:], A["consts"][:, P:]).then_inc(sem("const_landed"), 16)
            for b in range(4):
                act.wait_ge(sem("x_turned"), b + 1)
                act.activation(x_hi[:, 2 * b:2 * b + 2, :], bank2(b), ACT.Copy).then_inc(sem("x_hi_ready"), 1)
            split(2)
            act.wait_ge(sem("heads_landed"), 16 * 5)
            act.activation(head_vec[:, 2:3], head_vec[:, 1:2], ACT.Exp).then_inc(sem("a_ready"), 1)
            split(3)
            act.wait_ge(sem("dt_raw"), 1)
            act.activation(small[:, 2, :], small[:, 0, :], ACT.Abs).then_inc(sem("dt_act"), 1)
            act.wait_ge(sem("dt_act"), 1)
            act.activation(small[:, 2, :], small[:, 2, :], ACT.Exp, scale=-1.0).then_inc(sem("dt_act"), 1)
            act.wait_ge(sem("dt_act"), 2)
            act.activation(small[:, 2, :], small[:, 2, :], ACT.Ln, bias=1.0).then_inc(sem("dt_act"), 1)
            act.wait_ge(sem("vecs_ready"), 1)
            act.activation(silu_c[:, :], vecs[:, 2, 48:56], ACT.Silu).then_inc(sem("silu_c_ready"), 1)

            base = first["even"]

            def even_proj(p):
                split(base + p + 2)
                act.wait_ge(chunk_used, base + p + 1)
                bank = bank2(4 + p % 4 if p < 7 else 6 + p % 2)
                if p <= 6:
                    if p == 1:
                        act.wait_ge(sem("conv_pad"), 1)
                    if p >= 3:
                        act.wait_ge(sem("conv_done"), p - 2)
                    act.activation(conv_in[:, p % 2, :, 3:3 + S], bank, ACT.Copy).then_inc(sem("even_evac"), 1)
                    if p >= 2:
                        conv_silu(act, p - 1)
                elif p <= 8:
                    act.wait_ge(sem("pad_zero"), 3)
                    act.activation(u_pad[:, 2 * (p - 7):2 * (p - 7) + 2, 16:16 + S], bank, ACT.Copy)\
                       .then_inc(sem("even_evac"), 1)
                else:
                    act.activation(z_silu[:, 2 * (p - 9):2 * (p - 9) + 2, :], bank, ACT.Silu).then_inc(sem("even_evac"), 1)

            def even_small(_):
                conv_silu(act, 6)
                act.wait_ge(sem("b_turned"), 1)
                act.activation(b_tok[:, :], PS[:, 1, 0:S], ACT.Copy).then_inc(sem("b_tok_ready"), 1)

            def even_head(j):
                if j == 0:
                    act.wait_ge(sem("acs_ready"), 2)
                    act.activation(decay[:, 1, :], decay[:, 0, :], ACT.Exp).then_inc(sem("decay_ready"), 1)

            def even_pool(i):
                act.wait_ge(sem("pool_done"), i + 1)
                for g in (2 * i, 2 * i + 1):
                    act.activation(pool_y[:, g, :], PS[:, 7, (g % 2) * S:(g % 2) * S + S], ACT.Identity, scale=vec(1, g))\
                       .then_inc(sem("pool_scaled"), 1)
                act.wait_ge(sem("pool_scaled"), 2 * i + 2)
                act.activation(pool_hi[:, 2 * i:2 * i + 2, :], pool_y[:, 2 * i:2 * i + 2, :], ACT.Copy)\
                   .then_inc(sem("pool_hi_ready"), 1)

            def even_bcast(j):
                for q in range(4):
                    act.wait_ge(sem("seg_done"), 4 * j + q + 1)
                    for h in range(4 * q, 4 * q + 4):
                        if j and h == 0:
                            act.wait_ge(sem("y_done"), 8)
                        last = act.activation(lmat[:, h, :], seg[:, (h % 4) * P:(h % 4) * P + P], ACT.Exp,
                                              bias=neg_acs[:, j, h:h + 1])
                    last.then_inc(sem("exp_done"), 1)
                    if j and q == 3:
                        even_pool(0)
                    if j:
                        if q == 0:
                            act.wait_ge(sem("pool_diff"), 4)
                        act.activation(e_acs[:, 4 * q:4 * q + 4, :], PS[:, q, :].rearrange("p (h s) -> p h s", h=4), ACT.Exp)\
                           .then_inc(sem("eacs_done"), 1)

            def even_state(_):
                for g in range(2):
                    act.wait_ge(sem("state_done"), g + 1)
                    act.activation(state[:, g * 512:(g + 1) * 512], PS[:, 4 + g, :], ACT.Copy)\
                       .then_inc(sem("state_ready"), 1)

            even_proj(1)
            for step, arg in EVEN_STEPS:
                if step == "pool":
                    if arg == 1:
                        even_pool(1)
                    continue
                {"proj": even_proj, "small": even_small, "head": even_head, "bcast": even_bcast, "state": even_state,
                 "y": lambda j: None}[step](arg)
            split(first["even_out"] + 2)
            norm_stats("ssm", r, ready=(sem("gated"), 0))
            operand_hi("ssm", r, x_hi, lambda k: vec(1, 4 + k), None)
            base = first["even_out"]

            def layer_norm(name, following, need_hi=True):
                g, b = LNS[name]
                split(first[following] + 1)
                norm_stats(name, r, eps=LN_EPS, ready=norm(name, "resid", 0), upto=first[following] + 2)
                if need_hi:
                    i = list(NORM_TILES).index(name)
                    act.activation(table_sb[:, 11 + i:12 + i], eps_sb[:, 0:1], ACT.Exp if name == "ln1" else ACT.Silu)
                    operand_hi(name, r, x_hi, lambda k: vec(0, g + k), lambda k: vec(0, b + k))

            layer_norm("ln0", "ffn0")
            if not on("ffn0"):
                return
            ffn("ffn0", first["ffn0"])
            layer_norm("ln1", "odd")
            if not on("odd"):
                return

            base = first["odd"]
            act.wait_ge(chunk_used, base + 1)
            act.activation(small[0:8, 0, :], PS[0:8, 4, 0:S], ACT.Identity, bias=head_vec[0:8, 3:4])\
               .then_inc(sem("odd_evac"), 1)
            act.wait_ge(sem("odd_evac"), 1)
            act.activation(small[0:8, 1, :], small[0:8, 0, :], ACT.Abs).then_inc(sem("fg_act"), 1)
            act.wait_ge(sem("fg_act"), 1)
            act.activation(small[0:8, 1, :], small[0:8, 1, :], ACT.Exp, scale=-1.0).then_inc(sem("fg_act"), 1)
            act.wait_ge(sem("fg_act"), 2)
            act.activation(small[0:8, 1, :], small[0:8, 1, :], ACT.Ln, bias=1.0).then_inc(sem("fg_act"), 1)
            act.wait_ge(sem("qz_zero"), 1)

            def odd_proj(p):
                split(base + p + 2)
                wait_fill(act, p)
                bank = bank2(4 + p % 3)
                if p <= 2:
                    last = act.activation(kf[:, 2 * (p - 1):2 * (p - 1) + 2, :], bank, ACT.Copy)
                elif p <= 4:
                    t = 2 * (p - 3)
                    for e in range(2):
                        rs = slice(64 * e, 64 * e + 64)
                        last = act.activation(qz[rs, 2 * t + e:2 * t + e + 3:2, :], bank[rs], ACT.Copy, scale=0.125)
                elif p <= 6:
                    last = act.activation(v_tok[:, :, (p - 5) * S:(p - 4) * S], bank, ACT.Copy)
                elif p <= 8:
                    last = act.activation(cq[:, 2 * (p - 7):2 * (p - 7) + 2, :], bank, ACT.Copy)
                elif p == 9:
                    last = act.activation(ckv[:, :, :], bank, ACT.Copy)
                else:
                    last = act.activation(kr[:, 0, :], PS[0:96, 4 + p % 3, 0:S], ACT.Copy)
                last.then_inc(sem("odd_evac"), 1)

            def qn_sum(_):
                act.wait_ge(sem("odd_evac"), 11)
                squares("qn", cq, 4)
                norm_std("qn", width=512, bank=7)

            def qn_out(_):
                operand_hi("qn", cq, cq_hi, lambda k: vec(1, 12 + k), None, 4)

            def kvn_sum(_):
                squares("kvn", ckv, 2)
                act.wait_ge(*norm("qn", "rcp", 1))
                norm_std("kvn", width=256, bank=7)

            def kvn_out(_):
                operand_hi("kvn", ckv, ckv_hi, lambda k: vec(1, 16 + k), None, 2)

            def uq(c):
                split(base + 13)
                for f in (11 + 2 * c, 12 + 2 * c):
                    wait_fill(act, f)
                    act.activation(qm[:, 2 * (f - 11):2 * (f - 11) + 2, :], bank2(4 + f % 3)[0:96], ACT.Copy,
                                   scale=96 ** -0.5).then_inc(sem("odd_evac"), 1)

            def km_fills(_):
                for f in range(15, 19):
                    wait_fill(act, f)
                    act.activation(km[0:64, 2 * (f - 15):2 * (f - 15) + 2, :], bank2(4 + f % 3)[0:64], ACT.Copy)\
                       .then_inc(sem("odd_evac"), 1)

            def vm_fills(_):
                for f in (19, 20):
                    wait_fill(act, f)
                    act.activation(vm_tok[:, f - 19, :], PS[:, 4 + f % 3, :], ACT.Copy).then_inc(sem("odd_evac"), 1)
                split(base + 16)

            def exps(a):
                for j, kw, o in ((0, P, 0), (1, S, P)):
                    act.wait_ge(sem("neg_max"), a + 1)
                    if a >= 2 and j == 0:
                        act.wait_ge(sem("prob_turned"), a - 1)
                    act.activation(prob[:, a % 2, o:o + kw], sc_sb[:, a % 2, o:o + kw], ACT.Exp,
                                   bias=row_max[:, a % 2, j:j + 1], accum_out=row_sum[:, a % 2, j:j + 1])\
                       .then_inc(sem("exped"), 1)

            def o_hi(pair):
                act.wait_ge(sem("attended"), 2 * pair + 2)
                act.activation(x_hi[:, pair, :], PS[:, 3, 0:S], ACT.Copy).then_inc(sem("o_hi"), 1)

            def attention(a):
                if a < 16:
                    exps(a)
                if 1 <= a <= 16:
                    act.wait_ge(sem("prob_turned"), a)
                    if a >= 3:
                        act.wait_ge(sem("attended"), a - 2)
                    act.activation(prob_t[:, (a - 1) % 2, :], PS[:, 2, 0:384], ACT.Copy).then_inc(sem("prob_t_ready"), 1)
                if a >= 3 and a % 2:
                    o_hi((a - 3) // 2)

            odd_proj(1)
            for step, arg in ODD_STEPS:
                {"proj": odd_proj, "att": attention, "qn_sum": qn_sum, "qn_out": qn_out, "kvn_sum": kvn_sum,
                 "kvn_out": kvn_out, "uq": uq, "km": km_fills, "vm": vm_fills, "swap": lambda _: None}[step](arg)
            base = first["odd_out"]
            split(base + 3)
            layer_norm("ln2", "ffn1")
            if not on("ffn1"):
                return
            ffn("ffn1", first["ffn1"])
            layer_norm("ln3", "sc", need_hi=False)
            if not on("sc"):
                return
            norm_stats("pre", x, ready=(sem("ln3_x"), 0))
            act.wait_ge(sem("mod_evac"), 1)
            operand_hi("pre", r, x_hi, lambda k: gain[:, k:k + 1], lambda k: mod[:, k:k + 1])
            c, f = first["sc"], 0
            for q in range(4):
                for part in range(3):
                    split(c + 2)
                    act.wait_ge(chunk_used, c + 1)
                    b = 4 + f % 4
                    if part == 0:
                        if q >= 2:
                            act.wait_ge(sem("cv_ready"), q - 1)
                        act.activation(c_sb[:, q % 2, :, :], bank2(b), ACT.Copy).then_inc(sem("sc_evac_c"), 1)
                    elif part == 2:
                        if q >= 2:
                            act.wait_ge(sem("sc_y"), q - 1)
                        act.activation(b_sb[:, q % 2, :, :], bank2(b), ACT.Copy).then_inc(sem("sc_evac_b"), 1)
                    c, f = c + 1, f + 1
                if q:
                    split(c + 2)
                    c += 1
                act.wait_ge(sem("sc_y"), q + 1)
                act.activation(hid_hi[:, q % 2, :, :], hid[:, q % 2, :, :], ACT.Copy).then_inc(sem("sc_hi"), 1)
            split(first["mlp"] + 1)
            norm_stats("post", r, ready=(sem("post_taken"), 0), upto=first["mlp"] + 2)
            norm_stats("preff", x, ready=(sem("post_x"), 0))
            act.wait_ge(sem("mod_evac"), 3)
            operand_hi("preff", r, x_hi, lambda k: gain[:, 16 + k:17 + k], lambda k: mod[:, 24 + k:25 + k])
            if not on("mlp"):
                return
            base = first["mlp"]
            for i in range(NM):
                c = base if i == 0 else base + 1 + 2 * (i - 1)
                split(c + 2)
                act.wait_ge(chunk_used, c + 1)
                if i >= 2:
                    act.wait_ge(sem("mlp_hid"), i - 1)
                act.activation(gate_s[:, i % 2, :, :], bank2(4 + i % 3), ACT.Relu).then_inc(sem("mlp_relu"), 1)
                act.wait_ge(sem("mlp_hid"), i + 1)
                act.activation(hid_hi[:, i % 3, :, :], hid[:, i % 3, :, :], ACT.Copy).then_inc(sem("mlp_hi"), 1)
                split(c + 3)
            split(n_chunks)
            norm_stats("postff", r, ready=(sem("postff_taken"), 0))
            for half in range(2):
                act.wait_ge(sem("out_turned"), half + 1)
                act.activation(sq[:, 2 * half:2 * half + 2, :], bank2(half), ACT.Copy).then_inc(sem("out_rows_act"), 1)

        @block.vector
        def _(dve):
            done = [0]
            steps = [0]

            def split(upto):
                while done[0] <= min(upto, n_chunks - 1):
                    c = done[0]
                    dve.wait_ge(hi_split, c + 1)
                    dve.tensor_tensor(split_view(w_lo, c), split_view(raw, c), split_view(w_hi, c).bitcast(F32), ALU.subtract)\
                       .then_inc(lo_split, 1)
                    done[0] += 1

            def link(ins):
                steps[0] += 1
                ins.then_inc(sem("dve_link"), 1)
                dve.wait_ge(sem("dve_link"), steps[0])

            def resid(name, which):
                if name in ("ln1", "ln3"):
                    dve.wait_ge(sem("ffn0_hid_lo" if name == "ln1" else "ffn1_hid_lo"), NF)
                for q in range(4):
                    wait_acc(dve, which, q)
                    dve.scalar_tensor_tensor(out=r[:, 2 * q:2 * q + 2, :], in0=x[:, 2 * q:2 * q + 2, :], scalar=ALPHA,
                                             in1=bank2(q), op0=ALU.mult, op1=ALU.add).then_inc(sem("norm_resid"), 1)
                    if q % 2:
                        fold_resid(name, q // 2)

            def fold_resid(name, q):
                dve.wait_ge(*norm(name, "resid", 2 * q + 2))
                dve.tensor_tensor(hid[:, q, :, :], r[:, 4 * q:4 * q + 2, :], r[:, 4 * q + 2:4 * q + 4, :], ALU.add)\
                   .then_inc(sem("norm_folded"), 1)

            def fold_squares(name):
                done_ = 2 if name in LNS else 0
                for q in range(1, 4):
                    dve.wait_ge(*norm(name, "sq", q + 1))
                    if q > 1:
                        dve.wait_ge(*norm(name, "folded", done_ + q - 1))
                    dve.tensor_tensor(hid[:, 2, :, :], sq[:, 0:2, :] if q == 1 else hid[:, 2, :, :],
                                      sq[:, 2 * q:2 * q + 2, :], ALU.add).then_inc(sem("norm_folded"), 1)

            def take_acc(name, which):
                for q in range(4):
                    wait_acc(dve, which, q)
                    dve.tensor_copy(r[:, 2 * q:2 * q + 2, :], bank2(q)).then_inc(sem(f"{name}_taken"), 1)

            def inverse_std(name):
                if name in LNS:
                    dve.wait_ge(*norm(name, "var", 1))
                    dve.tensor_scalar(moments[:, 0:4], PS[:, 5, 0:4], 1.0 / D, None, ALU.mult).then_inc(sem("norm_small"), 1)
                    dve.wait_ge(*norm(name, "small", 1))
                    dve.scalar_tensor_tensor(out=moments[:, 4:6], in0=moments[:, 0:2], scalar=-1.0, in1=moments[:, 0:2],
                                             op0=ALU.mult, op1=ALU.mult).then_inc(sem("norm_small"), 1)
                    dve.wait_ge(*norm(name, "small", 2))
                    dve.tensor_tensor(moments[:, 2:4], moments[:, 2:4], moments[:, 4:6], ALU.add).then_inc(sem("norm_small"), 1)
                    dve.wait_ge(*norm(name, "small", 3))
                    dve.tensor_scalar(moments[:, 2:4], moments[:, 2:4], 0.0, None, ALU.max).then_inc(sem("norm_small"), 1)
                dve.wait_ge(*norm(name, "std", 1))
                if name in LNS:
                    link(dve.reciprocal(rstd[:, 0:2], std[:, :]))
                    dve.tensor_tensor(rstd[:, 2:4], rstd[:, 0:2], moments[:, 0:2], ALU.mult).then_inc(sem("norm_rcp"), 1)
                else:
                    dve.reciprocal(rstd[:, 0:2], std[:, :]).then_inc(sem("norm_rcp"), 1)

            def scale_pair(name, q, src, dst, bank=6):
                two = slice(2 * q, 2 * q + 2)
                ins = dve.tensor_tensor(dst[:, two, :], src[:, two, :], PS[:, bank:bank + 1, 0:S].to_broadcast([P, 2, S]),
                                        ALU.mult)
                if name in LNS:
                    ins.then_inc(sem("norm_scaled_r"), 1)
                    dve.wait_ge(*norm(name, "scaled_r", q + 1))
                    ins = dve.tensor_tensor(dst[:, two, :], dst[:, two, :],
                                            PS[:, bank:bank + 1, S:2 * S].to_broadcast([P, 2, S]), ALU.subtract)
                ins.then_inc(sem("norm_scaled"), 1)

            def modulation(part):
                lo_, hi_, done_ = ((0, 16, 2), (16, 24, 2), (24, 40, 4), (40, 48, 4))[part]
                dve.wait_ge(sem("mod_done"), done_)
                link(dve.tensor_tensor(mod[:, lo_:hi_], PS[:, 7, lo_:hi_], vecs[:, 2, lo_:hi_], ALU.add))
                g, weight = slice(8 * part, 8 * part + 8), vecs[:, 1, 18 + 8 * part:26 + 8 * part]
                if part % 2 == 0:
                    ins = dve.scalar_tensor_tensor(out=gain[:, g], in0=mod[:, hi_ - 8:hi_], scalar=1.0, in1=weight,
                                                   op0=ALU.add, op1=ALU.mult)
                else:
                    ins = dve.tensor_tensor(gain[:, g], mod[:, lo_:hi_], weight, ALU.mult)
                ins.then_inc(sem("mod_evac"), 1)

            def operand(name, src, full, hi, lo, gains, biases, t=KT, scaled_src=None, bank=6, upto=None, part=None):
                if name not in LNS:
                    fold_squares(name)
                inverse_std(name)
                if upto is not None:
                    split(upto)
                if part is not None:
                    modulation(part)
                    dve.wait_ge(sem("mod_evac"), part + 1)
                dve.wait_ge(*norm(name, "rb", 1))
                operand_tail(name, src, full, hi, lo, gains, biases, t, scaled_src, bank)

            def operand_tail(name, src, full, hi, lo, gains, biases, t=KT, scaled_src=None, bank=6):
                n = t // 2

                def low(q):
                    dve.wait_ge(*norm(name, "full", q + 1))
                    dve.wait_ge(*norm(name, "hi", 2 * q + 2))
                    dve.tensor_tensor(lo[:, 2 * q:2 * q + 2, :], full[:, 2 * q:2 * q + 2, :],
                                      hi[:, 2 * q:2 * q + 2, :].bitcast(F32), ALU.subtract).then_inc(sem("norm_lo"), 1)

                for q in range(n):
                    scale_pair(name, q, scaled_src if scaled_src is not None else src, src, bank)
                    if q >= 2:
                        low(q - 1)
                    dve.wait_ge(*norm(name, "scaled", q + 1))
                    for k in (2 * q, 2 * q + 1):
                        if biases:
                            ins = dve.tensor_scalar(full[:, k, :], src[:, k, :], gains(k), biases(k), ALU.mult, ALU.add)
                        else:
                            ins = dve.tensor_scalar(full[:, k, :], src[:, k, :], gains(k), None, ALU.mult)
                    ins.then_inc(sem("norm_full"), 1)
                    if q == 0:
                        low(0)
                if n > 1:
                    low(n - 1)

            def layer_norm(name, which, following):
                g, b = LNS[name]
                split(first[following] + 1)
                resid(name, which)
                fold_squares(name)
                if name != "ln3":
                    operand(name, r, x, x_hi, x_lo, lambda k: vec(0, g + k), lambda k: vec(0, b + k),
                            upto=first[following] + 2)
                    return
                inverse_std(name)
                split(first[following] + 2)
                dve.wait_ge(*norm(name, "rb", 1))
                for q in range(4):
                    scale_pair(name, q, r, r)
                    dve.wait_ge(*norm(name, "scaled", q + 1))
                    for k in (2 * q, 2 * q + 1):
                        ins = dve.tensor_scalar(x[:, k, :], r[:, k, :], vec(0, g + k), vec(0, b + k), ALU.mult, ALU.add)
                    ins.then_inc(sem("ln3_x"), 1)

            def ffn(name, base):
                for i in range(NF):
                    g = base if i == 0 else base + 2 + 3 * (i - 1)
                    ada = list(range(ADA_N * i // (NF - 1), ADA_N * (i + 1) // (NF - 1))) if name == "ffn1" and i < NF - 1 else []
                    if ada and i == 0:
                        dve.wait_ge(sem("silu_c_ready"), 1)
                    split(g + 2)
                    if len(ada) > 2:
                        ada_step(dve, ada.pop(0))
                    split(g + 3)
                    dve.wait_ge(sem(f"{name}_silu"), i + 1)
                    dve.wait_ge(chunk_used, g + 2)
                    dve.tensor_tensor(hid[:, i % 2, :, :], gate_s[:, i % 2, :, :], bank2(5 + 2 * (i % 2)), ALU.mult)\
                       .then_inc(sem(f"{name}_hid"), 1)
                    dve.wait_ge(sem(f"{name}_hid_hi"), i + 1)
                    dve.tensor_tensor(hid_lo[:, i % 2, :, :], hid[:, i % 2, :, :], hid_hi[:, i % 2, :, :].bitcast(F32),
                                      ALU.subtract).then_inc(sem(f"{name}_hid_lo"), 1)
                    if ada:
                        ada_step(dve, ada.pop(0))
                    if i < NF - 1:
                        split(g + 4 if i else g + 3)
                    for n in ada:
                        ada_step(dve, n)
            dve.memset(eps_sb[:, 0:1], LN_EPS)
            dve.memset(eps_sb[:, 1:2], RMS_EPS).then_inc(sem("eps_set"), 1)
            dve.memset(conv_in[:, :, :, 0:3], 0.0).then_inc(sem("conv_pad"), 1)
            for b in range(4):
                dve.wait_ge(sem("x_turned"), b + 1)
                dve.wait_ge(sem("x_hi_ready"), b + 1)
                dve.tensor_tensor(x_lo[:, 2 * b:2 * b + 2, :], bank2(b), x_hi[:, 2 * b:2 * b + 2, :].bitcast(F32),
                                  ALU.subtract).then_inc(sem("x_lo_ready"), 1)
            split(0)
            for b in range(4):
                dve.tensor_copy(x[:, 2 * b:2 * b + 2, :], bank2(b)).then_inc(sem("x_ready"), 1)
                if b == 1:
                    split(1)
            split(2)
            base = first["even"]
            dve.wait_ge(chunk_used, base + 1)
            dve.wait_ge(sem("heads_landed"), 16 * 5)
            dve.tensor_scalar(small[:, 0, :], PS[0:16, 4, 0:S], head_vec[:, 0:1], None, ALU.add).then_inc(sem("dt_raw"), 1)
            split(3)
            dve.wait_ge(sem("vecs_turned"), 1)
            dve.tensor_copy(vecs[:, 0, 0:124], PS[:, 7, 0:124])
            dve.tensor_copy(vecs[:, 1, 0:74], PS[:, 7, P:P + 74])
            dve.tensor_copy(vecs[:, 2, 0:56], PS[:, 7, 2 * P:2 * P + 56]).then_inc(sem("vecs_ready"), 1)
            dve.wait_ge(sem("dt_act"), 3)
            dve.wait_ge(sem("a_ready"), 1)
            dve.wait_ge(sem("dt_raw"), 1)
            link(dve.scalar_tensor_tensor(out=small[:, 0, :], in0=small[:, 0, :], scalar=0.0, in1=small[:, 2, :],
                                          op0=ALU.max, op1=ALU.add))
            dve.tensor_scalar(small[:, 1, :], small[:, 0, :], head_vec[:, 2:3], -1.0, ALU.mult, ALU.mult)\
               .then_inc(sem("da_ready"), 1)
            dve.wait_ge(sem("vecs_ready"), 1)

            def even_proj(p):
                split(base + p + 2)
                if p > 6:
                    return
                t0 = 8 + 2 * (p - 1) if p <= 2 else 2 * (p - 3)
                dve.wait_ge(sem("even_evac"), p)
                if p >= 3:
                    dve.wait_ge(sem("xbc_ready"), p - 2)
                for j in range(4):
                    for q in range(2):
                        w, src, dst = vec(0, 12 * j + t0 + q), conv_in[:, p % 2, q, j:j + S], conv_acc[:, p % 2, q, :]
                        if j == 0:
                            ins = dve.tensor_scalar(dst, src, w, vec(0, 48 + t0 + q), ALU.mult, ALU.add)
                        else:
                            ins = dve.scalar_tensor_tensor(out=dst, in0=src, scalar=w, in1=dst, op0=ALU.mult, op1=ALU.add)
                    if j < 3:
                        link(ins)
                    else:
                        ins.then_inc(sem("conv_done"), 1)

            def even_small(_):
                dve.wait_ge(sem("tok_turned"), 1)
                dve.tensor_copy(tok[:, :, :], PS[:, 0, 0:64].rearrange("p (j c) -> p j c", j=2)).then_inc(sem("tok_ready"), 1)
                dve.wait_ge(sem("cb_done"), 1)
                dve.tensor_copy(cb[:, :, :], PS[:, 2, :].rearrange("p (q s) -> p q s", q=4)).then_inc(sem("cb_ready"), 1)

            def by_head(t, n=8):
                return t.rearrange("p (h o) -> p h o", o=1).to_broadcast([P, n, 64])

            def even_head(j):
                if j == 0:
                    dve.wait_ge(sem("acs_done"), 1)
                    dve.tensor_scalar(neg_acs[:, :, :], PS[:, 0, 64:96].rearrange("p (j c) -> p j c", j=2), -1.0, None,
                                      ALU.mult).then_inc(sem("acs_ready"), 1)
                    dve.wait_ge(sem("acs_ready"), 1)
                    dve.tensor_tensor(decay[:, 0, :], neg_acs[:, 0, :], PS[:, 0, 96:112], ALU.add).then_inc(sem("acs_ready"), 1)
                    dve.wait_ge(sem("tok_ready"), 1)
                dve.wait_ge(sem("xtok_done"), j + 1)
                if j:
                    dve.wait_ge(sem("y_done"), 8)
                for g in range(2):
                    dve.tensor_tensor(x_dt[:, g * 512:(g + 1) * 512].rearrange("p (h e) -> p h e", h=8),
                                      PS[:, 4 + g, :].rearrange("p (h e) -> p h e", h=8),
                                      by_head(tok[:, j, 8 * g:8 * g + 8]), ALU.mult).then_inc(sem("xdt_ready"), 1)
                if j == 0:
                    dve.wait_ge(sem("decay_ready"), 1)
                    dve.wait_ge(sem("xdt_ready"), 2)
                    dve.tensor_tensor(x_dec.rearrange("p (h e) -> p h e", h=16), x_dt.rearrange("p (h e) -> p h e", h=16),
                                      by_head(decay[:, 1, :], 16), ALU.mult).then_inc(sem("xdec_ready"), 1)

            def even_pool(i):
                two = slice(2 * i, 2 * i + 2)
                dve.wait_ge(sem("pool_hi_ready"), i + 1)
                dve.tensor_tensor(pool_lo[:, two, :], pool_y[:, two, :], pool_hi[:, two, :].bitcast(F32), ALU.subtract)\
                   .then_inc(sem("pool_lo_ready"), 1)

            def even_bcast(j):
                for q in range(4):
                    dve.wait_ge(sem("acs_bcast"), 4 * j + q + 1)
                    if 4 * j + q:
                        dve.wait_ge(sem("exp_done"), 4 * j + q)
                    dve.tensor_tensor(seg.rearrange("p (h s) -> p h s", h=4), PS[:, q, :].rearrange("p (h s) -> p h s", h=4),
                                      cst("ssm_mask").rearrange("p (o s) -> p o s", o=1).to_broadcast([P, 4, P]), ALU.add)\
                       .then_inc(sem("seg_done"), 1)
                for g in range(2):
                    dve.wait_ge(sem("exp_done"), 4 * j + 2 * g + 2)
                    if g == 0:
                        dve.wait_ge(sem("cb_ready"), 1)
                    dve.tensor_tensor(lmat[:, 8 * g:8 * g + 8, :], lmat[:, 8 * g:8 * g + 8, :],
                                      cb[:, 2 * j + g:2 * j + g + 1, :].to_broadcast([P, 8, P]), ALU.mult)\
                       .then_inc(sem("lmat_ready"), 1)
                if j:
                    even_pool(0)
                    for g in range(2):
                        dve.wait_ge(sem("eacs_done"), 2 * g + 2)
                        dve.tensor_tensor(e_acs[:, 8 * g:8 * g + 8, :], e_acs[:, 8 * g:8 * g + 8, :],
                                          xbc[:, 10 + g:11 + g, P:S].to_broadcast([P, 8, P]), ALU.mult)\
                           .then_inc(sem("cdec_ready"), 1)

            def even_y(j):
                for k in range(KT):
                    dve.wait_ge(sem("y_done"), 8 * j + 4 * (k // 4) + 4)
                    dve.scalar_tensor_tensor(out=r[:, k, j * P:(j + 1) * P], in0=xbc[:, k, j * P:(j + 1) * P],
                                             scalar=d_skip[:, k:k + 1], in1=PS[:, 4 + k // 4, (k % 4) * P:(k % 4) * P + P],
                                             op0=ALU.mult, op1=ALU.add).then_inc(sem("y_ready"), 1)

            even_proj(1)
            for step, arg in EVEN_STEPS:
                {"proj": even_proj, "small": even_small, "head": even_head, "bcast": even_bcast,
                 "state": lambda _: None, "y": even_y, "pool": lambda i: even_pool(1) if i else None}[step](arg)
            dve.wait_ge(sem("y_ready"), 16)
            dve.wait_ge(sem("even_evac"), 12)
            for q in range(4):
                dve.tensor_tensor(r[:, 2 * q:2 * q + 2, :], r[:, 2 * q:2 * q + 2, :], z_silu[:, 2 * q:2 * q + 2, :], ALU.mult)\
                   .then_inc(sem("gated"), 1)
            split(first["even_out"] + 2)
            dve.wait_ge(sem("gated"), 4)
            operand("ssm", r, sq, x_hi, x_lo, lambda k: vec(1, 4 + k), None)
            layer_norm("ln0", "even_out", "ffn0")
            if not on("ffn0"):
                return
            ffn("ffn0", first["ffn0"])
            layer_norm("ln1", "ffn0", "odd")
            if not on("odd"):
                return
            base = first["odd"]
            dve.memset(neg_f[:, :], 0.0)
            dve.memset(qz[:, :, :], 0.0).then_inc(sem("qz_zero"), 1)
            dve.wait_ge(sem("fg_act"), 3)
            dve.wait_ge(sem("qz_zero"), 1)
            link(dve.tensor_scalar(small[0:8, 2, :], small[0:8, 0, :], -1.0, 0.0, ALU.mult, ALU.max))
            link(dve.tensor_tensor(small[0:8, 3, :], small[0:8, 2, :], small[0:8, 1, :], ALU.add))
            dve.tensor_tensor_scan(neg_f[0:8, :], small[0:8, 3, :], small[0:8, 3, :], 0.0, ALU.add, ALU.bypass)\
               .then_inc(sem("neg_f_ready"), 1)

            def qn_sum(_):
                inverse_std("qn")

            def qn_out(_):
                dve.wait_ge(*norm("qn", "rb", 1))
                operand_tail("qn", cq, r, cq_hi, cq_lo, lambda k: vec(1, 12 + k), None, 4, bank=7)

            def kvn_sum(_):
                inverse_std("kvn")

            def kvn_out(_):
                dve.wait_ge(*norm("kvn", "rb", 1))
                dve.wait_ge(*norm("qn", "lo", 2))
                operand_tail("kvn", ckv, r, ckv_hi, ckv_lo, lambda k: vec(1, 16 + k), None, 2, bank=7)

            def swap_fills(_):
                cos, sin = cst("cos", 96), cst("sin", 96)
                rr = slice(ROPE_ROW, 96)
                scratch = r[rr, 4:6, :]

                def both(t):
                    return t[rr, :].rearrange("p (o s) -> p o s", o=1).to_broadcast([32, 2, S])

                wait_fill(dve, 21)
                link(dve.tensor_tensor(kr[rr, 1, :], PS[rr, 4 + 21 % 3, 0:S], sin[rr, :], ALU.mult))
                link(dve.tensor_tensor(kr[rr, 0, :], kr[rr, 0, :], cos[rr, :], ALU.mult))
                link(dve.tensor_tensor(kr[rr, 0, :], kr[rr, 0, :], kr[rr, 1, :], ALU.add))
                dve.tensor_copy(km[rr, :, :], kr[rr, 0:1, :].to_broadcast([32, MLA_H, S])).then_inc(sem("kr_rot"), 1)
                for q in range(4):
                    wait_fill(dve, 22 + q)
                    two = slice(2 * q, 2 * q + 2)
                    if q:
                        dve.wait_ge(sem("qm_rot"), q)
                    dve.tensor_tensor(scratch, bank2(4 + (22 + q) % 3)[rr], both(sin), ALU.mult)
                    link(dve.tensor_tensor(qm[rr, two, :], qm[rr, two, :], both(cos), ALU.mult))
                    dve.tensor_tensor(qm[rr, two, :], qm[rr, two, :], scratch, ALU.add).then_inc(sem("qm_rot"), 1)
                split(base + 16)

            def masked(a):
                dve.wait_ge(sem("scored"), a + 1)
                b = a % 2
                if a >= 2:
                    dve.wait_ge(sem("exped"), 2 * a - 2)
                for j, kw, o in ((0, P, 0), (1, S, P)):
                    dve.tensor_tensor_reduce(out=sc_sb[:, b, o:o + kw], in0=PS[:, b, o:o + kw], in1=cst("attn_mask")[:, o:o + kw],
                                             scale=1.0, scalar=-3e38, op0=ALU.add, op1=ALU.max,
                                             accum_out=row_max[:, b, j:j + 1]).then_inc(sem("masked"), 1)
                dve.wait_ge(sem("masked"), 2 * a + 2)
                dve.tensor_scalar(row_max[:, b, :], row_max[:, b, :], -1.0, None, ALU.mult).then_inc(sem("neg_max"), 1)

            def normalised(a):
                b = a % 2
                dve.wait_ge(sem("exped"), 2 * a + 2)
                link(dve.reciprocal(row_sum[:, b, :], row_sum[:, b, :]))
                for j, kw, o in ((0, P, 0), (1, S, P)):
                    dve.tensor_scalar(prob[:, b, o:o + kw], prob[:, b, o:o + kw], row_sum[:, b, j:j + 1], None, ALU.mult)\
                       .then_inc(sem("prob_ready"), 1)

            def o_low(pair):
                dve.wait_ge(sem("o_hi"), pair + 1)
                dve.tensor_tensor(x_lo[:, pair, :], PS[:, 3, 0:S], x_hi[:, pair, :].bitcast(F32), ALU.subtract)\
                   .then_inc(sem("o_lo"), 1)

            def attention(a):
                if a < 16:
                    masked(a)
                    normalised(a)
                if a >= 3 and a % 2:
                    o_low((a - 3) // 2)

            for step, arg in ODD_STEPS:
                {"proj": lambda p: split(base + p + 2), "att": attention, "qn_sum": qn_sum, "qn_out": qn_out,
                 "kvn_sum": kvn_sum, "kvn_out": kvn_out, "uq": lambda c: split(base + 13), "km": lambda _: None,
                 "vm": lambda _: None, "swap": swap_fills}[step](arg)
            split(first["odd_out"] + 3)
            layer_norm("ln2", "odd_out", "ffn1")
            if not on("ffn1"):
                return
            ffn("ffn1", first["ffn1"])
            layer_norm("ln3", "ffn1", "sc")
            if not on("sc"):
                return
            dve.wait_ge(sem("ln3_x"), 4)
            operand("pre", r, sq, x_hi, x_lo, lambda k: gain[:, k:k + 1], lambda k: mod[:, k:k + 1], scaled_src=x, part=0)
            modulation(1)
            dve.memset(cv[:, :, :, 0:1], 0.0)
            link(dve.memset(cv[:, :, :, 1 + S:2 + S], 0.0))
            c, f = first["sc"], 0
            for q in range(4):
                i = q % 2
                split(c + 3)
                dve.wait_ge(sem("sc_evac_c"), q + 1)
                dve.wait_ge(chunk_used, c + 2)
                dve.tensor_tensor(cv[:, i, :, 1:1 + S], c_sb[:, i, :, :], bank2(4 + (f + 1) % 4), ALU.mult)\
                   .then_inc(sem("cv_ready"), 1)
                dve.wait_ge(sem("cv_ready"), q + 1)
                split(c + 4)
                for j in range(3):
                    for e in range(2):
                        w, src, dst = vec(1, 50 + 8 * j + 2 * q + e), cv[:, i, e, j:j + S], cv_acc[:, i, e, :]
                        if j == 0:
                            ins = dve.tensor_scalar(dst, src, w, None, ALU.mult)
                        else:
                            ins = dve.scalar_tensor_tensor(out=dst, in0=src, scalar=w, in1=dst, op0=ALU.mult, op1=ALU.add)
                    link(ins)
                dve.wait_ge(sem("sc_evac_b"), q + 1)
                dve.tensor_tensor(hid[:, i, :, :], cv_acc[:, i, :, :], b_sb[:, i, :, :], ALU.mult).then_inc(sem("sc_y"), 1)
                dve.wait_ge(sem("sc_hi"), q + 1)
                dve.tensor_tensor(hid_lo[:, i, :, :], hid[:, i, :, :], hid_hi[:, i, :, :].bitcast(F32), ALU.subtract)\
                   .then_inc(sem("sc_lo"), 1)
                c, f = c + (4 if q else 3), f + 3
                split(c + 1)
            split(first["mlp"] + 1)

            def add_post(norm_name, which, name, g0, upto=None):
                dve.wait_ge(*((sem("sc_lo"), 4) if name == "post_x" else (sem("mlp_lo"), NM)))
                take_acc(norm_name, which)
                fold_squares(norm_name)
                inverse_std(norm_name)
                if upto is not None:
                    split(upto)
                dve.wait_ge(*norm(norm_name, "rb", 1))
                dve.wait_ge(sem("mod_evac"), 2 if name == "post_x" else 4)
                for q in range(4):
                    scale_pair(norm_name, q, r, r)
                    dve.wait_ge(*norm(norm_name, "scaled", q + 1))
                    for k in (2 * q, 2 * q + 1):
                        ins = dve.scalar_tensor_tensor(out=x[:, k, :], in0=r[:, k, :], scalar=gain[:, g0 + k:g0 + k + 1],
                                                       in1=x[:, k, :], op0=ALU.mult, op1=ALU.add)
                        if name == "final_x" or k % 2:
                            ins.then_inc(sem(name), 1)

            add_post("post", "sc", "post_x", 8, upto=first["mlp"] + 2)
            dve.wait_ge(sem("post_x"), 4)
            operand("preff", r, sq, x_hi, x_lo, lambda k: gain[:, 16 + k:17 + k], lambda k: mod[:, 24 + k:25 + k],
                    scaled_src=x, part=2)
            modulation(3)
            if not on("mlp"):
                return
            base = first["mlp"]
            for i in range(NM):
                c = base if i == 0 else base + 1 + 2 * (i - 1)
                split(c + 2)
                dve.wait_ge(sem("mlp_relu"), i + 1)
                dve.tensor_tensor(hid[:, i % 3, :, :], gate_s[:, i % 2, :, :], gate_s[:, i % 2, :, :], ALU.mult)\
                   .then_inc(sem("mlp_hid"), 1)
                dve.wait_ge(sem("mlp_hi"), i + 1)
                dve.tensor_tensor(hid_lo[:, i % 3, :, :], hid[:, i % 3, :, :], hid_hi[:, i % 3, :, :].bitcast(F32),
                                  ALU.subtract).then_inc(sem("mlp_lo"), 1)
                split(c + 3)
            split(n_chunks)
            add_post("postff", "mlp", "final_x", 24)
            for half in range(2):
                dve.wait_ge(sem("out_turned"), half + 1)
                dve.tensor_copy(sq[:, 4 + 2 * half:6 + 2 * half, :], bank2(2 + half)).then_inc(sem("out_rows_dve"), 1)


_INS = ["x", "even_w_in", "pool_w", "pool_scale", "conv_w", "conv_b", "dt_bias", "a_log", "d_skip", "ssm_norm_w",
        "even_w_out", "odd_w_in", "fgate_b", "q_norm_w", "w_uq", "kv_norm_w", "w_ukv", "odd_w_out", "ffn_w_gate",
        "ffn_w_up", "ffn_w_down", "ln_mix_g", "ln_mix_b", "ln_ffn_g", "ln_ffn_b", "c_2", "ada_w_2", "ada_b_2",
        "norm_gains_2", "mlp_w_in_2", "mlp_w_out_2", "sc_w_in_2", "sc_conv_2", "sc_w_out_2"]


def kernel(**inputs):
    import concourse.bacc as bacc
    from concourse.bass_utils import run_bass_kernel_spmd

    nc = bacc.Bacc("TRN2", target_bir_lowering=False, num_devices=1)
    arrays = {name: np.ascontiguousarray(inputs[name]) for name in _INS}
    arrays["consts"] = shape_constants()
    aps = {n: nc.dram_tensor(n, a.shape, mybir.dt.from_np(a.dtype), kind="ExternalInput").ap() for n, a in arrays.items()}
    out = nc.dram_tensor("out", (1, S, D), F32, kind="ExternalOutput").ap()
    build(nc, aps, out)
    result = run_bass_kernel_spmd(nc, [arrays], core_ids=[0])
    return result.results[0]["out"]
```

```python
from contextlib import ExitStack

import numpy as np
import concourse.bass as bass
from concourse import mybir

F32 = mybir.dt.float32
F32R = mybir.dt.float32r
ALU = mybir.AluOpType
ACT = mybir.ActivationFunctionType

P = 128
S = 256
D = 1024
KT = D // P
CH = 2048
RING = 3
HEADS = 16
FOX_H = 8
MLA_H = 8
D_FF = 2816
D_FF2 = 4096
ALPHA = (2 * 2) ** 0.25
LN_EPS = 1e-5
RMS_EPS = 1e-6
NEG = -1e30

CONST_COLS = {}
_at = 0
for _n, _w in (("ident", 128), ("triu", 128), ("attn_mask", 384), ("ssm_mask", 128), ("cos", 256), ("sin", 256),
               ("swap", 96), ("inv_count", 64)):
    CONST_COLS[_n] = (_at, _w)
    _at += _w
CONST_W = _at
ROPE_ROW = 64


def shape_constants():
    c = np.zeros((P, CONST_W), np.float32)

    def put(name, a):
        o, w = CONST_COLS[name]
        c[:a.shape[0], o:o + w] = a

    i, j = np.arange(P)[:, None], np.arange(P)[None, :]
    put("ident", (i == j).astype(np.float32))
    put("triu", (i <= j).astype(np.float32))
    causal = np.where(j <= i, 0, NEG).astype(np.float32)
    put("attn_mask", np.concatenate([causal, np.zeros((P, P), np.float32), causal], 1))
    put("ssm_mask", np.where(i <= j, 0, NEG).astype(np.float32))
    half = 16
    freqs = np.power(np.float32(10000.0), -np.arange(half, dtype=np.float32) / np.float32(half)).astype(np.float32)
    ang = (freqs[:, None] * np.arange(S, dtype=np.float32)[None, :]).astype(np.float32)
    cos, sin = np.ones((96, S), np.float32), np.zeros((96, S), np.float32)
    cos[64:80] = cos[80:96] = np.cos(ang)
    sin[64:80], sin[80:96] = -np.sin(ang), np.sin(ang)
    put("cos", cos)
    put("sin", sin)
    swap = np.zeros((96, 96), np.float32)
    for r in range(half):
        swap[ROPE_ROW + half + r, ROPE_ROW + r] = swap[ROPE_ROW + r, ROPE_ROW + half + r] = 1
    put("swap", swap)
    t = np.arange(16)
    put("inv_count", np.tile(np.concatenate([1 / np.minimum(t + 1, w) for w in (2, 4, 8, 16)])[None], (P, 1)).astype(np.float32))
    return c


def build(nc, A, out, stop=None):
    ctx = ExitStack()
    with ctx:
        def sb(name, shape, dt=F32, stack=ctx):
            return stack.enter_context(nc.sbuf_tensor(name, shape, dt))

        sems = {}

        def sem(name):
            if name not in sems:
                sems[name] = ctx.enter_context(nc.semaphore(name))
            return sems[name]

        raw = sb("raw", [P, RING, CH])
        w_hi = sb("w_hi", [P, RING, CH], F32R)
        w_lo = sb("w_lo", [P, RING, CH], F32R)
        x = sb("x_res", [P, KT, S])
        x_hi = sb("x_hi", [P, KT, S], F32R)
        x_lo = sb("x_lo", [P, KT, S], F32R)
        r = sb("r", [P, KT, S])
        sq = sb("sq", [P, KT, S])
        const = sb("const", [P, CONST_W])
        vecs = sb("vecs", [P, 3, P])
        ones = sb("ones", [P, P])
        d_skip = sb("d_skip_sb", [P, KT])
        head_vec = sb("head_vec", [16, 4])
        std = sb("std", [P, 2])
        eps_sb = sb("eps_sb", [P, 2])
        table_sb = sb("table_sb", [P, 22])
        rstd = sb("rstd", [P, 4])
        moments = sb("moments", [P, 6])
        mod = sb("mod", [P, 48])
        gain = sb("gain", [P, 32])
        silu_c = sb("silu_c", [P, KT])
        small = sb("small", [16, 4, S])
        hid = sb("hid", [P, 3, 2, S])
        gate_s = sb("gate_s", [P, 2, 2, S])
        hid_hi = sb("hid_hi", [P, 3, 2, S], F32R)
        hid_lo = sb("hid_lo", [P, 3, 2, S], F32R)

        with ExitStack() as even:
            pool_hi = sb("pool_hi", [P, 4, S], F32R, even)
            pool_lo = sb("pool_lo", [P, 4, S], F32R, even)
            pool_y = sb("pool_y", [P, 4, S], F32, even)
            u_pad = sb("u_pad", [P, 4, 16 + S], F32, even)
            wins = sb("wins", [P, 2, 4, 16 + S], F32, even)
            z_silu = sb("z_silu", [P, KT, S], F32, even)
            conv_in = sb("conv_in", [P, 2, 2, 3 + S], F32, even)
            conv_acc = sb("conv_acc", [P, 2, 2, S], F32, even)
            xbc = sb("xbc", [P, 12, S], F32, even)
            tok = sb("tok", [P, 2, 32], F32, even)
            neg_acs = sb("neg_acs", [P, 2, 16], F32, even)
            decay = sb("decay", [P, 2, 16], F32, even)
            b_tok = sb("b_tok", [P, 2 * P], F32, even)
            cb = sb("cb", [P, 4, P], F32, even)
            state = sb("state", [P, D], F32, even)
        win_a, win_b = wins[:, 0, :, :], wins[:, 1, :, :]
        e_acs = wins[:, :, :, :].rearrange("p a g s -> p (a g s)")[:, 0:HEADS * P].rearrange("p (h s) -> p h s", h=HEADS)
        x_dt = hid[:, 0:2, :, :].rearrange("p a b s -> p (a b s)")
        x_dec = gate_s[:, :, :, :].rearrange("p a b s -> p (a b s)")
        seg = hid[:, 2, :, :].rearrange("p b s -> p (b s)")
        lmat = sq[:, :, :].rearrange("p k (a s) -> p (k a) s", a=2)
        rows = [sb(f"vec_rows{i}", [P, P]) for i in range(3)]
        pool_w_sb = sb("pool_w_sb", [P, 4, P])

        with ExitStack() as odd:
            qz = sb("qz", [P, FOX_H, S], F32, odd)
            kf = sb("kf", [P, 4, S], F32, odd)
            v_tok = sb("v_tok", [P, 2, 512], F32, odd)
            neg_f = sb("neg_f", [P, S], F32, odd)
            cq = sb("cq", [P, 4, S], F32, odd)
            cq_hi = sb("cq_hi", [P, 4, S], F32R, odd)
            cq_lo = sb("cq_lo", [P, 4, S], F32R, odd)
            ckv = sb("ckv", [P, 2, S], F32, odd)
            ckv_hi = sb("ckv_hi", [P, 2, S], F32R, odd)
            ckv_lo = sb("ckv_lo", [P, 2, S], F32R, odd)
            qm = sb("qm", [96, MLA_H, S], F32, odd)
            km = sb("km", [96, MLA_H, S], F32, odd)
            kr = sb("kr", [96, 2, S], F32, odd)
            vm_tok = sb("vm_tok", [P, 2, 512], F32, odd)
            row_max = sb("row_max", [P, 2, 2], F32, odd)
            row_sum = sb("row_sum", [P, 2, 2], F32, odd)

        kr_cos, kr_rot = x_dec[:, 768:1024], kr[:, 1, :]
        relu_s = r[:, 0:6, :].rearrange("p (a b) s -> p a b s", a=3)
        hid_flat = hid[:, :, :, :].rearrange("p a b s -> p (a b s)")
        prob = hid_flat[:, 0:768].rearrange("p (a n) -> p a n", a=2)
        prob_t = hid_flat[:, 768:1536].rearrange("p (a n) -> p a n", a=2)
        sc_sb = x_dec[:, 0:768].rearrange("p (a n) -> p a n", a=2)

        with ExitStack() as conv2:
            ada_raw = sb("ada_raw", [P, 2, CH], F32, conv2)
            ada_acc = sb("ada_acc", [P, 3, CH], F32, conv2)
            c_sb = sb("c_sb", [P, 2, 2, S], F32, conv2)
            b_sb = sb("b_sb", [P, 2, 2, S], F32, conv2)
            cv = sb("cv", [P, 2, 2, 1 + S + 1], F32, conv2)
            cv_acc = sb("cv_acc", [P, 2, 2, S], F32, conv2)

        def cst(name, rows_=P):
            o, w = CONST_COLS[name]
            return const[0:rows_, o:o + w]

        ident, triu = cst("ident"), cst("triu")

        def vec(t, c):
            return vecs[:, t, c:c + 1]

        PS = ctx.enter_context(nc.psum_tensor("PS", [P, 8, 512], F32))

        def bank2(b):
            return PS[:, b, :].rearrange("p (a s) -> p a s", a=2)

        chunks = []
        first = {}

        def col_chunk(w, k, c0, n, copies=1):
            chunks.append((w[0:k * P, c0:c0 + n].rearrange("(k p) n -> p k n", p=P), k, n, copies))

        def row_chunk(w, r0):
            chunks.append((w[r0:r0 + 2 * P, :].rearrange("(k p) n -> p k n", p=P), 2, D, 1))

        E_IN, O_IN = A["even_w_in"][0], A["odd_w_in"][0]
        XBC0, DT0 = 512 + 1024, 512 + 1024 + 1536
        first["even"] = len(chunks)
        col_chunk(E_IN, 8, DT0, 16, 8)
        for c in (XBC0 + 1024, XBC0 + 1280, XBC0, XBC0 + 256, XBC0 + 512, XBC0 + 768, 0, 256, 512, 768, 1024, 1280):
            col_chunk(E_IN, 8, c, 256)
        first["even_out"] = len(chunks)
        for q in range(6):
            row_chunk(A["even_w_out"][0], 2 * P * q)

        def ffn_chunks(name, gate, up, down, n):
            first[name] = len(chunks)
            col_chunk(gate, 8, 0, 256)
            col_chunk(up, 8, 0, 256)
            for i in range(1, n):
                col_chunk(gate, 8, 256 * i, 256)
                col_chunk(up, 8, 256 * i, 256)
                row_chunk(down, 256 * (i - 1))
            row_chunk(down, 256 * (n - 1))

        NF = D_FF // 256
        ffn_chunks("ffn0", A["ffn_w_gate"][0], A["ffn_w_up"][0], A["ffn_w_down"][0], NF)
        first["odd"] = len(chunks)
        col_chunk(O_IN, 8, 1536, 8, 16)
        for c in (512, 768, 0, 256, 1024, 1280, 1544, 1800, 2056):
            col_chunk(O_IN, 8, c, 256)
        col_chunk(O_IN, 8, 2312, 32, 3)
        chunks.append((A["w_uq"][0][:, 0:384].rearrange("(k p) n -> p k n", p=P), 4, 384, 1))
        chunks.append((A["w_uq"][0][:, 384:768].rearrange("(k p) n -> p k n", p=P), 4, 384, 1))
        chunks.append((A["w_ukv"][0].rearrange("(k p) n -> p k n", p=P), 2, 1024, 1))
        first["odd_out"] = len(chunks)
        for q in range(4):
            row_chunk(A["odd_w_out"][0], 2 * P * q)
        ffn_chunks("ffn1", A["ffn_w_gate"][1], A["ffn_w_up"][1], A["ffn_w_down"][1], NF)
        first["sc"] = len(chunks)
        SC_IN = A["sc_w_in_2"][0]
        for q in range(4):
            for part in (1, 2, 0):
                col_chunk(SC_IN, 8, part * D + 256 * q, 256)
            if q:
                row_chunk(A["sc_w_out_2"][0], 256 * (q - 1))
        row_chunk(A["sc_w_out_2"][0], 768)
        first["mlp"] = len(chunks)
        NM = D_FF2 // 256
        col_chunk(A["mlp_w_in_2"][0], 8, 0, 256)
        for i in range(1, NM):
            col_chunk(A["mlp_w_in_2"][0], 8, 256 * i, 256)
            row_chunk(A["mlp_w_out_2"][0], 256 * (i - 1))
        row_chunk(A["mlp_w_out_2"][0], 256 * (NM - 1))
        first["end"] = len(chunks)

        order = ["even", "ffn0", "odd", "ffn1", "sc", "mlp", "end"]
        n_chunks = first[order[order.index(stop) + 1]] if stop else len(chunks)
        last_stage = order.index(stop) if stop else len(order) - 1

        def on(stage):
            return order.index(stage) <= last_stage

        def slot(t, c):
            _, k, n, copies = chunks[c]
            n *= 1 if t is raw else copies
            return t[:, c % RING, 0:k * n].rearrange("p (k n) -> p k n", k=k)

        def split_view(t, c):
            _, k, n, copies = chunks[c]
            if copies == 1:
                return slot(t, c)
            if t is raw:
                return slot(t, c).rearrange("p k (o n) -> p k o n", o=1).to_broadcast([P, k, copies, n])
            return slot(t, c).rearrange("p k (o n) -> p k o n", o=copies)

        LAP_CHUNKS, LAPS = 2 * RING, 4
        FFN_LAP = range(2, 2 + LAP_CHUNKS // 3)
        MLP_LAP = range(2, 2 + LAP_CHUNKS // 2)
        FFN_TAIL = range(2 + LAPS * len(FFN_LAP), NF)
        MLP_TAIL = range(2 + LAPS * len(MLP_LAP), NM)
        assert len(FFN_TAIL) == 1 and len(MLP_TAIL) == 2
        lap_starts = {first[f] + 2 + 3: (f, (A["ffn_w_gate"][n], A["ffn_w_up"][n]), A["ffn_w_down"][n])
                      for n, f in enumerate(("ffn0", "ffn1"))}
        lap_starts[first["mlp"] + 1 + 2] = ("mlp", (A["mlp_w_in_2"][0],), A["mlp_w_out_2"][0])

        raw_landed = [sem(f"raw_landed{i}") for i in range(RING)]
        hi_split, lo_split, chunk_used = sem("hi_split"), sem("lo_split"), sem("chunk_used")

        NORM_TILES = {"ssm": 8, "ln0": 8, "ln1": 8, "qn": 4, "kvn": 2, "ln2": 8, "ln3": 8, "pre": 8, "post": 8,
                      "preff": 8, "postff": 8}

        def norm_incs(name, kind):
            pairs = NORM_TILES[name] // 2
            if kind in ("resid", "scaled_r"):
                return 4 if name in LNS else 0
            if kind == "folded":
                return 0 if name in ("qn", "kvn") else 6 if name in LNS else 4
            if kind == "small":
                return 4 if name in LNS else 0
            if kind in ("hi", "full", "lo"):
                return 0 if name in ("ln3", "post", "postff") else 2 * pairs if kind == "hi" else pairs
            return pairs if kind in ("sq", "scaled") else 1

        def norm(name, kind, n):
            before = 0
            for other in NORM_TILES:
                if other == name:
                    return sem(f"norm_{kind}"), before + n
                before += norm_incs(other, kind)

        NORM_BANKS = {"qn": (7, 7), "kvn": (7, 7), "ln2": (1, 2)}
        LNS = {"ln0": (60, 76), "ln1": (92, 108), "ln2": (68, 84), "ln3": (100, 116)}

        EVEN_STEPS = [("proj", p) for p in range(2, 7)] + [
            ("small", 0), ("proj", 7), ("head", 0), ("proj", 8), ("bcast", 0), ("proj", 9), ("state", 0), ("proj", 10),
            ("y", 0), ("proj", 11), ("head", 1), ("bcast", 1), ("pool", 0), ("proj", 12), ("pool", 1), ("y", 1)]
        ODD_STEPS = [("proj", p) for p in range(2, 7)] + [
            ("proj", 7), ("att", 0), ("proj", 8), ("att", 1), ("proj", 9), ("qn_sum", 0), ("att", 2), ("qn_out", 0),
            ("proj", 10), ("att", 3), ("uq", 0), ("kvn_sum", 0), ("att", 4), ("kvn_out", 0), ("att", 5), ("uq", 1),
            ("att", 6)] + [("mla", i) for i in range(5)] + [("att", 7)] + [
            ("mla", i) for i in range(5, 11)] + [("att", 8), ("rows", 0), ("att", 9), ("rows", 1), ("att", 10), ("att", 11),
            ("rows", 2), ("att", 12), ("att", 13), ("rows", 3), ("att", 14), ("rows", 4), ("att", 15), ("att", 16),
            ("rows", 5), ("att", 17)]
        MLA_ORDER = ["kr", "q0", "k0", "k1", "q1", "k2", "k3", "q2", "v0", "q3", "v1"]
        MLA_FILLS = [f for f in range(11, 26) if f not in (12, 14, 25)]

        def wait_fill_read(eng, f):
            kind = MLA_ORDER[f - 15] if f >= 15 else ""
            if kind == "kr":
                eng.wait_ge(sem("kr_sum"), 1)
            elif kind.startswith("q"):
                eng.wait_ge(sem("qm_rot"), int(kind[1]) + 1)
            else:
                swapped_before = sum(m == "kr" or m[0] == "q" for m in MLA_ORDER[:max(f - 15, 0)])
                eng.wait_ge(sem("odd_evac"), f + 1 - swapped_before)

        def wait_fill(eng, f):
            if f in MLA_FILLS:
                eng.wait_ge(sem("mla_fill"), MLA_FILLS.index(f) + 1)
            else:
                eng.wait_ge(chunk_used, first["odd"] + {12: 12, 14: 13, 25: 14}.get(f, f + 1))

        ACC_ENDS = ["even_out", "ffn0", "odd_out", "ffn1", "sc", "mlp"]

        def wait_acc(eng, which, q):
            if q < 3:
                eng.wait_ge(sem("acc_done"), 3 * ACC_ENDS.index(which) + q + 1)
            else:
                order_ = ["even", "even_out", "ffn0", "odd", "odd_out", "ffn1", "sc", "mlp", "end"]
                eng.wait_ge(chunk_used, first[order_[order_.index(which) + 1]])

        ADA_N = 3 * KT

        def ada_step(dve, n):
            b, k = n // KT, n % KT
            dve.wait_ge(sem(f"ada_landed{n % 2}"), 16 * (n // 2 + 1))
            if k:
                dve.wait_ge(sem("ada_fma"), n)
                dve.scalar_tensor_tensor(out=ada_acc[:, b, :], in0=ada_raw[:, n % 2, :], scalar=silu_c[:, k:k + 1],
                                         in1=ada_acc[:, b, :], op0=ALU.mult, op1=ALU.add).then_inc(sem("ada_fma"), 1)
            else:
                dve.tensor_scalar(ada_acc[:, b, :], ada_raw[:, n % 2, :], silu_c[:, k:k + 1], None, ALU.mult)\
                    .then_inc(sem("ada_fma"), 1)

        def conv_silu(act, p):
            t = 8 + 2 * (p - 1) if p <= 2 else 2 * (p - 3)
            act.wait_ge(sem("conv_done"), p)
            act.activation(xbc[:, t:t + 2, :], conv_acc[:, p % 2, :, :], ACT.Silu).then_inc(sem("xbc_ready"), 1)

        v1, v2, v3 = rows
        vector_rows = (
            (v1, 0, 48, A["conv_w"][0].rearrange("j (t p) -> (j t) p", p=P)),
            (v1, 48, 12, A["conv_b"][0].rearrange("(t p) -> t p", p=P)),
            (v1, 60, 16, A["ln_mix_g"].rearrange("l (t p) -> (l t) p", p=P)),
            (v1, 76, 16, A["ln_mix_b"].rearrange("l (t p) -> (l t) p", p=P)),
            (v1, 92, 16, A["ln_ffn_g"].rearrange("l (t p) -> (l t) p", p=P)),
            (v1, 108, 16, A["ln_ffn_b"].rearrange("l (t p) -> (l t) p", p=P)),
            (v2, 0, 4, A["pool_scale"][0].rearrange("(t p) -> t p", p=P)),
            (v2, 4, 8, A["ssm_norm_w"][0].rearrange("(t p) -> t p", p=P)),
            (v2, 12, 4, A["q_norm_w"][0].rearrange("(t p) -> t p", p=P)),
            (v2, 16, 2, A["kv_norm_w"][0].rearrange("(t p) -> t p", p=P)),
            (v2, 18, 32, A["norm_gains_2"][0].rearrange("i (t p) -> (i t) p", p=P)),
            (v2, 50, 24, A["sc_conv_2"][0].rearrange("j (t p) -> (j t) p", p=P)),
            (v3, 0, 48, A["ada_b_2"][0].rearrange("(t p) -> t p", p=P)),
            (v3, 48, 8, A["c_2"][0].rearrange("(t p) -> t p", p=P)))

        block = ctx.enter_context(nc.Block())

        @block.sync
        def _(sp):
            for t in range(2):
                sp.dma_start(sq[:, 4 * t:4 * t + 4, :].rearrange("p a s -> p (a s)"),
                             A["x"][0, t * P:(t + 1) * P, :]).then_inc(sem("x_landed"), 16)
            def load(c, lap=0, src=None):
                if c >= RING:
                    sp.wait_ge(lo_split, c - RING + 1 + LAP_CHUNKS * lap)
                sp.dma_start(slot(raw, c), chunks[c][0] if src is None else src).then_inc(raw_landed[c % RING], 16)

            def stream_laps(name, ins, down):
                per = len(ins) + 1
                blocks = LAP_CHUNKS // per
                with sp.Fori(0, LAPS) as lap:
                    for i in range(2, 2 + blocks):
                        c = first[name] + len(ins) + per * (i - 1)
                        for w in ins:
                            load(c, lap, w.rearrange("(k p) n -> p k n", p=P)[:, :, bass.ds(256 * i + 256 * blocks * lap, 256)])
                            c += 1
                        load(c, lap, down.rearrange("(k p) n -> p k n", p=P)[:, bass.ds(2 * (i - 1) + 2 * blocks * lap, 2), :])

            c = 0
            while c < n_chunks:
                if c in lap_starts:
                    stream_laps(*lap_starts[c])
                    c += LAP_CHUNKS * LAPS
                else:
                    load(c)
                    c += 1
            if stop:
                return
            for half in range(2):
                for t in range(2):
                    sp.wait_ge(sem(("out_rows_act", "out_rows_dve")[t]), half + 1)
                    sp.dma_start(out[0, t * P:(t + 1) * P, half * 512:half * 512 + 512],
                                 sq[:, 4 * t + 2 * half:4 * t + 2 * half + 2, :].rearrange("p a s -> p (a s)"))\
                      .then_inc(sem("stored"), 16)
            sp.wait_ge(sem("stored"), 64)

        @block.gpsimd
        def _(pool):
            for dst, o, n, src in vector_rows[6:]:
                pool.dma_start(dst[o:o + n, :], src).then_inc(sem("rows_landed_pool"), 16)
            pool.memset(ones[:, :], 1.0).then_inc(sem("fixed"), 1)
            with nc.allow_non_contiguous_dma(reason="a few small vectors"):
                for i, (name, n) in enumerate((("dt_bias", 16), ("a_log", 16), ("fgate_b", 8))):
                    pool.dma_start(head_vec[0:n, (0, 1, 3)[i]:(0, 1, 3)[i] + 1],
                                   A[name].rearrange("a (h o) -> (a h) o", o=1)).then_inc(sem("heads_landed"), 16)
                for e in range(2):
                    pool.dma_start(d_skip[64 * e:64 * e + 64, :],
                                   A["d_skip"][0:1, e::2].to_broadcast([64, KT])).then_inc(sem("heads_landed"), 16)
            pool.dma_start(pool_w_sb[:, :, :], A["pool_w"][0].rearrange("g c d -> c g d")).then_inc(sem("poolw_landed"), 16)

            for t in (u_pad[:, :, 0:16], win_a[:, :, 0:16], win_b[:, :, 0:16]):
                pool.memset(t, 0.0).then_inc(sem("pad_zero"), 1)
            pool.wait_ge(sem("pad_zero"), 3)
            pool.wait_ge(sem("even_evac"), 8)
            src = u_pad
            for lv, dst in enumerate((win_a, win_b, win_a, win_b)):
                sh = 1 << lv
                pool.tensor_tensor(dst[:, lv:4, 16:16 + S], src[:, lv:4, 16:16 + S], src[:, lv:4, 16 - sh:16 - sh + S],
                                   ALU.add).then_inc(sem("window"), 1)
                pool.wait_ge(sem("window"), lv + 1)
                src = dst
            for g, w in enumerate((2, 4, 8, 16)):
                t = (win_a, win_b)[g % 2]
                if g == 0:
                    pool.wait_ge(sem("const_landed"), 16)
                o = CONST_COLS["inv_count"][0] + 16 * g
                pool.tensor_tensor(t[:, g, 16:32], t[:, g, 16:32], const[:, o:o + 16], ALU.mult).then_inc(sem("window"), 1)
                pool.tensor_scalar(t[:, g, 32:16 + S], t[:, g, 32:16 + S], 1.0 / w, None, ALU.mult).then_inc(sem("window"), 1)
                pool.wait_ge(sem("window"), 4 + 2 * g + 2)
                pool.tensor_tensor(pool_y[:, g, :], t[:, g, 16:16 + S], u_pad[:, g, 16:16 + S], ALU.subtract)\
                    .then_inc(sem("pool_diff"), 1)

            if on("odd"):
                rr = slice(ROPE_ROW, 96)
                cos = cst("cos", 96)[rr, :]
                pool.wait_ge(sem("odd_evac"), 11)
                pool.tensor_tensor(kr_cos[rr, :], kr[rr, 0, :], cos, ALU.mult).then_inc(sem("kr_cos"), 1)
                pool.wait_ge(*norm("kvn", "var", 1))
                for q in range(4):
                    pool.wait_ge(sem("odd_evac"), 12 + q)
                    pool.tensor_tensor(sq[rr, 2 * q:2 * q + 2, :], qm[rr, 2 * q:2 * q + 2, :],
                                       cos.rearrange("p (o s) -> p o s", o=1).to_broadcast([32, 2, S]), ALU.mult)\
                        .then_inc(sem("qm_cos"), 1)
                pool.wait_ge(sem("kr_sum"), 1)
                pool.tensor_copy(km[rr, :, :], kr_rot[rr, :].rearrange("p (o s) -> p o s", o=1)
                                 .to_broadcast([32, MLA_H, S])).then_inc(sem("kr_rot"), 1)
            if on("ffn1"):
                pool.wait_ge(*norm("ln2", "lo", 4))
                for n in range(ADA_N):
                    if n >= 2:
                        pool.wait_ge(sem("ada_fma"), n - 1)
                    pool.dma_start(ada_raw[:, n % 2, :], A["ada_w_2"][0][n % KT * P:(n % KT + 1) * P,
                                                                         n // KT * CH:(n // KT + 1) * CH])\
                        .then_inc(sem(f"ada_landed{n % 2}"), 16)

        @block.tensor
        def _(pe):
            lap = [0]

            def mm3(dst, c, cols, k, hi, lo, start, stop_, kk=None):
                kk = k if kk is None else kk
                wh, wl = slot(w_hi, c)[:, kk, cols], slot(w_lo, c)[:, kk, cols]
                pe.matmul(dst, wh, hi, start=start, stop=False, skip_group_check=True)
                pe.matmul(dst, wh, lo, start=False, stop=False, skip_group_check=True)
                return pe.matmul(dst, wl, hi, start=False, stop=stop_, skip_group_check=True)

            def col(c, bank, hi, lo, operand=None):
                _, kt, n, copies = chunks[c]
                n *= copies
                pe.wait_ge(lo_split, c + 1 + LAP_CHUNKS * lap[0])
                for m in range(0, n, P):
                    w = min(P, n - m)
                    for k in range(kt):
                        if operand and m == 0 and k % 2 == 0:
                            pe.wait_ge(operand[0], operand[1] + k // 2 + 1)
                        last = mm3(PS[0:w, bank, (m // P) * S:(m // P) * S + S], c, slice(m, m + w), k,
                                   hi[:, k, :], lo[:, k, :], k == 0, k == kt - 1)
                last.then_inc(chunk_used, 1)

            def first_two(c, banks, hi, lo, operand):
                pe.wait_ge(lo_split, c + 2)
                for k in range(KT):
                    if k % 2 == 0:
                        pe.wait_ge(operand[0], operand[1] + k // 2 + 1)
                    for i in range(2):
                        n = chunks[c + i][2] * chunks[c + i][3]
                        for m in range(0, n, P):
                            last = mm3(PS[:, banks[i], (m // P) * S:(m // P) * S + S], c + i, slice(m, m + P), k,
                                       hi[:, k, :], lo[:, k, :], k == 0 and m == 0, k == KT - 1)
                        if k == KT - 1:
                            last.then_inc(chunk_used, 1)

            def rows_acc(c, hi, lo, k_first, k_last, b0=0, halves=(0, 1)):
                if 0 in halves:
                    pe.wait_ge(lo_split, c + 1 + LAP_CHUNKS * lap[0])
                acc = [PS[:, b0 + n // 2, (n % 2) * S:(n % 2) * S + S] for n in range(8)]
                if k_last:
                    for n in range(8):
                        for kk in range(2):
                            last = mm3(acc[n], c, slice(n * P, n * P + P), 0, hi[:, kk, :], lo[:, kk, :], False, kk == 1, kk=kk)
                        if n in (1, 3, 5):
                            last.then_inc(sem("acc_done"), 1)
                    last.then_inc(chunk_used, 1)
                    return
                for kk in halves:
                    for n in range(8):
                        last = mm3(acc[n], c, slice(n * P, n * P + P), 0, hi[:, kk, :], lo[:, kk, :],
                                   k_first and kk == 0 and n % 2 == 0, False, kk=kk)
                if 1 in halves:
                    last.then_inc(chunk_used, 1)

            def norm_sums(name, t=KT):
                bank = NORM_BANKS.get(name, (5, 6))[0]
                if name in LNS:
                    parts = [([hid[:, 0, 0, :], hid[:, 0, 1, :]], "folded", 1, 0),
                             ([hid[:, 1, 0, :], hid[:, 1, 1, :]], "folded", 2, 0), ([hid[:, 2, 0, :]], "folded", 6, 2)]
                elif t == KT:
                    parts = [([hid[:, 2, 0, :]], "folded", 4, 2)]
                else:
                    parts = [([sq[:, 2 * q, :], sq[:, 2 * q + 1, :]], "sq", q + 1, 2) for q in range(t // 2)]
                last_part = {o: i for i, (_, _, _, o) in enumerate(parts)}
                started = False
                for i, (tiles, kind, n, o) in enumerate(parts):
                    pe.wait_ge(*norm(name, kind, n))
                    for k, tile in enumerate(tiles):
                        for j in range(2):
                            last = pe.matmul(PS[:, bank, o + j:o + j + 1], tile[:, j * P:(j + 1) * P], ones[:, 0:1],
                                             start=not started, stop=i == last_part[o] and k == len(tiles) - 1,
                                             skip_group_check=True)
                            started = True
                last.then_inc(sem("norm_var"), 1)

            def norm_bcast(name):
                bank = NORM_BANKS.get(name, (5, 6))[1]
                pe.wait_ge(*norm(name, "rcp", 1))
                for i in range(4 if name in LNS else 2):
                    last = pe.matmul(PS[:, bank, i * P:(i + 1) * P], rstd[:, i:i + 1].to_broadcast([P, P]), ident,
                                     start=True, stop=True)
                last.then_inc(sem("norm_rb"), 1)

            def norm_scale(name, t=KT):
                norm_sums(name, t)
                norm_bcast(name)

            def ffn(name, base, operand):
                hid_lo_ok = sem(f"{name}_hid_lo")

                def fill(i, c):
                    b = 4 + 2 * (i % 2)
                    col(c, b, x_hi, x_lo)
                    col(c + 1, b + 1, x_hi, x_lo)

                first_two(base, (4, 5), x_hi, x_lo, norm(operand, "lo", 0))

                def block_(i):
                    fill(i, base + 2 + 3 * (i - 1))
                    pe.wait_ge(hid_lo_ok, i + len(FFN_LAP) * lap[0])
                    rows_acc(base + 4 + 3 * (i - 1), hid_hi[:, (i - 1) % 2, :, :], hid_lo[:, (i - 1) % 2, :, :],
                             i == 1, False)

                block_(1)
                with pe.Fori(0, LAPS) as lap[0]:
                    for i in FFN_LAP:
                        block_(i)
                lap[0] = 0
                for i in FFN_TAIL:
                    block_(i)
                pe.wait_ge(hid_lo_ok, NF)
                rows_acc(base + 2 + 3 * (NF - 1), hid_hi[:, (NF - 1) % 2, :, :], hid_lo[:, (NF - 1) % 2, :, :],
                         False, True)

            pe.wait_ge(sem("ident_landed"), 16)
            pe.wait_ge(sem("x_landed"), 32)
            xt = sq[:, :, :].rearrange("p (t q) s -> p t (q s)", t=2)
            for b in range(4):
                for k in (2 * b, 2 * b + 1):
                    for t in range(2):
                        o = (k % 2) * S + t * P
                        last = pe.transpose(PS[:, b, o:o + P], xt[:, t, k * P:(k + 1) * P], ident)
                last.then_inc(sem("x_turned"), 1)

            base = first["even"]
            col(base, 4, x_hi, x_lo, (sem("x_lo_ready"), 0))
            col(base + 1, 5, x_hi, x_lo)
            pe.wait_ge(sem("rows_landed_act"), 16 * 6)
            pe.wait_ge(sem("rows_landed_pool"), 16 * 8)
            for i, n in enumerate((124, 74, 56)):
                last = pe.transpose(PS[:, 7, i * P:i * P + n], rows[i][0:n, :], ident[0:n, 0:n])
            last.then_inc(sem("vecs_turned"), 1)
            pe.wait_ge(sem("const_landed"), 16)

            def even_proj(p):
                if p >= 9:
                    pe.wait_ge(sem("even_evac"), p - 2)
                elif p == 3:
                    pe.wait_ge(sem("vecs_ready"), 1)
                elif p == 4:
                    pe.wait_ge(sem("dt_raw"), 1)
                elif p > 4:
                    pe.wait_ge(sem("even_evac"), 6 if p == 8 else p - 4)
                col(base + p, 4 + p % 4 if p < 7 else 6 + p % 2, x_hi, x_lo)

            def even_small(_):
                pe.wait_ge(sem("da_ready"), 1)
                for j in range(2):
                    for q in range(2):
                        o = 32 * j + 16 * q
                        last = pe.transpose(PS[:, 0, o:o + 16], small[0:16, q, j * P:(j + 1) * P], ident[0:16, 0:16])
                last.then_inc(sem("tok_turned"), 1)
                pe.wait_ge(sem("xbc_ready"), 2)
                for g in range(2):
                    last = pe.transpose(PS[:, 1, g * P:(g + 1) * P], xbc[:, 8 + g, 0:P], ident)
                last.then_inc(sem("b_turned"), 1)
                for j in range(2):
                    for g in range(2):
                        q = 2 * j + g
                        last = pe.matmul(PS[:, 2, q * P:(q + 1) * P], xbc[:, 8 + g, j * P:(j + 1) * P],
                                         xbc[:, 10 + g, j * P:(j + 1) * P], start=True, stop=True)
                last.then_inc(sem("cb_done"), 1)

            def even_head(j):
                if j == 0:
                    pe.wait_ge(sem("tok_ready"), 1)
                    pe.wait_ge(sem("fixed"), 1)
                    for c in range(2):
                        pe.matmul(PS[:, 0, 64 + 16 * c:80 + 16 * c], triu, tok[:, c, 16:32], start=True, stop=True)
                    pe.matmul(PS[:, 0, 96:112], ones[:, :], tok[:, 0, 16:32], start=True, stop=True)\
                        .then_inc(sem("acs_done"), 1)
                if j == 0:
                    pe.wait_ge(sem("xbc_ready"), 6)
                    pe.wait_ge(sem("even_evac"), 5)
                else:
                    pe.wait_ge(sem("y_ready"), 8)
                for k in range(KT):
                    o = (k % 4) * P
                    last = pe.transpose(PS[:, 4 + k // 4, o:o + P], xbc[:, k, j * P:(j + 1) * P], ident)
                last.then_inc(sem("xtok_done"), 1)

            def even_bcast(j):
                if j == 0:
                    pe.wait_ge(sem("acs_ready"), 2)
                    pe.wait_ge(sem("b_tok_ready"), 1)
                    pe.wait_ge(sem("cb_ready"), 1)
                else:
                    pe.wait_ge(sem("seg_done"), 4)
                for h in range(HEADS):
                    last = pe.matmul(PS[:, h // 4, (h % 4) * P:(h % 4) * P + P],
                                     tok[:, j, 16 + h:17 + h].to_broadcast([P, P]), triu, start=True, stop=True)
                    if h % 4 == 3:
                        last.then_inc(sem("acs_bcast"), 1)

            def even_state(_):
                pe.wait_ge(sem("xdec_ready"), 1)
                for g in range(2):
                    pe.matmul(PS[:, 4 + g, :], b_tok[:, g * P:(g + 1) * P], x_dec[:, g * 512:(g + 1) * 512],
                              start=True, stop=True).then_inc(sem("state_done"), 1)

            def even_y(j):
                pe.wait_ge(sem("lmat_ready"), 2 * j + 2)
                if j:
                    pe.wait_ge(sem("xdt_ready"), 4)
                    pe.wait_ge(sem("cdec_ready"), 2)
                else:
                    pe.wait_ge(sem("state_ready"), 2)
                for k in range(KT):
                    o = (k % 4) * P
                    for e in range(2):
                        h = 2 * k + e
                        dst = PS[64 * e:64 * e + 64, 4 + k // 4, o:o + P]
                        last = pe.matmul(dst, x_dt[:, h * 64:h * 64 + 64], lmat[:, h, :], start=True, stop=j == 0)
                        if j:
                            last = pe.matmul(dst, state[:, h * 64:h * 64 + 64], e_acs[:, h, :], start=False, stop=True)
                    last.then_inc(sem("y_done"), 1)

            def even_pool(i):
                if i == 0:
                    pe.wait_ge(sem("even_evac"), 11)
                    pe.wait_ge(sem("pool_diff"), 4)
                    pe.wait_ge(sem("poolw_landed"), 16)
                else:
                    pe.wait_ge(sem("pool_scaled"), 2)
                for g in (2 * i, 2 * i + 1):
                    last = pe.matmul(PS[:, 7, (g % 2) * S:(g % 2) * S + S], pool_w_sb[:, g, :], pool_y[:, g, :],
                                     start=True, stop=True)
                last.then_inc(sem("pool_done"), 1)
                if i == 1:
                    pe.wait_ge(sem("seg_done"), 8)
                    pe.wait_ge(sem("eacs_done"), 4)
                    pe.wait_ge(sem("pool_lo_ready"), 1)
                    rows_acc(base + 13, pool_hi[:, 0:2, :], pool_lo[:, 0:2, :], True, False)

            for step, arg in EVEN_STEPS:
                {"proj": even_proj, "small": even_small, "head": even_head, "bcast": even_bcast, "state": even_state,
                 "y": even_y, "pool": even_pool}[step](arg)
            pe.wait_ge(sem("pool_lo_ready"), 2)
            rows_acc(base + 14, pool_hi[:, 2:4, :], pool_lo[:, 2:4, :], False, False)
            norm_scale("ssm")
            for q in range(4):
                pe.wait_ge(*norm("ssm", "lo", q + 1))
                rows_acc(base + 15 + q, x_hi[:, 2 * q:2 * q + 2, :], x_lo[:, 2 * q:2 * q + 2, :], False, q == 3)
            norm_scale("ln0")
            if not on("ffn0"):
                return
            ffn("ffn0", first["ffn0"], "ln0")
            norm_scale("ln1")
            if not on("odd"):
                return

            base = first["odd"]
            first_two(base, (4, 5), x_hi, x_lo, norm("ln1", "lo", 0))

            def odd_free(f):
                wait_fill_read(pe, f - 3)
                return 4 + f % 3

            def odd_proj(p):
                bank = odd_free(p) if p > 2 else 6
                if p not in (5, 6):
                    col(base + p, bank, x_hi, x_lo)
                    return
                pe.wait_ge(lo_split, base + p + 1)
                wh, wl = slot(w_hi, base + p), slot(w_lo, base + p)
                for j in range(2):
                    dst = PS[:, bank, j * S:(j + 1) * S]
                    for k in range(KT):
                        xh, xl = x_hi[:, k, j * P:(j + 1) * P], x_lo[:, k, j * P:(j + 1) * P]
                        pe.matmul(dst, xh, wh[:, k, :], start=k == 0, stop=False)
                        pe.matmul(dst, xh, wl[:, k, :], start=False, stop=False)
                        last = pe.matmul(dst, xl, wh[:, k, :], start=False, stop=k == KT - 1)
                last.then_inc(chunk_used, 1)

            def qn_sum(_):
                norm_sums("qn", 4)

            def qn_out(_):
                norm_bcast("qn")

            def kvn_sum(_):
                pe.wait_ge(*norm("qn", "scaled", 2))
                norm_sums("kvn", 2)

            def kvn_out(_):
                norm_bcast("kvn")

            def uq(c):
                pe.wait_ge(lo_split, base + 12 + c)
                if c == 0:
                    pe.wait_ge(*norm("qn", "lo", 2))
                for h in range(4 * c, 4 * c + 4):
                    bank = odd_free(11 + h // 2) if h % 2 == 0 else bank
                    for k in range(4):
                        last = mm3(PS[0:96, bank, (h % 2) * S:(h % 2) * S + S], base + 11 + c,
                                   slice(96 * (h % 4), 96 * (h % 4) + 96), k, cq_hi[:, k, :], cq_lo[:, k, :], k == 0, k == 3)
                    if h == 4 * c + 1:
                        last.then_inc(sem("mla_fill"), 1)
                last.then_inc(chunk_used, 1)

            kv_h, kv_l = (slot(t, base + 13).rearrange("p k (h e) -> p k h e", h=MLA_H) for t in (w_hi, w_lo))

            def mla(i):
                f, kind = 15 + i, MLA_ORDER[i]
                bank = odd_free(f)
                pair = bank2(bank)
                if kind == "kr" or kind[0] == "q":
                    swap = cst("swap", 96)
                    for e in range(1 if kind == "kr" else 2):
                        src = kr[:, 0, :] if kind == "kr" else qm[:, 2 * int(kind[1]) + e, :]
                        last = pe.matmul(pair[0:96, e, :], swap, src, start=True, stop=True)
                elif kind[0] == "k":
                    if kind == "k0":
                        pe.wait_ge(lo_split, base + 14)
                        pe.wait_ge(*norm("kvn", "lo", 1))
                    for e in range(2):
                        h = 2 * int(kind[1]) + e
                        for k in range(2):
                            pe.matmul(pair[0:96, e, :], kv_h[:, k, h, 0:96], ckv_hi[:, k, :], start=k == 0, stop=False)
                            pe.matmul(pair[0:96, e, :], kv_h[:, k, h, 0:96], ckv_lo[:, k, :], start=False, stop=False)
                            last = pe.matmul(pair[0:96, e, :], kv_l[:, k, h, 0:96], ckv_hi[:, k, :], start=False, stop=k == 1)
                else:
                    j = int(kind[1])
                    for k in range(2):
                        xh, xl = ckv_hi[:, k, j * P:(j + 1) * P], ckv_lo[:, k, j * P:(j + 1) * P]
                        pe.matmul(PS[:, bank, :], xh, kv_h[:, k, :, 64:128], start=k == 0, stop=False)
                        pe.matmul(PS[:, bank, :], xh, kv_l[:, k, :, 64:128], start=False, stop=False)
                        last = pe.matmul(PS[:, bank, :], xl, kv_h[:, k, :, 64:128], start=False, stop=k == 1)
                last.then_inc(chunk_used if kind == "v1" else sem("mla_fill"), 1)

            def out_rows(i):
                q, kk = i // 2, i % 2
                if kk == 0:
                    pe.wait_ge(sem("odd_evac"), 21)
                    pe.wait_ge(sem("qm_rot"), 4)
                    pe.wait_ge(sem("o_lo"), 2 * q + 2)
                rows_acc(first["odd_out"] + q, x_hi[:, 2 * q:2 * q + 2, :], x_lo[:, 2 * q:2 * q + 2, :], q == 0, False,
                         b0=4, halves=(kk,))

            def scores(a):
                if a >= 2:
                    pe.wait_ge(sem("masked"), 2 * (a - 1))
                if a == 0:
                    pe.wait_ge(sem("neg_f_ready"), 1)
                    pe.wait_ge(sem("odd_evac"), 5)
                if a == FOX_H:
                    pe.wait_ge(sem("odd_evac"), 19)
                    pe.wait_ge(sem("kr_rot"), 1)
                if a >= FOX_H and a % 2 == 0:
                    pe.wait_ge(sem("qm_rot"), (a - FOX_H) // 2 + 1)
                b = a % 2
                for j, kw, o in ((0, P, 0), (1, S, P)):
                    dst = PS[:, b, o:o + kw]
                    qs = slice(j * P, (j + 1) * P)
                    if a < FOX_H:
                        pe.matmul(dst, qz[:, a, qs], kf[:, a // 2, 0:kw], start=True, stop=False)
                        last = pe.matmul(dst, ident[:, a:a + 1].to_broadcast([P, P]), neg_f[:, 0:kw], start=False, stop=True)
                    else:
                        h = a - FOX_H
                        last = pe.matmul(dst, qm[:, h, qs], km[:, h, 0:kw], start=True, stop=True)
                last.then_inc(sem("scored"), 1)

            def turn(a):
                pe.wait_ge(sem("prob_ready"), 2 * a + 2)
                if a >= 1:
                    pe.wait_ge(sem("prob_t_ready"), a)
                for o in (0, P, 2 * P):
                    last = pe.transpose(PS[:, 2, o:o + P], prob[:, a % 2, o:o + P], ident)
                last.then_inc(sem("prob_turned"), 1)

            def attend(a):
                pe.wait_ge(sem("prob_t_ready"), a + 1)
                pair, e = a // 2, a % 2
                if e == 0 and pair >= 1:
                    pe.wait_ge(sem("o_lo"), pair)
                if a in (0, FOX_H):
                    pe.wait_ge(sem("odd_evac"), 21 if a else 7)
                v, h = (v_tok, a) if a < FOX_H else (vm_tok, a - FOX_H)
                pt = prob_t[:, a % 2, :]
                pe.matmul(PS[64 * e:64 * e + 64, 3, 0:S], v[:, 0, h * 64:h * 64 + 64], pt[:, 0:S], start=True, stop=False,
                          skip_group_check=True)
                pe.matmul(PS[64 * e:64 * e + 64, 3, P:S], v[:, 1, h * 64:h * 64 + 64], pt[:, S:384], start=False, stop=True,
                          skip_group_check=True).then_inc(sem("attended"), 1)

            def attention(a):
                if a < 16:
                    scores(a)
                if 1 <= a <= 16:
                    turn(a - 1)
                if a >= 2:
                    attend(a - 2)

            for step, arg in ODD_STEPS:
                {"proj": odd_proj, "att": attention, "qn_sum": qn_sum, "qn_out": qn_out, "kvn_sum": kvn_sum,
                 "kvn_out": kvn_out, "uq": uq, "mla": mla, "rows": out_rows}[step](arg)
            pe.wait_ge(sem("o_lo"), 8)
            rows_acc(first["odd_out"] + 3, x_hi[:, 6:8, :], x_lo[:, 6:8, :], False, True, b0=4)
            norm_scale("ln2")
            if not on("ffn1"):
                return
            ffn("ffn1", first["ffn1"], "ln2")
            if not on("sc"):
                norm_scale("ln3")
                return
            def mod_sums(n0, n1):
                pe.wait_ge(sem("ada_fma"), KT * ((n1 - 1) // 16 + 1))
                for n in range(n0, n1):
                    last = pe.matmul(PS[:, 7, n:n + 1], ada_acc[:, n // 16, (n % 16) * P:(n % 16) * P + P], ones[:, 0:1],
                                     start=True, stop=True)
                last.then_inc(sem("mod_done"), 1)

            norm_sums("ln3")
            mod_sums(0, 4)
            norm_bcast("ln3")
            mod_sums(4, 24)
            norm_scale("pre")
            base = first["sc"]
            c, f = base, 0
            for q in range(4):
                for part in range(3):
                    if q == 0 and part < 2:
                        if part == 0:
                            first_two(base, (4, 5), x_hi, x_lo, norm("pre", "lo", 0))
                        c, f = c + 1, f + 1
                        continue
                    if f == 3:
                        pe.wait_ge(sem("mod_evac"), 2)
                    if f >= 4:
                        pe.wait_ge(sem(("sc_evac_c", "cv_ready", "sc_evac_b")[(f - 4) % 3]), (f - 4) // 3 + 1)
                    col(c, 4 + f % 4, x_hi, x_lo)
                    c, f = c + 1, f + 1
                if q:
                    pe.wait_ge(sem("sc_lo"), q)
                    rows_acc(c, hid_hi[:, (q - 1) % 2, :, :], hid_lo[:, (q - 1) % 2, :, :], q == 1, False)
                    c += 1
            pe.wait_ge(sem("sc_lo"), 4)
            rows_acc(c, hid_hi[:, 1, :, :], hid_lo[:, 1, :, :], False, True)
            mod_sums(24, 32)
            norm_scale("post")
            mod_sums(32, 48)
            norm_scale("preff")
            if not on("mlp"):
                return
            base = first["mlp"]
            first_two(base, (4, 5), x_hi, x_lo, norm("preff", "lo", 0))

            def mlp_block(i):
                if i > 1:
                    col(base + 1 + 2 * (i - 1), 4 + i % 3, x_hi, x_lo)
                pe.wait_ge(sem("mlp_lo"), i + len(MLP_LAP) * lap[0])
                rows_acc(base + 2 + 2 * (i - 1), hid_hi[:, (i - 1) % 3, :, :], hid_lo[:, (i - 1) % 3, :, :], i == 1, False)

            mlp_block(1)
            with pe.Fori(0, LAPS) as lap[0]:
                for i in MLP_LAP:
                    mlp_block(i)
            lap[0] = 0
            for i in MLP_TAIL:
                mlp_block(i)
            pe.wait_ge(sem("mlp_lo"), NM)
            rows_acc(base + 1 + 2 * (NM - 1), hid_hi[:, (NM - 1) % 3, :, :], hid_lo[:, (NM - 1) % 3, :, :], False, True)
            norm_scale("postff")
            for k in range(KT):
                pe.wait_ge(sem("final_x"), k + 1)
                for t in range(2):
                    last = pe.transpose(PS[:, 2 * t + k // 4, (k % 4) * P:(k % 4) * P + P], x[:, k, t * P:(t + 1) * P], ident)
                if k % 4 == 3:
                    last.then_inc(sem("out_turned"), 1)

        @block.scalar
        def _(act):
            done = [0]
            lap = [0]

            def split(upto):
                while done[0] <= min(upto, n_chunks - 1):
                    c = done[0]
                    act.wait_ge(raw_landed[c % RING], 16 * (c // RING + 1) + 16 * LAP_CHUNKS // RING * lap[0])
                    if c >= RING:
                        act.wait_ge(chunk_used, c - RING + 1 + LAP_CHUNKS * lap[0])
                    act.activation(split_view(w_hi, c), split_view(raw, c), ACT.Copy).then_inc(hi_split, 1)
                    done[0] += 1

            def squares(name, src, t=KT, ready=None):
                for q in range(t // 2):
                    if ready:
                        act.wait_ge(ready[0], ready[1] + q + 1)
                    act.activation(sq[:, 2 * q:2 * q + 2, :], src[:, 2 * q:2 * q + 2, :], ACT.Square)\
                       .then_inc(sem("norm_sq"), 1)

            def norm_std(name, eps=RMS_EPS, width=D, bank=5):
                act.wait_ge(sem("eps_set"), 1)
                i = list(NORM_TILES).index(name)
                act.activation(table_sb[:, i:i + 1], eps_sb[:, 0:1], ACT.Sqrt)
                if name in LNS:
                    act.wait_ge(*norm(name, "small", 4))
                    act.activation(std[:, :], moments[:, 2:4], ACT.Sqrt, bias=eps_col(eps)).then_inc(sem("norm_std"), 1)
                else:
                    act.wait_ge(*norm(name, "var", 1))
                    act.activation(std[:, :], PS[:, bank, 2:4], ACT.Sqrt, bias=eps_col(eps), scale=1.0 / width)\
                       .then_inc(sem("norm_std"), 1)

            def norm_stats(name, src, eps=RMS_EPS, ready=None, upto=None):
                squares(name, src, KT, ready)
                if upto is not None:
                    split(upto)
                norm_std(name, eps)

            def eps_col(eps):
                return eps_sb[:, 0:1] if eps == LN_EPS else eps_sb[:, 1:2]

            def operand_hi(name, src, dst, gains, biases, t=KT):
                for k in range(t):
                    if k % 2 == 0:
                        act.wait_ge(*norm(name, "scaled", k // 2 + 1))
                    act.activation(dst[:, k, :], src[:, k, :], ACT.Identity, scale=gains(k),
                                   bias=biases(k) if biases else 0.0).then_inc(sem("norm_hi"), 1)

            def ffn(name, base):
                def block_(i):
                    g = base if i == 0 else base + 2 + 3 * (i - 1)
                    before = len(FFN_LAP) * lap[0]
                    split(g + 2)
                    act.wait_ge(chunk_used, g + 1 + LAP_CHUNKS * lap[0])
                    if i >= 2:
                        act.wait_ge(sem(f"{name}_hid"), i - 1 + before)
                    act.activation(gate_s[:, i % 2, :, :], bank2(4 + 2 * (i % 2)), ACT.Silu).then_inc(sem(f"{name}_silu"), 1)
                    split(g + 3)
                    act.wait_ge(sem(f"{name}_hid"), i + 1 + before)
                    act.activation(hid_hi[:, i % 2, :, :], hid[:, i % 2, :, :], ACT.Copy).then_inc(sem(f"{name}_hid_hi"), 1)
                    if i < NF - 1:
                        split(g + 4 if i else g + 3)

                block_(0)
                block_(1)
                with act.Fori(0, LAPS) as lap[0]:
                    for i in FFN_LAP:
                        block_(i)
                lap[0] = 0
                done[0] += LAP_CHUNKS * (LAPS - 1)
                for i in FFN_TAIL:
                    block_(i)

            act.dma_start(const[:, 0:P], A["consts"][:, 0:P]).then_inc(sem("ident_landed"), 16)
            for dst, o, n, src in vector_rows[:6]:
                act.dma_start(dst[o:o + n, :], src).then_inc(sem("rows_landed_act"), 16)
            act.dma_start(const[:, P:], A["consts"][:, P:]).then_inc(sem("const_landed"), 16)
            for b in range(4):
                act.wait_ge(sem("x_turned"), b + 1)
                act.activation(x_hi[:, 2 * b:2 * b + 2, :], bank2(b), ACT.Copy).then_inc(sem("x_hi_ready"), 1)
            split(2)
            act.wait_ge(sem("heads_landed"), 16 * 5)
            act.activation(head_vec[:, 2:3], head_vec[:, 1:2], ACT.Exp).then_inc(sem("a_ready"), 1)
            split(3)
            act.wait_ge(sem("dt_raw"), 1)
            act.activation(small[:, 2, :], small[:, 0, :], ACT.Abs).then_inc(sem("dt_act"), 1)
            act.wait_ge(sem("dt_act"), 1)
            act.activation(small[:, 2, :], small[:, 2, :], ACT.Exp, scale=-1.0).then_inc(sem("dt_act"), 1)
            act.wait_ge(sem("dt_act"), 2)
            act.activation(small[:, 2, :], small[:, 2, :], ACT.Ln, bias=1.0).then_inc(sem("dt_act"), 1)
            act.wait_ge(sem("vecs_ready"), 1)
            act.activation(silu_c[:, :], vecs[:, 2, 48:56], ACT.Silu).then_inc(sem("silu_c_ready"), 1)

            base = first["even"]

            def even_proj(p):
                split(base + p + 2)
                act.wait_ge(chunk_used, base + p + 1)
                bank = bank2(4 + p % 4 if p < 7 else 6 + p % 2)
                if p <= 6:
                    if p == 1:
                        act.wait_ge(sem("conv_pad"), 1)
                    if p >= 3:
                        act.wait_ge(sem("conv_done"), p - 2)
                    act.activation(conv_in[:, p % 2, :, 3:3 + S], bank, ACT.Copy).then_inc(sem("even_evac"), 1)
                    if p >= 2:
                        conv_silu(act, p - 1)
                elif p <= 8:
                    act.wait_ge(sem("pad_zero"), 3)
                    act.activation(u_pad[:, 2 * (p - 7):2 * (p - 7) + 2, 16:16 + S], bank, ACT.Copy)\
                       .then_inc(sem("even_evac"), 1)
                else:
                    act.activation(z_silu[:, 2 * (p - 9):2 * (p - 9) + 2, :], bank, ACT.Silu).then_inc(sem("even_evac"), 1)

            def even_small(_):
                conv_silu(act, 6)
                act.wait_ge(sem("b_turned"), 1)
                act.activation(b_tok[:, :], PS[:, 1, 0:S], ACT.Copy).then_inc(sem("b_tok_ready"), 1)

            def even_head(j):
                if j == 0:
                    act.wait_ge(sem("acs_ready"), 2)
                    act.activation(decay[:, 1, :], decay[:, 0, :], ACT.Exp).then_inc(sem("decay_ready"), 1)

            def even_pool(i):
                act.wait_ge(sem("pool_done"), i + 1)
                for g in (2 * i, 2 * i + 1):
                    act.activation(pool_y[:, g, :], PS[:, 7, (g % 2) * S:(g % 2) * S + S], ACT.Identity, scale=vec(1, g))\
                       .then_inc(sem("pool_scaled"), 1)
                act.wait_ge(sem("pool_scaled"), 2 * i + 2)
                act.activation(pool_hi[:, 2 * i:2 * i + 2, :], pool_y[:, 2 * i:2 * i + 2, :], ACT.Copy)\
                   .then_inc(sem("pool_hi_ready"), 1)

            def even_bcast(j):
                for q in range(4):
                    act.wait_ge(sem("seg_done"), 4 * j + q + 1)
                    for h in range(4 * q, 4 * q + 4):
                        if j and h == 0:
                            act.wait_ge(sem("y_done"), 8)
                        last = act.activation(lmat[:, h, :], seg[:, (h % 4) * P:(h % 4) * P + P], ACT.Exp,
                                              bias=neg_acs[:, j, h:h + 1])
                    last.then_inc(sem("exp_done"), 1)
                    if j and q == 3:
                        even_pool(0)
                    if j:
                        if q == 0:
                            act.wait_ge(sem("pool_diff"), 4)
                        act.activation(e_acs[:, 4 * q:4 * q + 4, :], PS[:, q, :].rearrange("p (h s) -> p h s", h=4), ACT.Exp)\
                           .then_inc(sem("eacs_done"), 1)

            def even_state(_):
                for g in range(2):
                    act.wait_ge(sem("state_done"), g + 1)
                    act.activation(state[:, g * 512:(g + 1) * 512], PS[:, 4 + g, :], ACT.Copy)\
                       .then_inc(sem("state_ready"), 1)

            even_proj(1)
            for step, arg in EVEN_STEPS:
                if step == "pool":
                    if arg == 1:
                        even_pool(1)
                    continue
                {"proj": even_proj, "small": even_small, "head": even_head, "bcast": even_bcast, "state": even_state,
                 "y": lambda j: None}[step](arg)
            split(first["even_out"] + 2)
            norm_stats("ssm", r, ready=(sem("gated"), 0))
            operand_hi("ssm", r, x_hi, lambda k: vec(1, 4 + k), None)

            def layer_norm(name, following, need_hi=True):
                g, b = LNS[name]
                split(first[following] + 1)
                norm_stats(name, r, eps=LN_EPS, ready=norm(name, "resid", 0), upto=first[following] + 2)
                if need_hi:
                    i = list(NORM_TILES).index(name)
                    act.activation(table_sb[:, 11 + i:12 + i], eps_sb[:, 0:1], ACT.Exp if name == "ln1" else ACT.Silu)
                    operand_hi(name, r, x_hi, lambda k: vec(0, g + k), lambda k: vec(0, b + k))

            layer_norm("ln0", "ffn0")
            if not on("ffn0"):
                return
            ffn("ffn0", first["ffn0"])
            layer_norm("ln1", "odd")
            if not on("odd"):
                return

            base = first["odd"]
            act.wait_ge(chunk_used, base + 1)
            act.activation(small[0:8, 0, :], PS[0:8, 4, 0:S], ACT.Identity, bias=head_vec[0:8, 3:4])\
               .then_inc(sem("odd_evac"), 1)
            act.wait_ge(sem("odd_evac"), 1)
            act.activation(small[0:8, 1, :], small[0:8, 0, :], ACT.Abs).then_inc(sem("fg_act"), 1)
            act.wait_ge(sem("fg_act"), 1)
            act.activation(small[0:8, 1, :], small[0:8, 1, :], ACT.Exp, scale=-1.0).then_inc(sem("fg_act"), 1)
            act.wait_ge(sem("fg_act"), 2)
            act.activation(small[0:8, 1, :], small[0:8, 1, :], ACT.Ln, bias=1.0).then_inc(sem("fg_act"), 1)
            act.wait_ge(sem("qz_zero"), 1)

            def odd_proj(p):
                split(base + p + 2)
                wait_fill(act, p)
                bank = bank2(4 + p % 3)
                if p <= 2:
                    last = act.activation(kf[:, 2 * (p - 1):2 * (p - 1) + 2, :], bank, ACT.Copy)
                elif p <= 4:
                    t = 2 * (p - 3)
                    for e in range(2):
                        rs = slice(64 * e, 64 * e + 64)
                        last = act.activation(qz[rs, 2 * t + e:2 * t + e + 3:2, :], bank[rs], ACT.Copy, scale=0.125)
                elif p <= 6:
                    last = act.activation(v_tok[:, :, (p - 5) * S:(p - 4) * S], bank, ACT.Copy)
                elif p <= 8:
                    last = act.activation(cq[:, 2 * (p - 7):2 * (p - 7) + 2, :], bank, ACT.Copy)
                elif p == 9:
                    last = act.activation(ckv[:, :, :], bank, ACT.Copy)
                else:
                    last = act.activation(kr[:, 0, :], PS[0:96, 4 + p % 3, 0:S], ACT.Copy)
                last.then_inc(sem("odd_evac"), 1)

            def qn_sum(_):
                act.wait_ge(sem("odd_evac"), 9)
                squares("qn", cq, 4)
                norm_std("qn", width=512, bank=7)

            def qn_out(_):
                operand_hi("qn", cq, cq_hi, lambda k: vec(1, 12 + k), None, 4)

            def kvn_sum(_):
                act.wait_ge(sem("odd_evac"), 10)
                act.wait_ge(*norm("qn", "var", 1))
                squares("kvn", ckv, 2)
                act.wait_ge(*norm("qn", "rcp", 1))
                norm_std("kvn", width=256, bank=7)

            def kvn_out(_):
                operand_hi("kvn", ckv, ckv_hi, lambda k: vec(1, 16 + k), None, 2)

            def uq(c):
                split(base + 13 + c)
                for f in (11 + 2 * c, 12 + 2 * c):
                    wait_fill(act, f)
                    act.activation(qm[:, 2 * (f - 11):2 * (f - 11) + 2, :], bank2(4 + f % 3)[0:96], ACT.Copy,
                                   scale=96 ** -0.5).then_inc(sem("odd_evac"), 1)

            def mla(i):
                f, kind = 15 + i, MLA_ORDER[i]
                if kind == "kr" or kind[0] == "q":
                    return
                wait_fill(act, f)
                if kind[0] == "k":
                    h = 2 * int(kind[1])
                    ins = act.activation(km[0:64, h:h + 2, :], bank2(4 + f % 3)[0:64], ACT.Copy)
                else:
                    ins = act.activation(vm_tok[:, int(kind[1]), :], PS[:, 4 + f % 3, :], ACT.Copy)
                ins.then_inc(sem("odd_evac"), 1)

            def exps(a):
                for j, kw, o in ((0, P, 0), (1, S, P)):
                    act.wait_ge(sem("neg_max"), a + 1)
                    if a >= 2 and j == 0:
                        act.wait_ge(sem("prob_turned"), a - 1)
                    act.activation(prob[:, a % 2, o:o + kw], sc_sb[:, a % 2, o:o + kw], ACT.Exp,
                                   bias=row_max[:, a % 2, j:j + 1], accum_out=row_sum[:, a % 2, j:j + 1])\
                       .then_inc(sem("exped"), 1)

            def o_hi(pair):
                act.wait_ge(sem("attended"), 2 * pair + 2)
                act.activation(x_hi[:, pair, :], PS[:, 3, 0:S], ACT.Copy).then_inc(sem("o_hi"), 1)

            def attention(a):
                if a < 16:
                    exps(a)
                if 1 <= a <= 16:
                    act.wait_ge(sem("prob_turned"), a)
                    if a >= 3:
                        act.wait_ge(sem("attended"), a - 2)
                    act.activation(prob_t[:, (a - 1) % 2, :], PS[:, 2, 0:384], ACT.Copy).then_inc(sem("prob_t_ready"), 1)
                if a >= 3 and a % 2:
                    o_hi((a - 3) // 2)
                if a in (7, 8, 12):
                    split(base + {7: 15, 8: 16, 12: 17}[a])

            odd_proj(1)
            for step, arg in ODD_STEPS:
                {"proj": odd_proj, "att": attention, "qn_sum": qn_sum, "qn_out": qn_out, "kvn_sum": kvn_sum,
                 "kvn_out": kvn_out, "uq": uq, "mla": mla, "rows": lambda _: None}[step](arg)
            layer_norm("ln2", "ffn1")
            if not on("ffn1"):
                return
            ffn("ffn1", first["ffn1"])
            layer_norm("ln3", "sc", need_hi=False)
            if not on("sc"):
                return
            norm_stats("pre", x, ready=(sem("ln3_x"), 0))
            act.wait_ge(sem("mod_evac"), 1)
            operand_hi("pre", r, x_hi, lambda k: gain[:, k:k + 1], lambda k: mod[:, k:k + 1])
            c, f = first["sc"], 0
            for q in range(4):
                for part in range(3):
                    split(c + 2)
                    act.wait_ge(chunk_used, c + 1)
                    b = 4 + f % 4
                    if part == 0:
                        if q >= 2:
                            act.wait_ge(sem("cv_ready"), q - 1)
                        act.activation(c_sb[:, q % 2, :, :], bank2(b), ACT.Copy).then_inc(sem("sc_evac_c"), 1)
                    elif part == 2:
                        if q >= 2:
                            act.wait_ge(sem("sc_y"), q - 1)
                        act.activation(b_sb[:, q % 2, :, :], bank2(b), ACT.Copy).then_inc(sem("sc_evac_b"), 1)
                    c, f = c + 1, f + 1
                if q:
                    split(c + 2)
                    c += 1
                act.wait_ge(sem("sc_y"), q + 1)
                act.activation(hid_hi[:, q % 2, :, :], hid[:, q % 2, :, :], ACT.Copy).then_inc(sem("sc_hi"), 1)
            split(first["mlp"] + 1)
            norm_stats("post", r, ready=(sem("post_taken"), 0), upto=first["mlp"] + 2)
            norm_stats("preff", x, ready=(sem("post_x"), 0))
            act.wait_ge(sem("mod_evac"), 3)
            operand_hi("preff", r, x_hi, lambda k: gain[:, 16 + k:17 + k], lambda k: mod[:, 24 + k:25 + k])
            if not on("mlp"):
                return
            base = first["mlp"]

            def mlp_block(i):
                c = base if i == 0 else base + 1 + 2 * (i - 1)
                before = len(MLP_LAP) * lap[0]
                split(c + 2)
                act.wait_ge(chunk_used, c + 1 + LAP_CHUNKS * lap[0])
                if i >= 2:
                    act.wait_ge(sem("mlp_hid"), i - 1 + before)
                act.activation(relu_s[:, i % 3, :, :], bank2(4 + i % 3), ACT.Relu).then_inc(sem("mlp_relu"), 1)
                act.wait_ge(sem("mlp_hid"), i + 1 + before)
                act.activation(hid_hi[:, i % 3, :, :], hid[:, i % 3, :, :], ACT.Copy).then_inc(sem("mlp_hi"), 1)
                split(c + 3)

            mlp_block(0)
            mlp_block(1)
            with act.Fori(0, LAPS) as lap[0]:
                for i in MLP_LAP:
                    mlp_block(i)
            lap[0] = 0
            done[0] += LAP_CHUNKS * (LAPS - 1)
            for i in MLP_TAIL:
                mlp_block(i)
            split(n_chunks)
            norm_stats("postff", r, ready=(sem("postff_taken"), 0))
            for half in range(2):
                act.wait_ge(sem("out_turned"), half + 1)
                act.activation(sq[:, 2 * half:2 * half + 2, :], bank2(half), ACT.Copy).then_inc(sem("out_rows_act"), 1)

        @block.vector
        def _(dve):
            done = [0]
            lap = [0]
            links = [0]

            def split(upto):
                while done[0] <= min(upto, n_chunks - 1):
                    c = done[0]
                    dve.wait_ge(hi_split, c + 1 + LAP_CHUNKS * lap[0])
                    dve.tensor_tensor(split_view(w_lo, c), split_view(raw, c), split_view(w_hi, c).bitcast(F32), ALU.subtract)\
                       .then_inc(lo_split, 1)
                    done[0] += 1

            def link(ins):
                links[0] += 1
                ins.then_inc(sem("dve_link"), 1)
                dve.wait_ge(sem("dve_link"), links[0])

            def resid(name, which):
                if name in ("ln1", "ln3"):
                    dve.wait_ge(sem("ffn0_hid_lo" if name == "ln1" else "ffn1_hid_lo"), NF)
                for q in range(4):
                    wait_acc(dve, which, q)
                    dve.scalar_tensor_tensor(out=r[:, 2 * q:2 * q + 2, :], in0=x[:, 2 * q:2 * q + 2, :], scalar=ALPHA,
                                             in1=bank2(q + (4 if which == "odd_out" else 0)), op0=ALU.mult, op1=ALU.add)\
                       .then_inc(sem("norm_resid"), 1)
                    if q % 2:
                        fold_resid(name, q // 2)

            def fold_resid(name, q):
                dve.wait_ge(*norm(name, "resid", 2 * q + 2))
                dve.tensor_tensor(hid[:, q, :, :], r[:, 4 * q:4 * q + 2, :], r[:, 4 * q + 2:4 * q + 4, :], ALU.add)\
                   .then_inc(sem("norm_folded"), 1)

            def fold_squares(name):
                done_ = 2 if name in LNS else 0
                for q in range(1, 4):
                    dve.wait_ge(*norm(name, "sq", q + 1))
                    if q > 1:
                        dve.wait_ge(*norm(name, "folded", done_ + q - 1))
                    dve.tensor_tensor(hid[:, 2, :, :], sq[:, 0:2, :] if q == 1 else hid[:, 2, :, :],
                                      sq[:, 2 * q:2 * q + 2, :], ALU.add).then_inc(sem("norm_folded"), 1)
                dve.wait_ge(*norm(name, "folded", done_ + 3))
                dve.tensor_tensor(hid[:, 2, 0, :], hid[:, 2, 0, :], hid[:, 2, 1, :], ALU.add).then_inc(sem("norm_folded"), 1)

            def take_acc(name, which):
                for q in range(4):
                    wait_acc(dve, which, q)
                    dve.tensor_copy(r[:, 2 * q:2 * q + 2, :], bank2(q)).then_inc(sem(f"{name}_taken"), 1)

            def inverse_std(name):
                if name in LNS:
                    dve.wait_ge(*norm(name, "var", 1))
                    bank = NORM_BANKS.get(name, (5, 6))[0]
                    dve.tensor_scalar(moments[:, 0:4], PS[:, bank, 0:4], 1.0 / D, None, ALU.mult)\
                       .then_inc(sem("norm_small"), 1)
                    dve.wait_ge(*norm(name, "small", 1))
                    dve.scalar_tensor_tensor(out=moments[:, 4:6], in0=moments[:, 0:2], scalar=-1.0, in1=moments[:, 0:2],
                                             op0=ALU.mult, op1=ALU.mult).then_inc(sem("norm_small"), 1)
                    dve.wait_ge(*norm(name, "small", 2))
                    dve.tensor_tensor(moments[:, 2:4], moments[:, 2:4], moments[:, 4:6], ALU.add).then_inc(sem("norm_small"), 1)
                    dve.wait_ge(*norm(name, "small", 3))
                    dve.tensor_scalar(moments[:, 2:4], moments[:, 2:4], 0.0, None, ALU.max).then_inc(sem("norm_small"), 1)
                dve.wait_ge(*norm(name, "std", 1))
                if name in LNS:
                    link(dve.reciprocal(rstd[:, 0:2], std[:, :]))
                    dve.tensor_tensor(rstd[:, 2:4], rstd[:, 0:2], moments[:, 0:2], ALU.mult).then_inc(sem("norm_rcp"), 1)
                else:
                    dve.reciprocal(rstd[:, 0:2], std[:, :]).then_inc(sem("norm_rcp"), 1)

            def scale_pair(name, q, src, dst):
                bank = NORM_BANKS.get(name, (5, 6))[1]
                two = slice(2 * q, 2 * q + 2)
                ins = dve.tensor_tensor(dst[:, two, :], src[:, two, :], PS[:, bank:bank + 1, 0:S].to_broadcast([P, 2, S]),
                                        ALU.mult)
                if name in LNS:
                    ins.then_inc(sem("norm_scaled_r"), 1)
                    dve.wait_ge(*norm(name, "scaled_r", q + 1))
                    ins = dve.tensor_tensor(dst[:, two, :], dst[:, two, :],
                                            PS[:, bank:bank + 1, S:2 * S].to_broadcast([P, 2, S]), ALU.subtract)
                ins.then_inc(sem("norm_scaled"), 1)

            def modulation(part):
                lo_, hi_, done_ = ((0, 16, 2), (16, 24, 2), (24, 40, 4), (40, 48, 4))[part]
                dve.wait_ge(sem("mod_done"), done_)
                link(dve.tensor_tensor(mod[:, lo_:hi_], PS[:, 7, lo_:hi_], vecs[:, 2, lo_:hi_], ALU.add))
                g, weight = slice(8 * part, 8 * part + 8), vecs[:, 1, 18 + 8 * part:26 + 8 * part]
                if part % 2 == 0:
                    ins = dve.scalar_tensor_tensor(out=gain[:, g], in0=mod[:, hi_ - 8:hi_], scalar=1.0, in1=weight,
                                                   op0=ALU.add, op1=ALU.mult)
                else:
                    ins = dve.tensor_tensor(gain[:, g], mod[:, lo_:hi_], weight, ALU.mult)
                ins.then_inc(sem("mod_evac"), 1)

            def operand(name, src, full, hi, lo, gains, biases, t=KT, scaled_src=None, upto=None, part=None):
                if name not in LNS:
                    fold_squares(name)
                inverse_std(name)
                if upto is not None:
                    split(upto)
                if part is not None:
                    modulation(part)
                    dve.wait_ge(sem("mod_evac"), part + 1)
                dve.wait_ge(*norm(name, "rb", 1))
                operand_tail(name, src, full, hi, lo, gains, biases, t, scaled_src)

            def operand_tail(name, src, full, hi, lo, gains, biases, t=KT, scaled_src=None):
                n = t // 2

                def low(q):
                    dve.wait_ge(*norm(name, "full", q + 1))
                    dve.wait_ge(*norm(name, "hi", 2 * q + 2))
                    dve.tensor_tensor(lo[:, 2 * q:2 * q + 2, :], full[:, 2 * q:2 * q + 2, :],
                                      hi[:, 2 * q:2 * q + 2, :].bitcast(F32), ALU.subtract).then_inc(sem("norm_lo"), 1)

                for q in range(n):
                    scale_pair(name, q, scaled_src if scaled_src is not None else src, src)
                    if q >= 2:
                        low(q - 1)
                    dve.wait_ge(*norm(name, "scaled", q + 1))
                    for k in (2 * q, 2 * q + 1):
                        if biases:
                            ins = dve.tensor_scalar(full[:, k, :], src[:, k, :], gains(k), biases(k), ALU.mult, ALU.add)
                        else:
                            ins = dve.tensor_scalar(full[:, k, :], src[:, k, :], gains(k), None, ALU.mult)
                    ins.then_inc(sem("norm_full"), 1)
                    if q == 0:
                        low(0)
                if n > 1:
                    low(n - 1)

            def layer_norm(name, which, following):
                g, b = LNS[name]
                split(first[following] + 1)
                resid(name, which)
                fold_squares(name)
                if name != "ln3":
                    operand(name, r, x, x_hi, x_lo, lambda k: vec(0, g + k), lambda k: vec(0, b + k),
                            upto=first[following] + 2)
                    return
                inverse_std(name)
                split(first[following] + 2)
                dve.wait_ge(*norm(name, "rb", 1))
                for q in range(4):
                    scale_pair(name, q, r, r)
                    dve.wait_ge(*norm(name, "scaled", q + 1))
                    for k in (2 * q, 2 * q + 1):
                        ins = dve.tensor_scalar(x[:, k, :], r[:, k, :], vec(0, g + k), vec(0, b + k), ALU.mult, ALU.add)
                    ins.then_inc(sem("ln3_x"), 1)

            def ffn(name, base):
                def block_(i):
                    g = base if i == 0 else base + 2 + 3 * (i - 1)
                    ada = list(range(ADA_N * i // (NF - 1), ADA_N * (i + 1) // (NF - 1))) if name == "ffn1" and i < NF - 1 else []
                    if ada and i == 0:
                        dve.wait_ge(sem("silu_c_ready"), 1)
                    split(g + 2)
                    if len(ada) > 2:
                        ada_step(dve, ada.pop(0))
                    split(g + 3)
                    before = len(FFN_LAP) * lap[0]
                    dve.wait_ge(sem(f"{name}_silu"), i + 1 + before)
                    dve.wait_ge(chunk_used, g + 2 + LAP_CHUNKS * lap[0])
                    dve.tensor_tensor(hid[:, i % 2, :, :], gate_s[:, i % 2, :, :], bank2(5 + 2 * (i % 2)), ALU.mult)\
                       .then_inc(sem(f"{name}_hid"), 1)
                    dve.wait_ge(sem(f"{name}_hid_hi"), i + 1 + before)
                    dve.tensor_tensor(hid_lo[:, i % 2, :, :], hid[:, i % 2, :, :], hid_hi[:, i % 2, :, :].bitcast(F32),
                                      ALU.subtract).then_inc(sem(f"{name}_hid_lo"), 1)
                    if ada:
                        ada_step(dve, ada.pop(0))
                    if i < NF - 1:
                        split(g + 4 if i else g + 3)
                    for n in ada:
                        ada_step(dve, n)

                if name == "ffn1":
                    for i in range(NF):
                        block_(i)
                    return
                block_(0)
                block_(1)
                with dve.Fori(0, LAPS) as lap[0]:
                    for i in FFN_LAP:
                        block_(i)
                lap[0] = 0
                done[0] += LAP_CHUNKS * (LAPS - 1)
                for i in FFN_TAIL:
                    block_(i)

            dve.memset(eps_sb[:, 0:1], LN_EPS)
            dve.memset(eps_sb[:, 1:2], RMS_EPS).then_inc(sem("eps_set"), 1)
            dve.memset(conv_in[:, :, :, 0:3], 0.0).then_inc(sem("conv_pad"), 1)
            for b in range(4):
                dve.wait_ge(sem("x_turned"), b + 1)
                dve.wait_ge(sem("x_hi_ready"), b + 1)
                dve.tensor_tensor(x_lo[:, 2 * b:2 * b + 2, :], bank2(b), x_hi[:, 2 * b:2 * b + 2, :].bitcast(F32),
                                  ALU.subtract).then_inc(sem("x_lo_ready"), 1)
            split(0)
            for b in range(4):
                dve.tensor_copy(x[:, 2 * b:2 * b + 2, :], bank2(b)).then_inc(sem("x_ready"), 1)
                if b == 1:
                    split(1)
            split(2)
            base = first["even"]
            dve.wait_ge(chunk_used, base + 1)
            dve.wait_ge(sem("heads_landed"), 16 * 5)
            dve.tensor_scalar(small[:, 0, :], PS[0:16, 4, 0:S], head_vec[:, 0:1], None, ALU.add).then_inc(sem("dt_raw"), 1)
            split(3)
            dve.wait_ge(sem("vecs_turned"), 1)
            dve.tensor_copy(vecs[:, 0, 0:124], PS[:, 7, 0:124])
            dve.tensor_copy(vecs[:, 1, 0:74], PS[:, 7, P:P + 74])
            dve.tensor_copy(vecs[:, 2, 0:56], PS[:, 7, 2 * P:2 * P + 56]).then_inc(sem("vecs_ready"), 1)
            dve.wait_ge(sem("dt_act"), 3)
            dve.wait_ge(sem("a_ready"), 1)
            dve.wait_ge(sem("dt_raw"), 1)
            link(dve.scalar_tensor_tensor(out=small[:, 0, :], in0=small[:, 0, :], scalar=0.0, in1=small[:, 2, :],
                                          op0=ALU.max, op1=ALU.add))
            dve.tensor_scalar(small[:, 1, :], small[:, 0, :], head_vec[:, 2:3], -1.0, ALU.mult, ALU.mult)\
               .then_inc(sem("da_ready"), 1)
            dve.wait_ge(sem("vecs_ready"), 1)

            def even_proj(p):
                split(base + p + 2)
                if p > 6:
                    return
                t0 = 8 + 2 * (p - 1) if p <= 2 else 2 * (p - 3)
                dve.wait_ge(sem("even_evac"), p)
                if p >= 3:
                    dve.wait_ge(sem("xbc_ready"), p - 2)
                for j in range(4):
                    for q in range(2):
                        w, src, dst = vec(0, 12 * j + t0 + q), conv_in[:, p % 2, q, j:j + S], conv_acc[:, p % 2, q, :]
                        if j == 0:
                            ins = dve.tensor_scalar(dst, src, w, vec(0, 48 + t0 + q), ALU.mult, ALU.add)
                        else:
                            ins = dve.scalar_tensor_tensor(out=dst, in0=src, scalar=w, in1=dst, op0=ALU.mult, op1=ALU.add)
                    if j < 3:
                        link(ins)
                    else:
                        ins.then_inc(sem("conv_done"), 1)

            def even_small(_):
                dve.wait_ge(sem("tok_turned"), 1)
                dve.tensor_copy(tok[:, :, :], PS[:, 0, 0:64].rearrange("p (j c) -> p j c", j=2)).then_inc(sem("tok_ready"), 1)
                dve.wait_ge(sem("cb_done"), 1)
                dve.tensor_copy(cb[:, :, :], PS[:, 2, :].rearrange("p (q s) -> p q s", q=4)).then_inc(sem("cb_ready"), 1)

            def by_head(t, n=8):
                return t.rearrange("p (h o) -> p h o", o=1).to_broadcast([P, n, 64])

            def even_head(j):
                if j == 0:
                    dve.wait_ge(sem("acs_done"), 1)
                    dve.tensor_scalar(neg_acs[:, :, :], PS[:, 0, 64:96].rearrange("p (j c) -> p j c", j=2), -1.0, None,
                                      ALU.mult).then_inc(sem("acs_ready"), 1)
                    dve.wait_ge(sem("acs_ready"), 1)
                    dve.tensor_tensor(decay[:, 0, :], neg_acs[:, 0, :], PS[:, 0, 96:112], ALU.add).then_inc(sem("acs_ready"), 1)
                    dve.wait_ge(sem("tok_ready"), 1)
                dve.wait_ge(sem("xtok_done"), j + 1)
                if j:
                    dve.wait_ge(sem("y_done"), 8)
                for g in range(2):
                    dve.tensor_tensor(x_dt[:, g * 512:(g + 1) * 512].rearrange("p (h e) -> p h e", h=8),
                                      PS[:, 4 + g, :].rearrange("p (h e) -> p h e", h=8),
                                      by_head(tok[:, j, 8 * g:8 * g + 8]), ALU.mult).then_inc(sem("xdt_ready"), 1)
                if j == 0:
                    dve.wait_ge(sem("decay_ready"), 1)
                    dve.wait_ge(sem("xdt_ready"), 2)
                    dve.tensor_tensor(x_dec.rearrange("p (h e) -> p h e", h=16), x_dt.rearrange("p (h e) -> p h e", h=16),
                                      by_head(decay[:, 1, :], 16), ALU.mult).then_inc(sem("xdec_ready"), 1)

            def even_pool(i):
                two = slice(2 * i, 2 * i + 2)
                dve.wait_ge(sem("pool_hi_ready"), i + 1)
                dve.tensor_tensor(pool_lo[:, two, :], pool_y[:, two, :], pool_hi[:, two, :].bitcast(F32), ALU.subtract)\
                   .then_inc(sem("pool_lo_ready"), 1)

            def even_bcast(j):
                for q in range(4):
                    dve.wait_ge(sem("acs_bcast"), 4 * j + q + 1)
                    if 4 * j + q:
                        dve.wait_ge(sem("exp_done"), 4 * j + q)
                    dve.tensor_tensor(seg.rearrange("p (h s) -> p h s", h=4), PS[:, q, :].rearrange("p (h s) -> p h s", h=4),
                                      cst("ssm_mask").rearrange("p (o s) -> p o s", o=1).to_broadcast([P, 4, P]), ALU.add)\
                       .then_inc(sem("seg_done"), 1)
                for g in range(2):
                    dve.wait_ge(sem("exp_done"), 4 * j + 2 * g + 2)
                    if g == 0:
                        dve.wait_ge(sem("cb_ready"), 1)
                    dve.tensor_tensor(lmat[:, 8 * g:8 * g + 8, :], lmat[:, 8 * g:8 * g + 8, :],
                                      cb[:, 2 * j + g:2 * j + g + 1, :].to_broadcast([P, 8, P]), ALU.mult)\
                       .then_inc(sem("lmat_ready"), 1)
                if j:
                    even_pool(0)
                    for g in range(2):
                        dve.wait_ge(sem("eacs_done"), 2 * g + 2)
                        dve.tensor_tensor(e_acs[:, 8 * g:8 * g + 8, :], e_acs[:, 8 * g:8 * g + 8, :],
                                          xbc[:, 10 + g:11 + g, P:S].to_broadcast([P, 8, P]), ALU.mult)\
                           .then_inc(sem("cdec_ready"), 1)

            def even_y(j):
                for k in range(KT):
                    dve.wait_ge(sem("y_done"), 8 * j + 4 * (k // 4) + 4)
                    dve.scalar_tensor_tensor(out=r[:, k, j * P:(j + 1) * P], in0=xbc[:, k, j * P:(j + 1) * P],
                                             scalar=d_skip[:, k:k + 1], in1=PS[:, 4 + k // 4, (k % 4) * P:(k % 4) * P + P],
                                             op0=ALU.mult, op1=ALU.add).then_inc(sem("y_ready"), 1)

            even_proj(1)
            for step, arg in EVEN_STEPS:
                {"proj": even_proj, "small": even_small, "head": even_head, "bcast": even_bcast,
                 "state": lambda _: None, "y": even_y, "pool": lambda i: even_pool(1) if i else None}[step](arg)
            dve.wait_ge(sem("y_ready"), 16)
            dve.wait_ge(sem("even_evac"), 12)
            for q in range(4):
                dve.tensor_tensor(r[:, 2 * q:2 * q + 2, :], r[:, 2 * q:2 * q + 2, :], z_silu[:, 2 * q:2 * q + 2, :], ALU.mult)\
                   .then_inc(sem("gated"), 1)
            split(first["even_out"] + 2)
            dve.wait_ge(sem("gated"), 4)
            operand("ssm", r, sq, x_hi, x_lo, lambda k: vec(1, 4 + k), None)
            layer_norm("ln0", "even_out", "ffn0")
            if not on("ffn0"):
                return
            ffn("ffn0", first["ffn0"])
            layer_norm("ln1", "ffn0", "odd")
            if not on("odd"):
                return
            base = first["odd"]
            dve.memset(neg_f[:, :], 0.0)
            dve.memset(qz[:, :, :], 0.0).then_inc(sem("qz_zero"), 1)
            dve.wait_ge(sem("fg_act"), 3)
            dve.wait_ge(sem("qz_zero"), 1)
            link(dve.tensor_scalar(small[0:8, 2, :], small[0:8, 0, :], -1.0, 0.0, ALU.mult, ALU.max))
            link(dve.tensor_tensor(small[0:8, 3, :], small[0:8, 2, :], small[0:8, 1, :], ALU.add))
            dve.tensor_tensor_scan(neg_f[0:8, :], small[0:8, 3, :], small[0:8, 3, :], 0.0, ALU.add, ALU.bypass)\
               .then_inc(sem("neg_f_ready"), 1)

            def qn_sum(_):
                inverse_std("qn")

            def qn_out(_):
                dve.wait_ge(*norm("qn", "rb", 1))
                operand_tail("qn", cq, r, cq_hi, cq_lo, lambda k: vec(1, 12 + k), None, 4)

            def kvn_sum(_):
                inverse_std("kvn")

            def kvn_out(_):
                dve.wait_ge(*norm("kvn", "rb", 1))
                dve.wait_ge(*norm("qn", "lo", 2))
                operand_tail("kvn", ckv, r, ckv_hi, ckv_lo, lambda k: vec(1, 16 + k), None, 2)

            rr = slice(ROPE_ROW, 96)

            def mla(i):
                f, kind = 15 + i, MLA_ORDER[i]
                sin, scratch = cst("sin", 96)[rr, :], r[rr, 4:6, :]
                if kind == "kr":
                    wait_fill(dve, f)
                    link(dve.tensor_tensor(kr[rr, 1, :], PS[rr, 4 + f % 3, 0:S], sin, ALU.mult))
                    dve.wait_ge(sem("kr_cos"), 1)
                    dve.tensor_tensor(kr_rot[rr, :], kr_cos[rr, :], kr[rr, 1, :], ALU.add).then_inc(sem("kr_sum"), 1)
                elif kind[0] == "q":
                    q = int(kind[1])
                    wait_fill(dve, f)
                    two = slice(2 * q, 2 * q + 2)
                    if q:
                        dve.wait_ge(sem("qm_rot"), q)
                    link(dve.tensor_tensor(scratch, bank2(4 + f % 3)[rr],
                                           sin.rearrange("p (o s) -> p o s", o=1).to_broadcast([32, 2, S]), ALU.mult))
                    dve.wait_ge(sem("qm_cos"), q + 1)
                    dve.tensor_tensor(qm[rr, two, :], sq[rr, two, :], scratch, ALU.add).then_inc(sem("qm_rot"), 1)

            def masked(a):
                dve.wait_ge(sem("scored"), a + 1)
                b = a % 2
                if a >= 2:
                    dve.wait_ge(sem("exped"), 2 * a - 2)
                for j, kw, o in ((0, P, 0), (1, S, P)):
                    dve.tensor_tensor_reduce(out=sc_sb[:, b, o:o + kw], in0=PS[:, b, o:o + kw], in1=cst("attn_mask")[:, o:o + kw],
                                             scale=1.0, scalar=-3e38, op0=ALU.add, op1=ALU.max,
                                             accum_out=row_max[:, b, j:j + 1]).then_inc(sem("masked"), 1)
                dve.wait_ge(sem("masked"), 2 * a + 2)
                dve.tensor_scalar(row_max[:, b, :], row_max[:, b, :], -1.0, None, ALU.mult).then_inc(sem("neg_max"), 1)

            def normalised(a):
                b = a % 2
                dve.wait_ge(sem("exped"), 2 * a + 2)
                link(dve.reciprocal(row_sum[:, b, :], row_sum[:, b, :]))
                for j, kw, o in ((0, P, 0), (1, S, P)):
                    dve.tensor_scalar(prob[:, b, o:o + kw], prob[:, b, o:o + kw], row_sum[:, b, j:j + 1], None, ALU.mult)\
                       .then_inc(sem("prob_ready"), 1)

            def o_low(pair):
                dve.wait_ge(sem("o_hi"), pair + 1)
                dve.tensor_tensor(x_lo[:, pair, :], PS[:, 3, 0:S], x_hi[:, pair, :].bitcast(F32), ALU.subtract)\
                   .then_inc(sem("o_lo"), 1)

            def attention(a):
                if a < 16:
                    masked(a)
                    normalised(a)
                if a >= 3 and a % 2:
                    o_low((a - 3) // 2)
                if a in (7, 8, 12):
                    split(base + {7: 15, 8: 16, 12: 17}[a])

            for step, arg in ODD_STEPS:
                {"proj": lambda p: split(base + p + 2), "att": attention, "qn_sum": qn_sum, "qn_out": qn_out,
                 "kvn_sum": kvn_sum, "kvn_out": kvn_out, "uq": lambda c: split(base + 13 + c), "mla": mla,
                 "rows": lambda _: None}[step](arg)
            layer_norm("ln2", "odd_out", "ffn1")
            if not on("ffn1"):
                return
            ffn("ffn1", first["ffn1"])
            layer_norm("ln3", "ffn1", "sc")
            if not on("sc"):
                return
            dve.wait_ge(sem("ln3_x"), 4)
            operand("pre", r, sq, x_hi, x_lo, lambda k: gain[:, k:k + 1], lambda k: mod[:, k:k + 1], scaled_src=x, part=0)
            modulation(1)
            dve.memset(cv[:, :, :, 0:1], 0.0)
            link(dve.memset(cv[:, :, :, 1 + S:2 + S], 0.0))
            c, f = first["sc"], 0
            for q in range(4):
                i = q % 2
                split(c + 3)
                dve.wait_ge(sem("sc_evac_c"), q + 1)
                dve.wait_ge(chunk_used, c + 2)
                dve.tensor_tensor(cv[:, i, :, 1:1 + S], c_sb[:, i, :, :], bank2(4 + (f + 1) % 4), ALU.mult)\
                   .then_inc(sem("cv_ready"), 1)
                dve.wait_ge(sem("cv_ready"), q + 1)
                split(c + 4)
                for j in range(3):
                    for e in range(2):
                        w, src, dst = vec(1, 50 + 8 * j + 2 * q + e), cv[:, i, e, j:j + S], cv_acc[:, i, e, :]
                        if j == 0:
                            ins = dve.tensor_scalar(dst, src, w, None, ALU.mult)
                        else:
                            ins = dve.scalar_tensor_tensor(out=dst, in0=src, scalar=w, in1=dst, op0=ALU.mult, op1=ALU.add)
                    link(ins)
                dve.wait_ge(sem("sc_evac_b"), q + 1)
                dve.tensor_tensor(hid[:, i, :, :], cv_acc[:, i, :, :], b_sb[:, i, :, :], ALU.mult).then_inc(sem("sc_y"), 1)
                dve.wait_ge(sem("sc_hi"), q + 1)
                dve.tensor_tensor(hid_lo[:, i, :, :], hid[:, i, :, :], hid_hi[:, i, :, :].bitcast(F32), ALU.subtract)\
                   .then_inc(sem("sc_lo"), 1)
                c, f = c + (4 if q else 3), f + 3
                split(c + 1)
            split(first["mlp"] + 1)

            def add_post(norm_name, which, name, g0, upto=None):
                dve.wait_ge(*((sem("sc_lo"), 4) if name == "post_x" else (sem("mlp_lo"), NM)))
                take_acc(norm_name, which)
                fold_squares(norm_name)
                inverse_std(norm_name)
                if upto is not None:
                    split(upto)
                dve.wait_ge(*norm(norm_name, "rb", 1))
                dve.wait_ge(sem("mod_evac"), 2 if name == "post_x" else 4)
                for q in range(4):
                    scale_pair(norm_name, q, r, r)
                    dve.wait_ge(*norm(norm_name, "scaled", q + 1))
                    for k in (2 * q, 2 * q + 1):
                        ins = dve.scalar_tensor_tensor(out=x[:, k, :], in0=r[:, k, :], scalar=gain[:, g0 + k:g0 + k + 1],
                                                       in1=x[:, k, :], op0=ALU.mult, op1=ALU.add)
                        if name == "final_x" or k % 2:
                            ins.then_inc(sem(name), 1)

            add_post("post", "sc", "post_x", 8, upto=first["mlp"] + 2)
            dve.wait_ge(sem("post_x"), 4)
            operand("preff", r, sq, x_hi, x_lo, lambda k: gain[:, 16 + k:17 + k], lambda k: mod[:, 24 + k:25 + k],
                    scaled_src=x, part=2)
            modulation(3)
            if not on("mlp"):
                return
            base = first["mlp"]

            def mlp_block(i):
                c = base if i == 0 else base + 1 + 2 * (i - 1)
                before = len(MLP_LAP) * lap[0]
                split(c + 2)
                dve.wait_ge(sem("mlp_relu"), i + 1 + before)
                dve.tensor_tensor(hid[:, i % 3, :, :], relu_s[:, i % 3, :, :], relu_s[:, i % 3, :, :], ALU.mult)\
                   .then_inc(sem("mlp_hid"), 1)
                dve.wait_ge(sem("mlp_hi"), i + 1 + before)
                dve.tensor_tensor(hid_lo[:, i % 3, :, :], hid[:, i % 3, :, :], hid_hi[:, i % 3, :, :].bitcast(F32),
                                  ALU.subtract).then_inc(sem("mlp_lo"), 1)
                split(c + 3)

            mlp_block(0)
            mlp_block(1)
            with dve.Fori(0, LAPS) as lap[0]:
                for i in MLP_LAP:
                    mlp_block(i)
            lap[0] = 0
            done[0] += LAP_CHUNKS * (LAPS - 1)
            for i in MLP_TAIL:
                mlp_block(i)
            split(n_chunks)
            add_post("postff", "mlp", "final_x", 24)
            for half in range(2):
                dve.wait_ge(sem("out_turned"), half + 1)
                dve.tensor_copy(sq[:, 4 + 2 * half:6 + 2 * half, :], bank2(2 + half)).then_inc(sem("out_rows_dve"), 1)


_INS = ["x", "even_w_in", "pool_w", "pool_scale", "conv_w", "conv_b", "dt_bias", "a_log", "d_skip", "ssm_norm_w",
        "even_w_out", "odd_w_in", "fgate_b", "q_norm_w", "w_uq", "kv_norm_w", "w_ukv", "odd_w_out", "ffn_w_gate",
        "ffn_w_up", "ffn_w_down", "ln_mix_g", "ln_mix_b", "ln_ffn_g", "ln_ffn_b", "c_2", "ada_w_2", "ada_b_2",
        "norm_gains_2", "mlp_w_in_2", "mlp_w_out_2", "sc_w_in_2", "sc_conv_2", "sc_w_out_2"]


def kernel(**inputs):
    import concourse.bacc as bacc
    from concourse.bass_utils import run_bass_kernel_spmd

    nc = bacc.Bacc("TRN2", target_bir_lowering=False, num_devices=1)
    arrays = {name: np.ascontiguousarray(inputs[name]) for name in _INS}
    arrays["consts"] = shape_constants()
    aps = {n: nc.dram_tensor(n, a.shape, mybir.dt.from_np(a.dtype), kind="ExternalInput").ap() for n, a in arrays.items()}
    out = nc.dram_tensor("out", (1, S, D), F32, kind="ExternalOutput").ap()
    build(nc, aps, out)
    result = run_bass_kernel_spmd(nc, [arrays], core_ids=[0])
    return result.results[0]["out"]
```
